# Optimizing a Trainium2 kernel written in Bass

```python
import math
import jax, jax.numpy as jnp
from jax import lax
import numpy as np

D_MODEL = 1024
BATCH = 1
SEQ = 256
DEPTH = 1

MLA_HEADS = 8
MLA_Q_RANK = 384
MLA_KV_RANK = 256
MLA_NOPE_DIM = 128
MLA_ROPE_DIM = 64
MLA_V_DIM = D_MODEL // MLA_HEADS
ROPE_THETA = 10000.0
Q_BLOCK = 128
DIL_GROUPS = ((128, 1), (512, 4), (2048, 16))
DIL_HEADS = 8
DIL_HEAD_DIM = D_MODEL // DIL_HEADS
N_DIL_HEADS = len(DIL_GROUPS) * DIL_HEADS
REL_BUCKETS = 32
REL_MAX_DIST = 1024
N_EXPERTS = 16
EC_CAPACITY_FACTOR = 2
D_FF_EXPERT = 2 * D_MODEL
N_BRANCHES = 2
NORM_EPS = 1e-6
NEG_INF = -1e30
COLS_DIL = len(DIL_GROUPS) * 3 * DIL_HEADS * DIL_HEAD_DIM
SPLIT_SIZES = (MLA_Q_RANK, MLA_KV_RANK, MLA_ROPE_DIM, COLS_DIL, N_BRANCHES * D_MODEL)
D_IN = sum(SPLIT_SIZES)


def rmsnorm(t, g):
    tf = t.astype(jnp.float32)
    y = tf * lax.rsqrt(jnp.mean(tf * tf, axis=-1, keepdims=True) + NORM_EPS)
    return (y * g.astype(jnp.float32)).astype(t.dtype)

def rope(t, cos, sin):
    t1, t2 = jnp.split(t, 2, axis=-1)
    return jnp.concatenate([t1 * cos - t2 * sin, t1 * sin + t2 * cos], axis=-1).astype(t.dtype)

def t5_bucket(rel):
    nb = REL_BUCKETS // 2
    ret = jnp.where(rel > 0, nb, 0)
    n = jnp.abs(rel)
    max_exact = nb // 2
    nf = jnp.maximum(n, 1).astype(jnp.float32)
    large = max_exact + (jnp.log(nf / max_exact) / math.log(REL_MAX_DIST / max_exact)
                         * (nb - max_exact)).astype(jnp.int32)
    large = jnp.minimum(large, nb - 1)
    return ret + jnp.where(n < max_exact, n, large)

def mla_attention(c_q, c_kv, k_pe, g_q_lat, g_kv_lat, w_uq, w_ukv, cos, sin):
    B, S, _ = c_q.shape
    q = (rmsnorm(c_q, g_q_lat) @ w_uq).reshape(B, S, MLA_HEADS, MLA_NOPE_DIM + MLA_ROPE_DIM)
    q_nope = q[..., :MLA_NOPE_DIM]
    q_pe = rope(q[..., MLA_NOPE_DIM:], cos[:, :, None], sin[:, :, None])
    kv = (rmsnorm(c_kv, g_kv_lat) @ w_ukv).reshape(B, S, MLA_HEADS, MLA_NOPE_DIM + MLA_V_DIM)
    k_nope, v = kv[..., :MLA_NOPE_DIM], kv[..., MLA_NOPE_DIM:]
    k_pe = rope(k_pe, cos, sin)
    scale = (MLA_NOPE_DIM + MLA_ROPE_DIM) ** -0.5
    nqb = S // Q_BLOCK

    def to_blocks(t):
        return jnp.moveaxis(t.reshape((B, nqb, Q_BLOCK) + t.shape[2:]), 1, 0)

    def attend(blk):
        qn, qp = blk
        s = (jnp.einsum('bqhc,bkhc->bhqk', qn, k_nope)
             + jnp.einsum('bqhr,bkr->bhqk', qp, k_pe))
        p = jax.nn.softmax(s.astype(jnp.float32) * scale, axis=-1).astype(v.dtype)
        return jnp.einsum('bhqk,bkhc->bqhc', p, v)

    o = lax.map(attend, (to_blocks(q_nope), to_blocks(q_pe)))
    return jnp.moveaxis(o, 0, 1).reshape(B, S, MLA_HEADS * MLA_V_DIM)

def dilated_band_attention(q, k, v, pos, bias_table, window, dilation):
    B, S, H, Dh = q.shape
    d = dilation
    r = window // (2 * d)
    L = S // d
    nb = -(-L // r)
    Lp = nb * r

    def to_classes(t):
        t = jnp.moveaxis(t.reshape((B, L, d) + t.shape[2:]), 2, 1)
        return jnp.pad(t, [(0, 0), (0, 0), (0, Lp - L)] + [(0, 0)] * (t.ndim - 3))

    def band(t):
        t = jnp.pad(t, [(0, 0), (0, 0), (r, r)] + [(0, 0)] * (t.ndim - 3))
        t = t.reshape((B, d, nb + 2, r) + t.shape[3:])
        return jnp.concatenate([t[:, :, :-2], t[:, :, 1:-1], t[:, :, 2:]], axis=3)

    qc, kc, vc, pc = to_classes(q), to_classes(k), to_classes(v), to_classes(pos)
    kb, vb, pkb = band(kc), band(vc), band(pc)
    qb = qc.reshape(B, d, nb, r, H, Dh)
    pqb = pc.reshape(B, d, nb, r)
    s = jnp.einsum('bgnqhc,bgnkhc->bgnhqk', qb, kb).astype(jnp.float32) * (Dh ** -0.5)
    rel = pkb[:, :, :, None, :] - pqb[..., None]
    bias = bias_table[t5_bucket(rel)]
    s = s + jnp.moveaxis(bias, -1, 3).astype(jnp.float32)
    qi = jnp.arange(nb)[:, None, None] * r + jnp.arange(r)[None, :, None]
    kj = (jnp.arange(nb)[:, None, None] - 1) * r + jnp.arange(3 * r)[None, None, :]
    valid = (jnp.abs(kj - qi) <= r) & (kj >= 0) & (kj < L)
    s = jnp.where(valid[:, None], s, NEG_INF)
    m = jnp.max(s, axis=-1, keepdims=True)
    p = jnp.exp(s - m)
    den = jnp.sum(p, axis=-1, keepdims=True)
    o = jnp.einsum('bgnhqk,bgnkhc->bgnqhc', (p / den).astype(v.dtype), vb)
    lse = (m + jnp.log(den))[..., 0]
    o = o.reshape(B, d, Lp, H, Dh)[:, :, :L]
    o = jnp.moveaxis(o, 1, 2).reshape(B, S, H, Dh)
    lse = jnp.moveaxis(lse, 3, 4).reshape(B, d, Lp, H)[:, :, :L]
    lse = jnp.moveaxis(lse, 1, 2).reshape(B, S, H)
    return o, lse

def expert_choice_ffn(h, w_router, w_gate, w_up, w_down):
    B, S, D = h.shape
    cap = EC_CAPACITY_FACTOR * S // N_EXPERTS
    aff = jax.nn.softmax((h @ w_router).astype(jnp.float32), axis=-1)
    gate, idx = lax.top_k(jnp.swapaxes(aff, 1, 2), cap)
    bidx = jnp.arange(B)[:, None, None]
    xe = h[bidx, idx]
    hid = (jax.nn.silu(jnp.einsum('becd,edf->becf', xe, w_gate))
           * jnp.einsum('becd,edf->becf', xe, w_up))
    ye = jnp.einsum('becf,efd->becd', hid, w_down) * gate[..., None].astype(h.dtype)
    return jnp.zeros_like(h).at[bidx, idx].add(ye)

def first_inputs(seed: int = 0) -> dict:
    key = jax.random.key(seed)
    ks = jax.random.split(key, 20)
    f32 = jnp.float32

    def nrm(k, shape, s):
        return jax.random.normal(k, shape, f32) * s

    def gain(k, shape):
        return 1.0 + 0.02 * jax.random.normal(k, shape, f32)

    x = nrm(ks[0], (BATCH, SEQ, D_MODEL), 1.0)
    c = nrm(ks[1], (BATCH, D_MODEL), 1.0)
    offs = jax.random.randint(ks[2], (BATCH, 1), 0, 4096, dtype=jnp.int32)
    positions = offs + jnp.arange(SEQ, dtype=jnp.int32)[None, :]
    w_ada = nrm(ks[3], (DEPTH, D_MODEL, 6 * D_MODEL), 0.02)
    b_ada = nrm(ks[4], (DEPTH, 6 * D_MODEL), 0.02)
    g_norm_mix = gain(ks[5], (DEPTH, D_MODEL))
    w_in = nrm(ks[6], (DEPTH, D_MODEL, D_IN), D_MODEL ** -0.5)
    g_q_lat = gain(ks[7], (DEPTH, MLA_Q_RANK))
    g_kv_lat = gain(ks[8], (DEPTH, MLA_KV_RANK))
    w_uq = nrm(ks[9], (DEPTH, MLA_Q_RANK, MLA_HEADS * (MLA_NOPE_DIM + MLA_ROPE_DIM)), MLA_Q_RANK ** -0.5)
    w_ukv = nrm(ks[10], (DEPTH, MLA_KV_RANK, MLA_HEADS * (MLA_NOPE_DIM + MLA_V_DIM)), MLA_KV_RANK ** -0.5)
    rel_bias = nrm(ks[11], (REL_BUCKETS, N_DIL_HEADS), 0.5)
    w_out = nrm(ks[12], (DEPTH, D_MODEL, D_MODEL), D_MODEL ** -0.5)
    g_norm_ffn = gain(ks[13], (DEPTH, D_MODEL))
    w_router = nrm(ks[14], (DEPTH, D_MODEL, N_EXPERTS), D_MODEL ** -0.5)
    w_gate = nrm(ks[15], (DEPTH, N_EXPERTS, D_MODEL, D_FF_EXPERT), D_MODEL ** -0.5)
    w_up = nrm(ks[16], (DEPTH, N_EXPERTS, D_MODEL, D_FF_EXPERT), D_MODEL ** -0.5)
    w_down = nrm(ks[17], (DEPTH, N_EXPERTS, D_FF_EXPERT, D_MODEL), D_FF_EXPERT ** -0.5)
    g_final = gain(ks[18], (D_MODEL,))
    return {'x': x, 'c': c, 'positions': positions, 'w_ada': w_ada, 'b_ada': b_ada,
            'g_norm_mix': g_norm_mix, 'w_in': w_in, 'g_q_lat': g_q_lat, 'g_kv_lat': g_kv_lat,
            'w_uq': w_uq, 'w_ukv': w_ukv, 'rel_bias': rel_bias, 'w_out': w_out,
            'g_norm_ffn': g_norm_ffn, 'w_router': w_router, 'w_gate': w_gate, 'w_up': w_up,
            'w_down': w_down, 'g_final': g_final}

def first_block(x, c, positions, w_ada, b_ada, g_norm_mix, w_in, g_q_lat, g_kv_lat, w_uq, w_ukv,
              rel_bias, w_out, g_norm_ffn, w_router, w_gate, w_up, w_down, g_final):
    B, S, D = x.shape
    inv_freq = ROPE_THETA ** (-jnp.arange(0, MLA_ROPE_DIM, 2, dtype=jnp.float32) / MLA_ROPE_DIM)
    ang = positions.astype(jnp.float32)[..., None] * inv_freq
    cos, sin = jnp.cos(ang), jnp.sin(ang)
    cond = jax.nn.silu(c)
    split_at = [int(v) for v in np.cumsum(SPLIT_SIZES)[:-1]]
    for l in range(DEPTH):
        mod = (cond @ w_ada[l] + b_ada[l])[:, None, :]
        sh1, sc1, gt1, sh2, sc2, gt2 = jnp.split(mod, 6, axis=-1)
        h = rmsnorm(x, g_norm_mix[l]) * (1.0 + sc1) + sh1
        c_q, c_kv, k_pe, dil, gates = jnp.split(h @ w_in[l], split_at, axis=-1)
        o_a = mla_attention(c_q, c_kv, k_pe, g_q_lat[l], g_kv_lat[l], w_uq[l], w_ukv[l], cos, sin)
        dil = dil.reshape(B, S, len(DIL_GROUPS), 3, DIL_HEADS, DIL_HEAD_DIM)
        outs, lses = [], []
        for gi, (win, dd) in enumerate(DIL_GROUPS):
            o_g, lse_g = dilated_band_attention(
                dil[:, :, gi, 0], dil[:, :, gi, 1], dil[:, :, gi, 2], positions,
                rel_bias[:, gi * DIL_HEADS:(gi + 1) * DIL_HEADS], win, dd)
            outs.append(o_g)
            lses.append(lse_g)
        wts = jax.nn.softmax(jnp.stack(lses), axis=0)
        o_b = jnp.einsum('gbsh,gbshc->bshc', wts.astype(x.dtype), jnp.stack(outs)).reshape(B, S, D)
        g_a, g_b = jnp.split(jax.nn.sigmoid(gates), 2, axis=-1)
        x = x + gt1 * ((g_a * o_a + g_b * o_b) @ w_out[l])
        h2 = rmsnorm(x, g_norm_ffn[l]) * (1.0 + sc2) + sh2
        x = x + gt2 * expert_choice_ffn(h2, w_router[l], w_gate[l], w_up[l], w_down[l])
    return rmsnorm(x, g_final)


DEPTH_2 = 2

N_MIXERS = 2
N_SSD_LAYERS = (DEPTH_2 + N_MIXERS - 1) // N_MIXERS
N_LRU_LAYERS = DEPTH_2 // N_MIXERS
SSD_EXPAND = 2
SSD_D_INNER = SSD_EXPAND * D_MODEL
SSD_HEADDIM = 64
SSD_HEADS = SSD_D_INNER // SSD_HEADDIM
SSD_GROUPS = 4
SSD_HPG = SSD_HEADS // SSD_GROUPS
SSD_D_STATE = 128
SSD_CONV = 4
SSD_CHUNK = 128
SSD_CONV_DIM = SSD_D_INNER + 2 * SSD_GROUPS * SSD_D_STATE
SSD_IN_DIM = SSD_D_INNER + SSD_CONV_DIM + SSD_HEADS
LRU_WIDTH = 1280
LRU_HEADS = 10
LRU_BLOCK = LRU_WIDTH // LRU_HEADS
LRU_CONV = 4
LRU_C = 8.0
D_FF = 4 * D_MODEL
FFN_CONV = 3
EPS = 1e-6


def rmsnorm_2(x, w):
    xf = x.astype(jnp.float32)
    y = xf * lax.rsqrt(jnp.mean(xf * xf, axis=-1, keepdims=True) + EPS)
    return (y * w.astype(jnp.float32)).astype(x.dtype)

def causal_dwconv(x, w, b):
    k = w.shape[0]
    s = x.shape[1]
    xp = jnp.pad(x, ((0, 0), (k - 1, 0), (0, 0)))
    y = b
    for j in range(k):
        y = y + xp[:, j:j + s, :] * w[j]
    return y

def ssd_chunked_scan(xh, dt, a, bm, cm):
    bsz, s, h, p = xh.shape
    nc = s // SSD_CHUNK
    xdt = (xh * dt[..., None]).reshape(bsz, nc, SSD_CHUNK, SSD_GROUPS, SSD_HPG, p)
    da = (dt * a).reshape(bsz, nc, SSD_CHUNK, SSD_GROUPS, SSD_HPG)
    bc = bm.reshape(bsz, nc, SSD_CHUNK, SSD_GROUPS, SSD_D_STATE)
    cc = cm.reshape(bsz, nc, SSD_CHUNK, SSD_GROUPS, SSD_D_STATE)
    cs = jnp.moveaxis(jnp.cumsum(da, axis=2), 2, -1)
    tri = jnp.tril(jnp.ones((SSD_CHUNK, SSD_CHUNK), dtype=bool))
    decay_in = jnp.exp(jnp.where(tri, cs[..., :, None] - cs[..., None, :], -jnp.inf))
    cb = jnp.einsum('bclgn,bcsgn->bcgls', cc, bc)
    scores = cb[:, :, :, None] * decay_in
    y_diag = jnp.einsum('bcgels,bcsgep->bclgep', scores, xdt)
    decay_out = jnp.moveaxis(jnp.exp(cs[..., -1:] - cs), -1, 2)
    states = jnp.einsum('bclgn,bclgep->bcgepn', bc, xdt * decay_out[..., None])
    tot = cs[..., -1]
    inc = jnp.moveaxis(jnp.cumsum(tot, axis=1), 1, -1)
    exc = inc - jnp.moveaxis(tot, 1, -1)
    stri = jnp.tril(jnp.ones((nc, nc), dtype=bool), -1)
    decay_chunk = jnp.exp(jnp.where(stri, exc[..., :, None] - inc[..., None, :], -jnp.inf))
    entering = jnp.einsum('bgezc,bcgepn->bzgepn', decay_chunk, states)
    state_decay = jnp.moveaxis(jnp.exp(cs), -1, 2)
    y_off = jnp.einsum('bclgn,bcgepn->bclgep', cc, entering) * state_decay[..., None]
    return (y_diag + y_off).reshape(bsz, s, h, p)

def gated_group_rmsnorm(y, z, w):
    bsz, s, d = y.shape
    g = (y * jax.nn.silu(z.astype(jnp.float32))).reshape(bsz, s, SSD_GROUPS, d // SSD_GROUPS)
    g = g * lax.rsqrt(jnp.mean(g * g, axis=-1, keepdims=True) + EPS)
    return g.reshape(bsz, s, d) * w.astype(jnp.float32)

def ssd_mixer(u, w_in, conv_w, conv_b, dt_bias, a_log, d_skip, norm_w, w_out):
    bsz, s, _ = u.shape
    proj = u @ w_in
    z = proj[..., :SSD_D_INNER]
    xbc = proj[..., SSD_D_INNER:SSD_D_INNER + SSD_CONV_DIM]
    dt_raw = proj[..., SSD_D_INNER + SSD_CONV_DIM:]
    xbc = jax.nn.silu(causal_dwconv(xbc, conv_w, conv_b)).astype(jnp.float32)
    xs = xbc[..., :SSD_D_INNER].reshape(bsz, s, SSD_HEADS, SSD_HEADDIM)
    bm = xbc[..., SSD_D_INNER:SSD_D_INNER + SSD_GROUPS * SSD_D_STATE].reshape(bsz, s, SSD_GROUPS, SSD_D_STATE)
    cm = xbc[..., SSD_D_INNER + SSD_GROUPS * SSD_D_STATE:].reshape(bsz, s, SSD_GROUPS, SSD_D_STATE)
    dt = jax.nn.softplus(dt_raw.astype(jnp.float32) + dt_bias.astype(jnp.float32))
    a = -jnp.exp(a_log.astype(jnp.float32))
    y = ssd_chunked_scan(xs, dt, a, bm, cm)
    y = y + d_skip.astype(jnp.float32)[:, None] * xs
    y = gated_group_rmsnorm(y.reshape(bsz, s, SSD_D_INNER), z, norm_w)
    return (y.astype(u.dtype) @ w_out).astype(u.dtype)

def _linear_combine(c1, c2):
    a1, b1 = c1
    a2, b2 = c2
    return a1 * a2, a2 * b1 + b2

def rglru_mixer(u, w_in, b_in, conv_w, conv_b, w_gx, b_gx, w_ga, b_ga, lam, w_out, b_out):
    bsz, s, _ = u.shape
    proj = u @ w_in + b_in
    ybr = jax.nn.gelu(proj[..., :LRU_WIDTH].astype(jnp.float32))
    xbr = causal_dwconv(proj[..., LRU_WIDTH:], conv_w, conv_b)
    xh = xbr.reshape(bsz, s, LRU_HEADS, LRU_BLOCK)
    gx = jax.nn.sigmoid((jnp.einsum('bshi,hij->bshj', xh, w_gx).reshape(bsz, s, LRU_WIDTH) + b_gx).astype(jnp.float32))
    ga = jax.nn.sigmoid((jnp.einsum('bshi,hij->bshj', xh, w_ga).reshape(bsz, s, LRU_WIDTH) + b_ga).astype(jnp.float32))
    log_a = LRU_C * ga * jax.nn.log_sigmoid(lam.astype(jnp.float32))
    a_t = jnp.exp(log_a)
    mult = jnp.sqrt(-jnp.expm1(2.0 * log_a))
    b_t = mult * gx * xbr.astype(jnp.float32)
    _, h = lax.associative_scan(_linear_combine, (a_t, b_t), axis=1)
    out = (h * ybr).astype(u.dtype) @ w_out + b_out
    return out.astype(u.dtype)

def conv_ffn(u, w_up, conv_w, conv_b, w_down):
    hcv = causal_dwconv(u @ w_up, conv_w, conv_b)
    g = hcv[..., :D_FF]
    v = hcv[..., D_FF:]
    return ((jax.nn.gelu(g.astype(jnp.float32)) * v.astype(jnp.float32)).astype(u.dtype) @ w_down).astype(u.dtype)

def second_inputs(seed: int = 0) -> dict:
    key = jax.random.key(seed)
    ks = jax.random.split(key, 32)
    f32 = jnp.float32

    def nrm(k, shape, scale):
        return scale * jax.random.normal(k, shape, f32)

    def gain(k, shape):
        return 1.0 + 0.1 * jax.random.normal(k, shape, f32)

    na, nb = N_SSD_LAYERS, N_LRU_LAYERS
    dt0 = jnp.exp(jax.random.uniform(ks[9], (na, SSD_HEADS), f32, math.log(1e-3), math.log(1e-1)))
    lam_u = jax.random.uniform(ks[20], (nb, LRU_WIDTH), f32, 0.9, 0.999)
    return {
        'x': jax.random.normal(ks[0], (BATCH, SEQ, D_MODEL), f32),
        'norm_mix_pre': gain(ks[1], (DEPTH_2, D_MODEL)),
        'norm_mix_post': gain(ks[2], (DEPTH_2, D_MODEL)),
        'norm_ffn_pre': gain(ks[3], (DEPTH_2, D_MODEL)),
        'norm_ffn_post': gain(ks[4], (DEPTH_2, D_MODEL)),
        'ssd_w_in': nrm(ks[5], (na, D_MODEL, SSD_IN_DIM), D_MODEL ** -0.5),
        'ssd_conv_w': nrm(ks[6], (na, SSD_CONV, SSD_CONV_DIM), SSD_CONV ** -0.5),
        'ssd_conv_b': nrm(ks[7], (na, SSD_CONV_DIM), 0.01),
        'ssd_dt_bias': dt0 + jnp.log(-jnp.expm1(-dt0)),
        'ssd_a_log': jnp.log(jax.random.uniform(ks[10], (na, SSD_HEADS), f32, 1.0, 16.0)),
        'ssd_d': gain(ks[11], (na, SSD_HEADS)),
        'ssd_norm': gain(ks[12], (na, SSD_D_INNER)),
        'ssd_w_out': nrm(ks[13], (na, SSD_D_INNER, D_MODEL), SSD_D_INNER ** -0.5),
        'lru_w_in': nrm(ks[14], (nb, D_MODEL, 2 * LRU_WIDTH), D_MODEL ** -0.5),
        'lru_b_in': nrm(ks[15], (nb, 2 * LRU_WIDTH), 0.01),
        'lru_conv_w': nrm(ks[16], (nb, LRU_CONV, LRU_WIDTH), LRU_CONV ** -0.5),
        'lru_conv_b': nrm(ks[17], (nb, LRU_WIDTH), 0.01),
        'lru_w_gx': nrm(ks[18], (nb, LRU_HEADS, LRU_BLOCK, LRU_BLOCK), LRU_BLOCK ** -0.5),
        'lru_b_gx': nrm(ks[19], (nb, LRU_WIDTH), 0.01),
        'lru_w_ga': nrm(ks[21], (nb, LRU_HEADS, LRU_BLOCK, LRU_BLOCK), LRU_BLOCK ** -0.5),
        'lru_b_ga': nrm(ks[22], (nb, LRU_WIDTH), 0.01),
        'lru_lambda': jnp.log(lam_u) - jnp.log1p(-lam_u),
        'lru_w_out': nrm(ks[23], (nb, LRU_WIDTH, D_MODEL), LRU_WIDTH ** -0.5),
        'lru_b_out': nrm(ks[24], (nb, D_MODEL), 0.01),
        'ffn_w_up': nrm(ks[25], (DEPTH_2, D_MODEL, 2 * D_FF), D_MODEL ** -0.5),
        'ffn_conv_w': nrm(ks[26], (DEPTH_2, FFN_CONV, 2 * D_FF), FFN_CONV ** -0.5),
        'ffn_conv_b': nrm(ks[27], (DEPTH_2, 2 * D_FF), 0.01),
        'ffn_w_down': nrm(ks[28], (DEPTH_2, D_FF, D_MODEL), D_FF ** -0.5),
    }

def second_block(x, norm_mix_pre, norm_mix_post, norm_ffn_pre, norm_ffn_post,
              ssd_w_in, ssd_conv_w, ssd_conv_b, ssd_dt_bias, ssd_a_log, ssd_d, ssd_norm, ssd_w_out,
              lru_w_in, lru_b_in, lru_conv_w, lru_conv_b, lru_w_gx, lru_b_gx, lru_w_ga, lru_b_ga,
              lru_lambda, lru_w_out, lru_b_out,
              ffn_w_up, ffn_conv_w, ffn_conv_b, ffn_w_down):
    for i in range(DEPTH_2):
        h = rmsnorm_2(x, norm_mix_pre[i])
        j = i // N_MIXERS
        if i % N_MIXERS == 0:
            m = ssd_mixer(h, ssd_w_in[j], ssd_conv_w[j], ssd_conv_b[j], ssd_dt_bias[j],
                          ssd_a_log[j], ssd_d[j], ssd_norm[j], ssd_w_out[j])
        else:
            m = rglru_mixer(h, lru_w_in[j], lru_b_in[j], lru_conv_w[j], lru_conv_b[j],
                            lru_w_gx[j], lru_b_gx[j], lru_w_ga[j], lru_b_ga[j],
                            lru_lambda[j], lru_w_out[j], lru_b_out[j])
        x = x + rmsnorm_2(m, norm_mix_post[i])
        h = rmsnorm_2(x, norm_ffn_pre[i])
        f = conv_ffn(h, ffn_w_up[i], ffn_conv_w[i], ffn_conv_b[i], ffn_w_down[i])
        x = x + rmsnorm_2(f, norm_ffn_post[i])
    return x


def setup_inputs(seed=0):
    out = dict(first_inputs(seed))
    for name, value in second_inputs(seed + 1).items():
        if name != "x":
            out[name + "_2"] = value
    return out


def reference(
    x, c, positions, w_ada, b_ada, g_norm_mix, w_in, g_q_lat, g_kv_lat, w_uq, w_ukv, rel_bias,
    w_out, g_norm_ffn, w_router, w_gate, w_up, w_down, g_final, norm_mix_pre_2, norm_mix_post_2,
    norm_ffn_pre_2, norm_ffn_post_2, ssd_w_in_2, ssd_conv_w_2, ssd_conv_b_2, ssd_dt_bias_2,
    ssd_a_log_2, ssd_d_2, ssd_norm_2, ssd_w_out_2, lru_w_in_2, lru_b_in_2, lru_conv_w_2,
    lru_conv_b_2, lru_w_gx_2, lru_b_gx_2, lru_w_ga_2, lru_b_ga_2, lru_lambda_2, lru_w_out_2,
    lru_b_out_2, ffn_w_up_2, ffn_conv_w_2, ffn_conv_b_2, ffn_w_down_2,
):
    x = first_block(
        x, c, positions, w_ada, b_ada, g_norm_mix, w_in, g_q_lat, g_kv_lat, w_uq, w_ukv,
        rel_bias, w_out, g_norm_ffn, w_router, w_gate, w_up, w_down, g_final,
    )
    return second_block(
        x, norm_mix_pre_2, norm_mix_post_2, norm_ffn_pre_2, norm_ffn_post_2, ssd_w_in_2,
        ssd_conv_w_2, ssd_conv_b_2, ssd_dt_bias_2, ssd_a_log_2, ssd_d_2, ssd_norm_2,
        ssd_w_out_2, lru_w_in_2, lru_b_in_2, lru_conv_w_2, lru_conv_b_2, lru_w_gx_2, lru_b_gx_2,
        lru_w_ga_2, lru_b_ga_2, lru_lambda_2, lru_w_out_2, lru_b_out_2, ffn_w_up_2,
        ffn_conv_w_2, ffn_conv_b_2, ffn_w_down_2,
    )


_drawn_inputs = setup_inputs


def setup_inputs(seed=0):
    import zlib

    import numpy as np

    out = dict(_drawn_inputs(seed))
    spreads = {}
    factors = {'g_norm_mix': 6.433,
     'g_q_lat': 8.0,
     'g_kv_lat': 8.0,
     'g_norm_ffn': 3.61,
     'ssd_conv_b_2': 3.615,
     'lru_b_in_2': 2.698,
     'lru_conv_b_2': 2.911,
     'lru_b_gx_2': 26.328,
     'lru_b_ga_2': 46.653,
     'lru_b_out_2': 3.82,
     'ffn_conv_b_2': 4.27}
    for name, (base, spread) in spreads.items():
        noise = np.random.default_rng([zlib.crc32(name.encode()), seed]).standard_normal(out[name].shape)
        drawn = base * np.exp(spread * noise) if base else spread * noise
        out[name] = __import__('jax').numpy.asarray(drawn.astype(out[name].dtype))
    for name, factor in factors.items():
        out[name] = (out[name] * factor).astype(out[name].dtype)
    return out
```

```python
import concourse.bass as bass
from concourse import mybir
from contextlib import ExitStack
from collections import deque
import numpy as np

F32 = mybir.dt.float32
F32R = mybir.dt.float32r
BF16 = mybir.dt.bfloat16
I32 = mybir.dt.int32
ALU = mybir.AluOpType
ACT = mybir.ActivationFunctionType
AX = mybir.AxisListType

SEQ = 256
DM = 1024
EPS = 1e-6
BIG = 1e30
NEXP = 16

PAGE = 2048
NPAGE = 25
CONST = 1952

TAG = 1 << 20
SPANS = [(1, 2), (3, 4), (3, 6), (6, 11), (7, 8), (9, 10), (9, 11), (13, 14), (15, 17)]

THRESH = ([-BIG, -558, -304, -165, -90, -49, -26, -14] + list(range(-7, 1))
          + list(range(1, 8)) + [8, 15, 27, 50, 91, 166, 305, 559] + [BIG])
BUCKET = [15, 14, 13, 12, 11, 10, 9, 8, 7, 6, 5, 4, 3, 2, 1, 0] + list(range(17, 32)) + [None]

ADA_FIRST = [2, 3, 0, 1]
ADA_LATER = [4, 5, 6, 7, 8, 9, 10, 11]
DIL0 = 704
GATE0 = 704 + 9216
SSD_TILES = ["dt"] + [("b", i) for i in range(4)] + [("c", i) for i in range(4)] \
    + [("x", i) for i in range(16)] + [("z", i) for i in range(16)]


def token_order():
    return [16 * l + 4 * j + c for c in range(4) for j in range(4) for l in range(16)]


def ada_after(i):
    return ADA_LATER[i // 4] if i % 4 == 3 and i // 4 < 8 else None



CONST_COLS = {}


def const_layout():
    at = 0
    for name, n in [("ident", 128), ("iota", 32), ("thr", 1), ("invf", 1), ("sgn", 1), ("pmod", 1), ("sel4", 1),
                    ("c", 8), ("g_mix", 8), ("g_ffn", 8), ("b_ada", 48), ("g_q", 3), ("g_kv", 2), ("w_router", 128),
                    ("pre", 32), ("conv_w", 96), ("conv_b", 24), ("dt_b", 1), ("a_log", 1), ("d", 16), ("ssd_n", 16),
                    ("l_bin", 20), ("l_cw", 40), ("l_cb", 10), ("l_bgx", 10), ("l_bga", 10), ("lam", 10),
                    ("f_cw", 384), ("f_cb", 128)]:
        CONST_COLS[name] = (at, n)
        at += n
    return at


NCST = const_layout()
NCST1 = CONST_COLS["pre"][0]


def cols(v):
    return np.ascontiguousarray(np.reshape(v, (-1, 128)).T)


def lay_out(i):
    f32 = np.float32
    order = token_order()
    out = {}
    p = np.arange(128)
    cst = np.zeros((128, NCST), f32)

    def put(name, v):
        at, n = CONST_COLS[name]
        cst[:, at:at + n] = np.reshape(v, (128, n))

    put("ident", np.eye(128, dtype=f32))
    put("iota", np.tile(np.arange(32, dtype=f32), (128, 1)))
    put("thr", np.array(THRESH, f32)[p % 32])
    inv = (10000.0 ** (-np.arange(0, 64, 2, dtype=np.float64) / 64)).astype(f32)
    put("invf", inv[p % 32])
    put("sgn", np.where(p % 64 < 32, -1, 1).astype(f32))
    put("pmod", (p % 32).astype(f32))
    put("sel4", (p % 32 == 0).astype(f32))
    put("c", cols(i["c"][0]))
    put("g_mix", cols(i["g_norm_mix"][0]))
    put("g_ffn", cols(i["g_norm_ffn"][0]))
    put("b_ada", cols(i["b_ada"][0]))
    put("g_q", cols(i["g_q_lat"][0]))
    put("g_kv", cols(i["g_kv_lat"][0]))
    put("w_router", i["w_router"][0].reshape(8, 128, 16).transpose(1, 0, 2))
    put("pre", np.concatenate([cols(i["norm_mix_pre_2"][0]), cols(i["norm_ffn_pre_2"][0]),
                               cols(i["norm_mix_pre_2"][1]), cols(i["norm_ffn_pre_2"][1])], 1))
    put("conv_w", i["ssd_conv_w_2"][0].reshape(4, 24, 128).transpose(2, 1, 0))
    put("conv_b", cols(i["ssd_conv_b_2"][0]))
    put("dt_b", np.tile(i["ssd_dt_bias_2"][0], 4))
    put("a_log", np.tile(i["ssd_a_log_2"][0], 4))
    put("d", cols(np.repeat(i["ssd_d_2"][0], 64)))
    put("ssd_n", cols(i["ssd_norm_2"][0]))
    put("l_bin", cols(i["lru_b_in_2"][0]))
    put("l_cw", i["lru_conv_w_2"][0].reshape(4, 10, 128).transpose(2, 1, 0))
    put("l_cb", cols(i["lru_conv_b_2"][0]))
    put("l_bgx", cols(i["lru_b_gx_2"][0]))
    put("l_bga", cols(i["lru_b_ga_2"][0]))
    put("lam", cols(i["lru_lambda_2"][0]))
    put("f_cw", i["ffn_conv_w_2"].reshape(2, 3, 64, 128).transpose(3, 0, 2, 1))
    put("f_cb", i["ffn_conv_b_2"].reshape(2, 64, 128).transpose(2, 0, 1))
    out["cst"] = cst

    q = np.array(order)
    cls4 = q % 4
    mask = np.zeros((128, 2, 512), f32)
    for ch in range(2):
        tq = q[ch * 128:(ch + 1) * 128, None]
        mask[:, ch, 0:256] = np.where(np.abs(tq - q[None, :]) <= 64, 0, BIG)
        tk = q[None, ch * 128:(ch + 1) * 128]
        mask[:, ch, 256:384] = np.where(tq % 4 == tk % 4, 0, BIG)
        mask[:, ch, 384:512] = np.where(tq % 16 == tk % 16, 0, BIG)
    out["mask"] = mask.reshape(128, 1024)
    tri = np.where(np.arange(128)[:, None] <= np.arange(128)[None, :], 0, -BIG).astype(f32)
    out["tri"] = np.tile(tri, (1, 4))

    pos = i["positions"][0]
    posi = np.zeros((128, 321), np.int32)
    posi[:, 0:64] = pos[q].reshape(64, 4)[:, p // 32].T
    posi[:, 64:320] = pos[q][None, :]
    posi[:, 320] = pos[0]
    out["posi"] = posi
    rb = i["rel_bias"]
    tab = np.zeros((128, 2, 96), f32)
    for kk in range(4):
        for j in range(31):
            tab[kk * 32 + j, 0, kk * 24:kk * 24 + 24] = rb[BUCKET[j]]
            if j:
                tab[kk * 32 + j, 1, kk * 24:kk * 24 + 24] = rb[BUCKET[j - 1]]
    out["tab"] = tab.reshape(128, 192)

    x = i["x"][0]
    out["xp"] = np.ascontiguousarray(x[q].reshape(2, 128, 1024).transpose(1, 0, 2)).reshape(128, 2048)
    out["xn"] = np.ascontiguousarray(x.reshape(2, 128, 1024).transpose(1, 0, 2)).reshape(128, 2048)
    ba = i["b_ada"][0].reshape(6, 1024)
    out["rows"] = np.stack([ba[2], ba[5], i["g_final"], i["norm_mix_post_2"][0], i["norm_ffn_post_2"][0],
                            i["norm_mix_post_2"][1], i["norm_ffn_post_2"][1], i["lru_b_out_2"][0]])

    units = []

    def by_cols(w, n):
        k = w.shape[0] // 128
        a = w.reshape(k, 128, w.shape[1] // n, n).transpose(2, 1, 0, 3)
        return [u.reshape(128, k * n) for u in a]

    def by_rows(w, k):
        a = w.reshape(w.shape[0] // (128 * k), k, 128, w.shape[1]).transpose(0, 2, 1, 3)
        return [u.reshape(128, -1) for u in a]

    ada = i["w_ada"][0]

    def ada_units(cb):
        return by_rows(ada[:, cb * 512:(cb + 1) * 512], 4)

    for cb in ADA_FIRST:
        units += ada_units(cb)
    win = i["w_in"][0]
    kpe = np.arange(640, 704)
    sw = np.concatenate([kpe[32:], kpe[:32]])
    units += by_cols(win[:, np.concatenate([np.arange(640), kpe, kpe])], 256)
    units += by_cols(win[:, np.concatenate([sw, sw])], 128)
    uq = i["w_uq"][0].reshape(384, 8, 192)
    units += by_cols(uq[:, :, :128].reshape(384, 1024), 512)
    pe = uq[:, :, 128:]
    units += by_cols(pe.reshape(384, 512), 512)
    units += by_cols(np.concatenate([pe[:, :, 32:], pe[:, :, :32]], 2).reshape(384, 512), 512)
    ukv = i["w_ukv"][0].reshape(256, 8, 256)
    units += by_cols(ukv[:, :, :128].reshape(256, 1024), 1024)
    units += by_cols(ukv[:, :, 128:].reshape(256, 1024), 1024)
    n = 0
    for hp in range(4):
        for t, g in DIL_UNITS:
            at = DIL0 + ((g * 3 + t) * 8 + 2 * hp) * 128
            units += by_cols(win[:, at:at + 256], 256)
            if ada_after(n) is not None:
                units += ada_units(ada_after(n))
            n += 1
    for j in range(8):
        a = win[:, GATE0 + j * 128:GATE0 + (j + 1) * 128]
        b = win[:, GATE0 + 1024 + j * 128:GATE0 + 1024 + (j + 1) * 128]
        units += by_cols(np.concatenate([a, b], 1), 256)
    units += by_rows(i["w_out"][0], 2)

    sw_in = i["ssd_w_in_2"][0]
    z, xs, b, c, dt = (sw_in[:, s] for s in (slice(0, 2048), slice(2048, 4096), slice(4096, 4608),
                                             slice(4608, 5120), slice(5120, 5152)))
    allc = np.concatenate([dt, dt, dt, dt, b, c, xs, z], 1)
    units += by_cols(allc[:, :5120], 256) + by_cols(allc[:, 5120:], 128)
    units += by_rows(i["ssd_w_out_2"][0], 2)

    def ffn(l):
        up, down = i["ffn_w_up_2"][l], by_rows(i["ffn_w_down_2"][l], 2)
        g, v = by_cols(up[:, :4096], 256), by_cols(up[:, 4096:], 256)
        out = []
        for j in range(16):
            out += [g[j], v[j]] + ([down[j - 1]] if j else [])
        return out + [down[15]]

    units += ffn(0)
    lw = i["lru_w_in_2"][0]
    units += by_cols(lw[:, 1280:], 256)
    units += [i[k][0].transpose(1, 0, 2).reshape(128, 1280) for k in ("lru_w_gx_2", "lru_w_ga_2")]
    units += by_cols(lw[:, :1280], 256)
    units += by_rows(i["lru_w_out_2"][0], 2)
    units += ffn(1)
    out["dense"] = np.concatenate([np.ascontiguousarray(u, dtype=f32).reshape(-1) for u in units])
    for k in ("w_gate", "w_up", "w_down"):
        out[k] = i[k][0]
    return out


DIL_UNITS = [(0, 0), (1, 0), (0, 1), (1, 1), (0, 2), (1, 2), (2, 0), (2, 1), (2, 2)]


def unit_plan():
    ada = [(2048, False)] * 2
    block1 = ada * 4 + [(2048, True)] * 3 + [(1024, True)] + [(1536, True)] * 4 + [(2048, True)] * 2
    for n in range(36):
        block1 += [(2048, True)] + (ada if ada_after(n) is not None else [])
    block1 += [(2048, True)] * 12
    ffn = [(2048, True)] * 48
    block2 = [(2048, True)] * 20 + [(1024, True)] + [(2048, True)] * 8 + ffn
    block2 += [(2048, True)] * 5 + [(1280, False)] * 2 + [(2048, True)] * 10 + ffn
    return block1, block2


def dense_size():
    return 128 * sum(n for b in unit_plan() for n, _ in b)



class Tok:

    def __init__(self, sem, val=0):
        self.sem, self.val, self.used = sem, val, False


def flat(xs):
    for x in xs:
        if isinstance(x, Tok):
            yield x
        elif x is not None:
            yield from flat(x)


class Queue:

    def __init__(self, sem):
        self.sem, self.ops = sem, []

    def do(self, fn, *after):
        tok = Tok(self.sem)
        self.ops.append((fn, list(flat(after)), tok, 1))
        for t in self.ops[-1][1]:
            t.used = True
        return tok

    def dma(self, out, in_, sem, *after):
        sem.count += 16
        tok = Tok(sem.handle, sem.count)
        tok.used = True
        self.ops.append((lambda e: e.dma_start(out, in_), list(flat(after)), tok, 16))
        for t in self.ops[-1][1]:
            t.used = True
        return tok

    def number(self):
        n = 0
        for _, _, tok, inc in self.ops:
            if inc == 1 and tok.used:
                n += 1
                tok.val = n

    def emit(self, e):
        seen = {}
        for fn, after, tok, inc in self.ops:
            need = {}
            for t in after:
                need[t.sem] = max(need.get(t.sem, 0), t.val)
            for sem, val in need.items():
                if seen.get(sem, 0) < val:
                    e.wait_ge(sem, val)
                    seen[sem] = val
            ins = fn(e)
            if tok.used:
                ins.then_inc(tok.sem, inc)


class Arena:

    def __init__(self, nc, name, dt, per=1):
        self.per, self.tensors = per, []
        with ExitStack() as ctx:
            for lo, n in [(0, CONST)] + [(CONST + i * PAGE, PAGE) for i in range(NPAGE)]:
                self.tensors.append((lo, ctx.enter_context(nc.sbuf_tensor(f"{name}_{lo}", [128, n * per], dt))))
        for a, b in SPANS:
            lo, n = CONST + a * PAGE, (b - a + 1) * PAGE
            with nc.sbuf_tensor(f"{name}_below_{a}_{b}", [128, lo * per], dt):
                with nc.sbuf_tensor(f"{name}_span_{a}_{b}", [128, n * per], dt) as t:
                    self.tensors.append((lo, t))

    def __getitem__(self, at):
        p, c = at
        tag, lo = divmod(c.start, TAG)
        i = (NPAGE + tag if tag else 0 if lo < CONST else 1 + (lo - CONST) // PAGE)
        base, t = self.tensors[i]
        lo -= base
        return t[p, lo * self.per:(lo + c.stop - c.start) * self.per]


def page(i):
    return CONST + i * PAGE


def span(a, b):
    return (SPANS.index((a, b)) + 1) * TAG + page(a)


class Slot:

    def __init__(self, at):
        self.at, self.free = at, []


class Ring:
    def __init__(self, ats):
        self.slots, self.i = [Slot(a) for a in ats], 0

    def next(self):
        s = self.slots[self.i % len(self.slots)]
        self.i += 1
        return s


class DmaSem:
    def __init__(self, handle):
        self.handle, self.count = handle, 0


class Unit:
    def __init__(self, src, n, split):
        self.src, self.n, self.split = src, n, split
        self.page = self.loaded = self.tok = self.hl = None




def program(nc, a):
    ctx = ExitStack()
    with ctx:
        F, R, I = (Arena(nc, name, dt) for name, dt in (("F", F32), ("R", F32R), ("I", I32)))
        B = Arena(nc, "B", BF16, 2)
        PB = [ctx.enter_context(nc.psum_tensor(f"ps{i}", [128, 512], F32)) for i in range(8)]

        def sem(name):
            return ctx.enter_context(nc.semaphore(name))

        pe, act, dve, pool, sp = (Queue(sem(f"s_{n}")) for n in ("pe", "act", "dve", "pool", "sp"))
        page_sem = [DmaSem(sem(f"s_page{i}")) for i in range(NPAGE)]

        def fv(at, n, p0=0, p1=128):
            return F[p0:p1, at:at + n]

        def rv(at, n, p0=0, p1=128):
            return R[p0:p1, at:at + n]

        def rf(at, n, p0=0, p1=128):
            return R[p0:p1, at:at + n].bitcast(F32)

        def B16(at, n):
            return B[:, at:at + n // 2]

        def three(ap, n):
            return ap.rearrange("p (a b) -> p a b", b=n)

        def cc(name, i=0, n=1):
            at, _ = CONST_COLS[name]
            return at + i

        def ccol(name, i=0, p0=0, p1=128):
            at = cc(name, i)
            return F[p0:p1, at:at + 1]

        free_at = [NCST]

        def small(n):
            at = free_at[0]
            free_at[0] += n
            assert free_at[0] <= CONST
            return at

        ident = fv(cc("ident"), 128)

        plan1, plan2 = unit_plan()
        units = []
        at = 0
        for n, split in plan1:
            units.append(Unit(a["dense"][at:at + 128 * n].rearrange("(p n) -> p n", p=128), n, split))
            at += 128 * n
        for e in range(NEXP):
            for w in ("w_gate", "w_up"):
                for k in range(8):
                    units.append(Unit(a[w][e, k * 128:(k + 1) * 128, :], 2048, False))
            for c in range(4):
                down = a["w_down"][e].rearrange("(j c p) n -> p j c n", j=4, c=4)
                for j in (0, 2):
                    units.append(Unit(down[:, j:j + 2, c, :], 2048, False))
        for n, split in plan2:
            units.append(Unit(a["dense"][at:at + 128 * n].rearrange("(p n) -> p n", p=128), n, split))
            at += 128 * n

        class W:
            issued = split = taken = 0
            pages, retiring, given = deque(), set(), {}
            hl = deque()

        def pump():
            while W.issued < len(units) and W.pages:
                u = units[W.issued]
                u.page, after = W.pages.popleft()
                W.issued += 1
                dst = fv(page(u.page), u.n)
                if len(u.src.shape) == 3:
                    dst = three(dst, 1024)
                u.loaded = sp.dma(dst, u.src, page_sem[u.page], after)
            while W.split < W.issued:
                u = units[W.split]
                if u.split:
                    if not W.hl:
                        break
                    split_unit(u)
                W.split += 1

        def split_unit(u):
            hi, lo, free = W.hl.popleft()
            u.hl = (hi, lo)
            u.hi, u.lo = page(hi), page(lo)
            src, n = page(u.page), u.n
            th = act.do(lambda e: e.activation(rv(u.hi, n), fv(src, n), ACT.Copy), u.loaded, free)
            u.tok = dve.do(lambda e: e.tensor_tensor(rv(u.lo, n), fv(src, n), rf(u.hi, n), ALU.subtract),
                           th, u.loaded, free)
            give(u.page, [th, u.tok])

        def give(p, toks):
            if p in W.retiring:
                W.retiring.remove(p)
                W.given[p] = toks
            else:
                W.pages.append((p, toks))

        def retire(*ps):
            for p in ps:
                for item in list(W.pages):
                    if item[0] == p:
                        W.pages.remove(item)
                        W.given[p] = item[1]
                        break
                else:
                    W.retiring.add(p)

        def retired(*ps):
            return [W.given.pop(p) for p in ps]

        def take():
            u = units[W.taken]
            assert u.loaded is not None, "not issued"
            assert u.split == (u.tok is not None)
            W.taken += 1
            return u

        def done(u, tok):
            if u.split:
                W.hl.append((*u.hl, [tok]))
            else:
                give(u.page, [tok])
            pump()

        def mm(out, lhsT, rhs, start, stop, *after):
            return pe.do(lambda e: e.matmul(out, lhsT, rhs, start=start, stop=stop), *after)

        def tr(out, in_, *after, n=128):
            return pe.do(lambda e: e.transpose(out, in_, ident if n == 128 else F[0:n, cc("ident"):cc("ident") + n]),
                         *after)

        def acti(out, in_, func, *after, bias=0.0, scale=1.0, accum=None):
            if accum is None:
                return act.do(lambda e: e.activation(out, in_, func, bias=bias, scale=scale), *after)
            return act.do(lambda e: e.activation(out, in_, func, bias=bias, scale=scale, accum_out=accum), *after)

        def tt(out, in0, in1, op, *after, q=None):
            return (q or dve).do(lambda e: e.tensor_tensor(out, in0, in1, op), *after)

        def ts(out, in0, s1, op0, *after, s2=None, op1=None, q=None):
            if op1 is None:
                return (q or dve).do(lambda e: e.tensor_scalar(out, in0, s1, None, op0), *after)
            return (q or dve).do(lambda e: e.tensor_scalar(out, in0, s1, s2, op0, op1), *after)

        def stt(out, in0, s, in1, op0, op1, *after):
            return dve.do(lambda e: e.scalar_tensor_tensor(out=out, in0=in0, scalar=s, in1=in1, op0=op0, op1=op1),
                          *after)

        def cp(out, in_, *after, q=None):
            return (q or dve).do(lambda e: e.tensor_copy(out, in_), *after)

        def red(out, in_, op, *after):
            return dve.do(lambda e: e.tensor_reduce(out, in_, AX.X, op), *after)

        def recip(out, in_, *after):
            return dve.do(lambda e: e.reciprocal(out, in_), *after)

        def zero(out, v, *after, q=None):
            return (q or pool).do(lambda e: e.memset(out, v), *after)

        misc = {}

        def load(name, out, in_, *after):
            if name not in misc:
                misc[name] = DmaSem(sem("s_" + name))
            return sp.dma(out, in_, misc[name], after)

        def fm(u, ncol, nk, xh, xl, bank, tiles, *after, xtok=None, t0=0):
            first = [u.tok, after]
            for t in range(tiles):
                o = PB[bank][:, t * 256:(t + 1) * 256]
                for k in range(nk):
                    w = k * ncol + (t0 + t) * 128
                    wh, wl = rv(u.hi + w, 128), rv(u.lo + w, 128)
                    h, l = rv(xh + k * 256, 256), rv(xl + k * 256, 256)
                    mm(o, wh, h, k == 0, False, first, xtok[k] if xtok and t == 0 else None)
                    mm(o, wh, l, False, False)
                    tok = mm(o, wl, h, False, k == nk - 1)
                    first = None
            return tok

        def tm(u, ncol, c0, n, nk, xh, xl, out, ch, start, stop, *after):
            first = [u.tok, after]
            for k in range(nk):
                w = k * ncol + c0
                wh, wl = rv(u.hi + w, n), rv(u.lo + w, n)
                h, l = rv(xh + k * 256 + ch * 128, 128), rv(xl + k * 256 + ch * 128, 128)
                mm(out, h, wh, start and k == 0, False, first)
                mm(out, h, wl, False, False)
                tok = mm(out, l, wh, False, stop and k == nk - 1)
                first = None
            return tok

        bg = []

        def tick():
            for g in list(bg):
                try:
                    next(g)
                except StopIteration:
                    bg.remove(g)

        class Bank:
            U, S, T, O = Ring([0, 1]), Ring([2, 3]), Ring([4, 5]), Ring([6, 7])

        ms = small(8)
        eps_half = small(4)
        t_eps = [zero(fv(eps_half, 2), -0.5)]

        def rsqrt_small(out, in_, n, *after):
            t = ts(out, in_, EPS, ALU.add, after, q=pool)
            return tt(out, out, F[0:128, eps_half:eps_half + 1].to_broadcast([128, n]), ALU.pow, t, t_eps, q=pool)


        X, HTH, HTL, BIAS = page(0), page(1), page(2), span(3, 6)
        OA, OB, QN, QPE, KN, VM = page(7), page(8), page(9), page(10), page(11), page(12)
        COS, SIN, KPE = QPE + 1024, QPE + 1280, QPE + 1536
        CF, CH, CL = span(13, 14), span(13, 14) + 1280, span(13, 14) + 2560
        XNT, HF = page(18), page(19)

        W.pages.extend([(24, []), (12, [])])

        mod = small(48)
        scale1, scale2 = small(8), small(8)
        cond = small(256)
        ones = small(1)
        t_ones = zero(fv(ones, 1), 1.0)
        inv_n, rcol = small(3), small(4)
        t_inv = [zero(fv(inv_n + i, 1), 1.0 / n) for i, n in enumerate((384, 256, 512))]

        t_cst = load("cst", fv(0, NCST1), a["cst"][:, 0:NCST1])
        posi = page(11)
        t_pos = load("pos", I[:, posi:posi + 321], a["posi"])
        maskat, rel, thr_k, tab = page(8), page(8) + 1024, page(8) + 1344, page(8) + 1408
        t_tab = load("tab", fv(tab + 96, 192), a["tab"])
        pump()
        t_x = load("x", fv(X, 2048), a["xp"])
        t_mask = load("mask", fv(maskat, 1024), a["mask"])
        W.pages.extend([(p, []) for p in (7, 15, 16)])
        pump()
        t_cst2 = load("cst2", fv(NCST1, NCST - NCST1), a["cst"][:, NCST1:NCST])

        t_cond = acti(three(fv(cond, 256), 32), fv(cc("c"), 8).unsqueeze(2).to_broadcast([128, 8, 32]), ACT.Silu, t_cst)

        hi_i, lo_i, hi_f, lo_f = (page(13) + 321 * k for k in range(4))
        posf = page(14)
        iv = lambda at: I[:, at:at + 321]
        ta = ts(iv(hi_i), iv(posi), 16, ALU.arith_shift_right, t_pos)
        tb = ts(iv(lo_i), iv(posi), 65535, ALU.bitwise_and, t_pos)
        t_posf = cp(fv(posf, 256), I[:, posi + 64:posi + 320], t_pos)
        ta = cp(fv(hi_f, 321), iv(hi_i), ta)
        tb = cp(fv(lo_f, 321), iv(lo_i), tb)
        ta = ts(fv(hi_f, 320), fv(hi_f, 320), fv(hi_f + 320, 1), ALU.subtract, ta)
        tb = ts(fv(lo_f, 320), fv(lo_f, 320), fv(lo_f + 320, 1), ALU.subtract, tb)
        t_rel = stt(fv(rel, 320), fv(hi_f, 320), 65536.0, fv(lo_f, 320), ALU.mult, ALU.add, ta, tb)
        t_thr = ts(fv(thr_k, 64), fv(rel, 64), ccol("thr"), ALU.subtract, t_rel, t_cst)
        t_tab = tt(fv(tab, 96), fv(tab + 96, 96), fv(tab + 192, 96), ALU.subtract, t_tab)

        ind_rings = [Ring([page(9), page(9) + 1024]), Ring([page(0), page(0) + 1024])]
        bias_toks = []
        tabv = fv(tab, 96)
        tab0 = tabv.rearrange("p (k h) -> p k h", k=4)[:, :, 0:8]

        def bias_view(ch, at, n):
            return three(fv(BIAS + ch * 4096, 4096), 512)[:, :, at:at + n]

        def mask_view(ch, at, n):
            return fv(maskat + ch * 512 + at, n).unsqueeze(1).to_broadcast([128, 8, n])

        def bias_group(g):
            s = ind_rings[g >= 5].next()
            toks = []
            for i in range(4):
                toks.append(ts(fv(s.at + i * 256, 256), fv(rel + 64, 256), fv(thr_k + 4 * g + i, 1), ALU.is_le,
                               t_rel, t_thr, s.free, q=pool if i == 3 else dve))
            own = g // 8
            b = Bank.S.next()
            for i in range(4):
                q = s.at + i * 256
                mm(PB[b.at][:, i * 96:(i + 1) * 96], fv(q + own * 128, 128), tabv, True, True, toks, t_tab, b.free)
                t = mm(PB[b.at][:, 384 + i * 32:416 + i * 32], fv(q + (1 - own) * 128, 128), tab0, True, True)
            s.free = [t]
            src = PB[b.at][:, 0:384].rearrange("p (k g h) -> p g h k", g=3, h=8)
            src0 = PB[b.at][:, 384:512].rearrange("p (k h) -> p h k", h=8)
            b.free = []
            for ch, at, ps in ((own, 16 * g, src[:, 0]), (1 - own, 16 * g, src0),
                               (own, 256 + 16 * (g % 8), src[:, 1]), (own, 384 + 16 * (g % 8), src[:, 2])):
                b.free.append(tt(bias_view(ch, at, 16), mask_view(ch, at, 16), ps, ALU.subtract, t, t_mask))
            bias_toks.append(b.free[-1])

        part = Ring([page(17) + 512, page(17) + 1024])
        t_mod = {}
        GT = page(14)
        t_gt = {}

        def ada_block(cb):
            b = Bank.U.next()
            for half in range(2):
                u = take()
                for k in range(4):
                    t = mm(PB[b.at][32 * k:32 * k + 32, :], fv(cond + (4 * half + k) * 32, 32),
                           fv(page(u.page) + k * 512, 512), half == 0, half == 1, u.loaded, t_cond, b.free)
                done(u, t)
            s = part.next()
            e = acti(fv(s.at, 512), PB[b.at][:, :], ACT.Copy, t, s.free)
            b.free = [e]
            yield
            b = Bank.T.next()
            if cb in (4, 5, 10, 11):
                t = mm(PB[b.at][:, :], F[:, cc("sel4"):cc("sel4") + 1].to_broadcast([128, 128]), fv(s.at, 512),
                       True, True, e, b.free)
                at = GT + (cb // 10) * 1024 + (cb % 2) * 512
                t_mod[cb] = tt(fv(at, 512), PB[b.at][:, :], fv(at, 512), ALU.add, t, t_gt["rows"])
            else:
                for i in range(4):
                    t = mm(PB[b.at][:, i:i + 1], fv(s.at + i * 128, 128), ccol("sel4"), True, True, e, b.free)
                t_mod[cb] = tt(fv(mod + cb * 4, 4), PB[b.at][:, 0:4], fv(cc("b_ada", cb * 4), 4), ALU.add, t)
            s.free = [t]
            b.free = [t_mod[cb]]

        first = [ada_block(cb) for cb in ADA_FIRST]
        next(first[0])
        bias_group(0)
        bias_group(1)
        next(first[0], None)

        t_sq = [acti(fv(HF + ch * 1024, 1024), fv(X + ch * 1024, 1024), ACT.Square, t_x, scale=1 / 32,
                     accum=fv(ms + ch, 1)) for ch in range(2)]
        t_rs = rsqrt_small(fv(ms + 2, 2), fv(ms, 2), 2, t_sq)
        t_xn = [ts(fv(X + ch * 1024, 1024), fv(X + ch * 1024, 1024), fv(ms + 2 + ch, 1), ALU.mult, t_rs)
                for ch in range(2)]
        t_xnt = []
        for b in range(4):
            s = (Bank.O, Bank.T)[b % 2].next()
            for k in (2 * b, 2 * b + 1):
                for ch in range(2):
                    t = tr(PB[s.at][:, (k % 2) * 256 + ch * 128:(k % 2) * 256 + ch * 128 + 128],
                           fv(X + ch * 1024 + k * 128, 128), t_xn[ch], s.free)
            e = cp(fv(XNT + b * 512, 512), PB[s.at][:, :], t)
            s.free = [e]
            t_xnt.append(e)
        t_xdone = t
        next(first[1])
        bias_group(2)
        next(first[1], None)
        t_s1 = stt(fv(scale1, 8), fv(mod + 8, 8), 1.0, fv(cc("g_mix"), 8), ALU.add, ALU.mult, t_mod[2], t_mod[3])
        next(first[2])
        bias_group(3)
        next(first[2], None)
        next(first[3])
        bias_group(4)
        next(first[3], None)
        t_hf, t_h = [], []
        for k in range(8):
            mods = [t_xnt, t_s1, t_mod[0], t_mod[1]]
            col = dict(scale=fv(scale1 + k, 1), bias=fv(mod + k, 1))
            th = acti(rv(HTH + k * 256, 256), fv(XNT + k * 256, 256), ACT.Identity, mods, **col)
            e = ts(fv(HF + k * 256, 256), fv(XNT + k * 256, 256), col["scale"], ALU.mult, mods, s2=col["bias"],
                   op1=ALU.add)
            t_hf.append(e)
            tl = tt(rv(HTL + k * 256, 256), fv(HF + k * 256, 256), rf(HTH + k * 256, 256), ALU.subtract, th, e)
            t_h.append([th, tl])
        W.hl.extend([(20, 21, []), (22, 23, [])])
        for s in ind_rings[1].slots:
            s.free = [t_xdone]
        pump()

        def bias_rest():
            for g in range(5, 16):
                bias_group(g)
                yield
            give(0, [s.free for s in ind_rings[1].slots])

        bg.append(bias_rest())

        TWO_PI = 6.283185307179586
        P1 = 6.28125
        P2 = float(np.float32(TWO_PI - P1))
        P3 = float(np.float32(TWO_PI - P1 - float(np.float32(TWO_PI - P1))))
        MAGIC = 12582912.0
        ang, kk, rr = (page(14) + 512 + 256 * i for i in range(3))
        t_ang = ts(fv(ang, 256), fv(posf, 256), ccol("invf"), ALU.mult, t_posf, t_cst)
        t_prev = []
        t_rope = []
        for out, quarter in ((COS, 0.25), (SIN, 0.0)):
            t = ts(fv(kk, 256), fv(ang, 256), 1 / TWO_PI, ALU.mult, t_ang, t_prev, s2=quarter, op1=ALU.add)
            t = ts(fv(kk, 256), fv(kk, 256), MAGIC, ALU.add, t)
            t = ts(fv(kk, 256), fv(kk, 256), MAGIC, ALU.subtract, t)
            t = stt(fv(rr, 256), fv(kk, 256), -P1, fv(ang, 256), ALU.mult, ALU.add, t)
            t = stt(fv(rr, 256), fv(kk, 256), -P2, fv(rr, 256), ALU.mult, ALU.add, t)
            t = stt(fv(rr, 256), fv(kk, 256), -P3, fv(rr, 256), ALU.mult, ALU.add, t)
            if quarter:
                t = ts(fv(rr, 256), fv(rr, 256), TWO_PI / 4, ALU.add, t)
            t = ts(fv(rr, 256), fv(rr, 256), 3.1415925, ALU.min, t, s2=-3.1415925, op1=ALU.max)
            t = acti(fv(out, 256), fv(rr, 256), ACT.Sin, t)
            t_prev = [t]
            if not quarter:
                t = ts(fv(out, 256), fv(out, 256), ccol("sgn"), ALU.mult, t)
            t_rope.append(t)

        def next_unit_fm(ncol, nk, xh, xl, tiles, t0=0, u=None, xtok=None, after=None):
            u = u or take()
            b = Bank.U.next()
            t = fm(u, ncol, nk, xh, xl, b.at, tiles, b.free, after, xtok=xtok, t0=t0)
            return u, b, t

        retire(12, 7, 15, 16)
        t_c = []
        startup = [t_rope, t_rel, t_thr, [s.free for s in ind_rings[0].slots]]
        for n in range(2):
            u, b, t = next_unit_fm(256, 8, HTH, HTL, 2, xtok=t_h if n == 0 else None)
            e = acti(fv(CF + n * 512, 512), PB[b.at][:, :], ACT.Copy, t, startup)
            b.free = [e]
            t_c.append(e)
            done(u, t)
            tick()
        u, b, t = next_unit_fm(256, 8, HTH, HTL, 2)
        e = acti(fv(CF + 1024, 256), PB[b.at][:, 0:256], ACT.Copy, t)
        e2 = tt(fv(KPE, 256), PB[b.at][:, 256:512], fv(COS, 256), ALU.mult, e, t_rope[0], startup)
        b.free = [e2]
        t_c.append(e)
        done(u, t)
        tick()
        u, b, t = next_unit_fm(128, 8, HTH, HTL, 1)
        tmp = page(14) + 1792
        e = tt(fv(tmp, 256), PB[b.at][:, 0:256], fv(SIN, 256), ALU.mult, t, t_rope[1], startup)
        b.free = [e]
        done(u, t)
        e = tt(fv(KPE, 256), fv(KPE, 256), fv(tmp, 256), ALU.add, e, e2)
        t_kpe = ts(fv(KPE, 256), fv(KPE, 256), -(192.0 ** -0.5), ALU.mult, e)

        def rstd_rows(sq, n, col, inv, t_sq, bank_c, bank_b):
            b = bank_c.next()
            for ch in range(2):
                for k in range(n):
                    t = mm(PB[b.at][:, ch:ch + 1], fv(sq + k * 256 + ch * 128, 128), fv(inv, 1), k == 0, k == n - 1,
                           t_sq, t_inv, b.free)
            e = ts(fv(col, 2), PB[b.at][:, 0:2], EPS, ALU.add, t)
            b.free = [e]
            t = tt(fv(col, 2), fv(col, 2), F[0:128, eps_half:eps_half + 1].to_broadcast([128, 2]), ALU.pow, e, t_eps,
                   q=pool)
            yield
            b = bank_b.next()
            for ch in range(2):
                t2 = mm(PB[b.at][:, ch * 128:ch * 128 + 128], F[:, col + ch:col + ch + 1].to_broadcast([128, 128]),
                        ident, True, True, t, b.free)
            yield b, t2

        SQ = page(9)
        t_sq = acti(fv(SQ, 1280), fv(CF, 1280), ACT.Square, t_c, startup)
        lat = [rstd_rows(SQ + lo * 256, n, rcol + 2 * (lo > 0), inv_n + (lo > 0), t_sq, Bank.T, Bank.T)
               for lo, n in ((0, 3), (3, 2))]
        for g in lat:
            next(g)
        tick()
        t_cn = []
        for g, lo, hi in ((lat[0], 0, 3), (lat[1], 3, 5)):
            b, t_r = next(g)
            for k in range(lo, hi):
                c = fv(CF + k * 256, 256)
                w = ccol("g_q", k) if lo == 0 else ccol("g_kv", k - 3)
                e = stt(c, c, w, PB[b.at][:, 0:256], ALU.mult, ALU.mult, t_r, t_sq)
                th = acti(rv(CH + k * 256, 256), c, ACT.Copy, e)
                tl = tt(rv(CL + k * 256, 256), c, rf(CH + k * 256, 256), ALU.subtract, th, e)
                t_cn.append([th, tl])
            b.free = [e]

        t_qn, t_qp = [], []
        for n in range(2):
            u = take()
            for half in range(2):
                _, b, t = next_unit_fm(512, 3, CH, CL, 2, t0=2 * half, u=u, after=t_cn)
                h = 4 * n + 2 * half
                e = cp(fv(QN + h * 256, 512), PB[b.at][:, :], t, t_cn, q=dve) if half else \
                    acti(fv(QN + h * 256, 512), PB[b.at][:, :], ACT.Copy, t, t_cn)
                b.free = [e]
                t_qn += [e, e]
            done(u, t)
            tick()
        for n in range(2):
            u = take()
            for half in range(2):
                _, b, t = next_unit_fm(512, 3, CH, CL, 2, t0=2 * half, u=u)
                d = three(fv(QPE + half * 512, 512), 256)
                table = fv((COS, SIN)[n], 256).unsqueeze(1).to_broadcast([128, 2, 256])
                src = three(PB[b.at][:, :], 256)
                if n == 0:
                    e = tt(d, src, table, ALU.mult, t, t_rope)
                    b.free = [e]
                    t_qp.append(e)
                else:
                    e = tt(src, src, table, ALU.mult, t, t_rope)
                    e = tt(d, src, d, ALU.add, e, t_qp[half])
                    b.free = [e]
                    t_qp[half] = e
            done(u, t)
            tick()
        t_qp = [t_qp[0]] * 4 + [t_qp[1]] * 4

        t_kn, t_v = [], []
        u = take()
        for n in range(4):
            _, b, t = next_unit_fm(1024, 2, CH + 768, CL + 768, 2, t0=2 * n, u=u)
            e = acti(fv(KN + n * 512, 512), PB[b.at][:, :], ACT.Copy, t, startup, scale=-(192.0 ** -0.5))
            b.free = [e]
            t_kn += [e, e]
        done(u, t)
        tick()
        u = take()
        t12 = retired(12)
        for ch in range(2):
            for n in range(2):
                b = Bank.U.next()
                t = tm(u, 1024, n * 512, 512, 2, CH + 768, CL + 768, PB[b.at][:, :], ch, True, True, b.free)
                e = cp(fv(VM + ch * 1024 + n * 512, 512), PB[b.at][:, :], t, t12)
                b.free = [e]
                t_v.append(e)
        done(u, t)
        t_lat = t
        give(13, [t_lat, t_cn])
        pump()
        t_gt["rows"] = [load("rows", fv(GT + r * 1024, 1024), a["rows"][r, :].partition_broadcast(128), t_lat, t_cn,
                             t_kpe) for r in range(2)][-1]

        P_RING = Ring([page(18) + 512 * i for i in range(4)])
        PT_RING = Ring([page(19) + 512 * i for i in range(4)])
        st_at = small(32)
        ST_RING = Ring([st_at + 8 * i for i in range(4)])
        t_oa, t_ob = [], []
        t_p0 = [t_h, t_hf]
        for r in (P_RING, PT_RING):
            for s in r.slots:
                s.free = t_p0
        t7 = retired(7)

        def mla_head(h):
            s, p, st = Bank.S.next(), P_RING.next(), ST_RING.next()
            half = 64 * (h % 2)
            for ch in range(2):
                o = PB[s.at][:, ch * 256:(ch + 1) * 256]
                mm(o, fv(QN + h * 256 + ch * 128, 128), fv(KN + h * 256, 256), True, False, s.free, t_qn[h], t_kn[h])
                t = mm(o, fv(QPE + (h // 2) * 256 + ch * 128, 128, half, half + 64), fv(KPE, 256, half, half + 64),
                       False, True, t_qp[h], t_kpe)
            nmx, den, rd = (fv(st.at + 2 * i, 2) for i in range(3))
            t1 = red(nmx, three(PB[s.at][:, :], 256), ALU.min, t, st.free)
            t2 = [acti(fv(p.at + ch * 256, 256), PB[s.at][:, ch * 256:(ch + 1) * 256], ACT.Exp, t, t1, p.free, st.free,
                       bias=fv(st.at + ch, 1), scale=-1.0, accum=fv(st.at + 2 + ch, 1)) for ch in range(2)]
            s.free = t2
            t3 = recip(rd, den, t2)
            t4 = [ts(fv(p.at + ch * 256, 256), fv(p.at + ch * 256, 256), fv(st.at + 4 + ch, 1), ALU.mult, t3)
                  for ch in range(2)]
            st.free = t4
            yield
            s, pt = Bank.T.next(), PT_RING.next()
            for k in range(2):
                for ch in range(2):
                    t = tr(PB[s.at][:, k * 256 + ch * 128:k * 256 + ch * 128 + 128], fv(p.at + ch * 256 + k * 128, 128),
                           t4, s.free)
            p.free = [t]
            e = acti(fv(pt.at, 512), PB[s.at][:, :], ACT.Copy, t, pt.free)
            s.free = [e]
            yield
            s = Bank.O.next()
            for k in range(2):
                t = mm(PB[s.at][:, 0:256], fv(VM + k * 1024 + h * 128, 128), fv(pt.at + k * 256, 256), k == 0, k == 1,
                       e, t_v, s.free)
            pt.free = [t]
            e = acti(fv(OA + h * 256, 256), PB[s.at][:, 0:256], ACT.Copy, t, t7)
            s.free = [e]
            t_oa.append(e)

        DIL = [span(15, 17), span(9, 11)]
        dil_free = [[], []]
        t_bias_read = []

        def dil_item(hp, hh, ch, t_qk, t_vv, pair):
            at = DIL[hp % 2]
            h = 2 * hp + hh
            q = lambda g: fv(at + g * 512 + hh * 256 + ch * 128, 128)
            k = lambda g, c0, n: fv(at + 1536 + g * 512 + hh * 256 + c0, n)
            v = lambda g, c: fv(at + 3072 + g * 512 + c * 256 + hh * 128, 128)
            s, p, st = Bank.S.next(), P_RING.next(), ST_RING.next()
            mm(PB[s.at][:, 0:256], q(0), k(0, 0, 256), True, True, s.free, t_qk)
            mm(PB[s.at][:, 256:384], q(1), k(1, ch * 128, 128), True, True)
            t = mm(PB[s.at][:, 384:512], q(2), k(2, ch * 128, 128), True, True)
            dil_free[hp % 2].append(t)
            nmx, den, rd = (fv(st.at + i, 1) for i in range(3))
            sc, pv, bias = PB[s.at][:, :], fv(p.at, 512), fv(BIAS + ch * 4096 + h * 512, 512)
            t1 = dve.do(lambda e: e.tensor_tensor_reduce(out=pv, in0=sc, in1=bias, scale=1.0, scalar=3e38,
                                                         op0=ALU.add, op1=ALU.min, accum_out=nmx),
                        t, p.free, st.free, bias_toks)
            s.free = [t1]
            t2 = acti(pv, pv, ACT.Exp, t1, bias=nmx, scale=-1.0, accum=den)
            t3 = recip(rd, den, t2)
            t4 = ts(pv, pv, rd, ALU.mult, t3, t2)
            st.free = [t4]
            t_bias_read.append(t1)
            yield
            s, pt = Bank.T.next(), PT_RING.next()
            for i in range(4):
                t = tr(PB[s.at][:, i * 128:(i + 1) * 128], fv(p.at + i * 128, 128), t4, s.free)
            p.free = [t]
            if ch:
                e = acti(fv(pt.at, 512), PB[s.at][:, :], ACT.Copy, t, pt.free)
            else:
                e = cp(fv(pt.at, 512), PB[s.at][:, :], t, pt.free)
            s.free = [e]
            yield
            if "bank" not in pair:
                pair["bank"] = Bank.O.next()
            s = pair["bank"]
            o = PB[s.at][:, hh * 256 + ch * 128:hh * 256 + ch * 128 + 128]
            for i, (g, c) in enumerate(((0, 0), (0, 1), (1, ch), (2, ch))):
                t = mm(o, v(g, c), fv(pt.at + i * 128, 128), i == 0, i == 3, e, t_vv, s.free)
            pt.free = [t]
            dil_free[hp % 2].append(t)
            pair["n"] = pair.get("n", 0) + 1
            if pair["n"] == 4:
                e = cp(fv(OB + hp * 512, 512), PB[s.at][:, :], t, t_ob_free)
                s.free = [e]
                t_ob.append(e)

        def dil_pair(hp, t_qk, t_vv):
            pair = {}
            live = []
            for hh, ch in ((0, 0), (0, 1), (1, 0), (1, 1), (None, None), (None, None)):
                if hh is not None:
                    live.append(dil_item(hp, hh, ch, t_qk, t_vv, pair))
                for g in list(live):
                    if next(g, "end") == "end":
                        live.remove(g)
                yield

        def mla_heads():
            live, h = [], 0
            for n in (2, 2, 1, 1, 1, 1, 0, 0):
                for _ in range(n):
                    live.append(mla_head(h))
                    h += 1
                for g in list(live):
                    if next(g, "end") == "end":
                        live.remove(g)
                yield

        bg.append(mla_heads())
        t_dil_pages = retired(15, 16)
        
        t_ob_free = bias_toks
        n = 0
        for hp in range(4):
            at = DIL[hp % 2]
            free = [dil_free[hp % 2], t_dil_pages if hp == 0 else None, t_oa if hp == 1 else None]
            dil_free[hp % 2] = []
            t_qk, t_vv = [], []
            for i, (t_, g) in enumerate(DIL_UNITS):
                u = take()
                b = Bank.U.next()
                dst = fv(at + t_ * 1536 + g * 512, 512)
                if t_ < 2:
                    t = fm(u, 256, 8, HTH, HTL, b.at, 2, b.free)
                else:
                    for ch in range(2):
                        t = tm(u, 256, 0, 256, 8, HTH, HTL, PB[b.at][:, ch * 256:(ch + 1) * 256], ch, True, True, b.free)
                if t_ == 0:
                    e = acti(dst, PB[b.at][:, :], ACT.Copy, t, free, scale=-(128.0 ** -0.5))
                elif t_ == 1 or g == 0:
                    e = cp(dst, PB[b.at][:, :], t, free)
                else:
                    e = acti(dst, PB[b.at][:, :], ACT.Copy, t, free)
                (t_vv if t_ == 2 else t_qk).append(e)
                b.free = [e]
                done(u, t)
                if ada_after(n) is not None:
                    bg.append(ada_block(ada_after(n)))
                n += 1
                tick()
            if hp == 0:
                assert len(t_oa) == 8 and len(bias_toks) == 16
            bg.append(dil_pair(hp, t_qk, t_vv))

        YH, YL, X1 = page(3), page(4), page(5)
        YF_RING = Ring([page(16) + 512, page(16) + 768])
        nat = lambda ap: ap.rearrange("p (l j c) -> p c j l", l=16, j=4)
        perm = lambda ap: ap.rearrange("p (c j l) -> p c j l", c=4, j=4)
        t_y = []

        def gate_mix(j, g, t_g):
            e1 = tt(fv(g, 256), fv(g, 256), fv(OA + j * 256, 256), ALU.mult, t_g, t_oa)
            e2 = tt(fv(g + 256, 256), fv(g + 256, 256), fv(OB + j * 256, 256), ALU.mult, t_g, t_ob)
            f = YF_RING.next()
            e = tt(nat(fv(f.at, 256)), perm(fv(g, 256)), perm(fv(g + 256, 256)), ALU.add, e1, e2, f.free,
                   t_dil_a)
            th = acti(rv(YH + j * 256, 256), fv(f.at, 256), ACT.Copy, e, t_bias_read)
            tl = tt(rv(YL + j * 256, 256), fv(f.at, 256), rf(YH + j * 256, 256), ALU.subtract, th, e)
            f.free = [th, tl]
            t_y.append([th, tl])

        t_dil_a = dil_free[0]
        gates = []
        for j in range(8):
            u = take()
            b = Bank.U.next()
            t = fm(u, 256, 8, HTH, HTL, b.at, 2, b.free)
            tick()
            g = page(15) + j * 512 if j < 4 else page(12) + (j - 4) * 512
            e = acti(fv(g, 512), PB[b.at][:, :], ACT.Sigmoid, t, t_dil_a if j < 4 else t_oa)
            b.free = [e]
            gates.append((j, g, e))
            done(u, t)
            if j == 5:
                assert len(t_ob) == 4
                t_xr = load("xr", fv(X1, 2048), a["xn"], t_bias_read)
            if j >= 4:
                gate_mix(*gates[j - 4])
        t_h_read = t
        for j in range(4, 8):
            gate_mix(*gates[j])

        def out_units(n, xh, xl, banks, xtok, free):
            for i in range(n):
                u = take()
                for ch in range(2):
                    for half in range(2):
                        for k in range(2):
                            w = k * 1024 + half * 512
                            wh, wl = rv(u.hi + w, 512), rv(u.lo + w, 512)
                            h = rv(xh + (2 * i + k) * 256 + ch * 128, 128)
                            l = rv(xl + (2 * i + k) * 256 + ch * 128, 128)
                            o = PB[banks[2 * ch + half]][:, :]
                            mm(o, h, wh, i == k == 0, False, u.tok, xtok[2 * i + k], free)
                            mm(o, h, wl, False, False)
                            t = mm(o, l, wh, False, i == n - 1 and k == 1)
                done(u, t)
            return t

        banks = [2, 3, 4, 5]
        bank_free = [Bank.S.slots[0].free, Bank.S.slots[1].free, Bank.T.slots[0].free, Bank.T.slots[1].free]
        t_o = out_units(4, YH, YL, banks, t_y, bank_free)
        SC = page(6)
        t_x1 = []
        for ch in range(2):
            for half in range(2):
                o = ch * 1024 + half * 512
                bk = PB[banks[2 * ch + half]][:, :]
                e = tt(fv(SC + o, 512), bk, fv(GT + half * 512, 512), ALU.mult, t_o, t_mod[4], t_mod[5], t_bias_read)
                bank_free[2 * ch + half] = [e]
                t_x1.append(tt(fv(X1 + o, 512), fv(SC + o, 512), fv(X1 + o, 512), ALU.add, e, t_xr))
        for r, i in ((Bank.S, 0), (Bank.T, 2)):
            for k in range(2):
                r.slots[k].free = bank_free[i + k]

        XN2, XNH, XNL, H2T, XET = page(6), page(9), page(10), page(11), span(1, 2)
        t_sq = [acti(fv(XN2 + ch * 1024, 1024), fv(X1 + ch * 1024, 1024), ACT.Square, t_x1, scale=1 / 32,
                     accum=fv(ms + ch, 1)) for ch in range(2)]
        t_rs = rsqrt_small(fv(ms + 2, 2), fv(ms, 2), 2, t_sq)
        t_xn = [ts(fv(XN2 + ch * 1024, 1024), fv(X1 + ch * 1024, 1024), fv(ms + 2 + ch, 1), ALU.mult, t_rs)
                for ch in range(2)]
        t_s2 = stt(fv(scale2, 8), fv(mod + 32, 8), 1.0, fv(cc("g_ffn"), 8), ALU.add, ALU.mult, t_mod[8], t_mod[9])
        t_aff2 = [t_s2, t_mod[6], t_mod[7]]
        t_h2 = []
        dil_b_free = dil_free[1]
        for i in range(4):
            s = (Bank.S, Bank.T)[i % 2].next()
            for k in (2 * i, 2 * i + 1):
                for ch in range(2):
                    o = (k % 2) * 256 + ch * 128
                    t = tr(PB[s.at][:, o:o + 128], fv(XN2 + ch * 1024 + k * 128, 128), t_xn[ch], s.free)
            s.free = []
            for k in (2 * i, 2 * i + 1):
                src = PB[s.at][:, (k % 2) * 256:(k % 2) * 256 + 256]
                if i % 2:
                    e = acti(fv(H2T + k * 256, 256), src, ACT.Identity, t, t_aff2, dil_b_free,
                             bias=fv(mod + 24 + k, 1), scale=fv(scale2 + k, 1))
                else:
                    e = ts(fv(H2T + k * 256, 256), src, fv(scale2 + k, 1), ALU.mult, t, t_aff2, dil_b_free,
                           s2=fv(mod + 24 + k, 1), op1=ALU.add)
                s.free.append(e)
                t_h2.append(e)
        t_xh = [acti(rv(XNH + ch * 1024, 1024), fv(XN2 + ch * 1024, 1024), ACT.Copy, t_xn[ch], dil_b_free)
                for ch in range(2)]

        b = Bank.O.next()
        for ch in range(2):
            for k in range(8):
                t = mm(PB[b.at][:, ch * 16:ch * 16 + 16], fv(H2T + k * 256 + ch * 128, 128),
                       fv(cc("w_router", k * 16), 16), k == 0, k == 7, t_h2, b.free)
        t_lg = t
        RT = page(7)
        lg, aff, mx, sm, rsm = RT, RT + 32, RT + 64, RT + 66, RT + 68
        SLOT, AT, WK, T8, CUM, SEL = (page(8) + 256 * i for i in range(6))
        thr8, nrest = RT + 72, RT + 72 + 32
        t_gm = t_y
        bc = lambda at: fv(at, 2).unsqueeze(2).to_broadcast([128, 2, 16])
        e = red(fv(mx, 2), three(PB[b.at][:, 0:32], 16), ALU.max, t, t_gm)
        e = tt(three(fv(lg, 32), 16), three(PB[b.at][:, 0:32], 16), bc(mx), ALU.subtract, e)
        b.free = [e]
        e = acti(fv(lg, 32), fv(lg, 32), ACT.Exp, e)
        e1 = red(fv(sm, 2), three(fv(lg, 32), 16), ALU.add, e)
        e1 = recip(fv(rsm, 2), fv(sm, 2), e1)
        t_af = tt(three(fv(aff, 32), 16), three(fv(lg, 32), 16), bc(rsm), ALU.mult, e1)
        s = Bank.S.next()
        for ch in range(2):
            t = tr(PB[s.at][0:16, ch * 128:ch * 128 + 128], fv(aff + ch * 16, 16), t_af, s.free)
        w16 = lambda at, n=256: fv(at, n, 0, 16)
        t_at = cp(w16(AT), PB[s.at][0:16, 0:256], t, t_gm)
        s.free = [t_at]
        e = cp(w16(WK), w16(AT), t_at)
        for i in range(4):
            m8 = w16(thr8 + 8 * i, 8)
            e = dve.do(lambda e_, o=m8: e_.max(o, w16(WK)), e)
            if i < 3:
                e = dve.do(lambda e_, o=m8: e_.match_replace(w16(WK), o, w16(WK), -1.0), e)
        thr = w16(thr8 + 31, 1)
        e1 = dve.do(lambda e_: e_.tensor_scalar(w16(SEL), w16(AT), thr, None, ALU.is_gt), e)
        e2 = ts(w16(T8), w16(AT), thr, ALU.is_equal, e)
        e3 = red(w16(nrest, 1), w16(SEL), ALU.add, e1)
        e3 = ts(w16(nrest, 1), w16(nrest, 1), -1.0, ALU.mult, e3, s2=32.0, op1=ALU.add)
        one16 = F[0:16, ones:ones + 1].to_broadcast([16, 256])

        def cumsum(out, in_, *after):
            return dve.do(lambda e_: e_.tensor_tensor_scan(out, one16, in_, 0.0, ALU.mult, ALU.add), after)

        e4 = cumsum(w16(CUM), w16(T8), e2, t_ones)
        e = stt(w16(T8), w16(CUM), w16(nrest, 1), w16(T8), ALU.is_le, ALU.mult, e4, e3)
        e = tt(w16(SEL), w16(SEL), w16(T8), ALU.add, e, e1, e3)
        e1 = cumsum(w16(CUM), w16(SEL), e)
        e = tt(w16(SLOT), w16(CUM), w16(SEL), ALU.mult, e1)
        t_slot = ts(w16(SLOT), w16(SLOT), -1.0, ALU.add, e)

        ST = RT + 160
        s = Bank.S.next()
        for ch in range(2):
            t = tr(PB[s.at][:, ch * 16:ch * 16 + 16], w16(SLOT + ch * 128, 128), t_slot, s.free, n=16)
        e = cp(fv(ST, 32), PB[s.at][:, 0:32], t)
        s.free = [e]
        PH = page(12)
        t_p = []
        iota = fv(cc("iota"), 32)
        for ch in range(2):
            o = rv(PH + ch * 512, 512).rearrange("p (e s) -> p e s", s=32)
            t_p.append(tt(o, fv(ST + ch * 16, 16).unsqueeze(2).to_broadcast([128, 16, 32]),
                          iota.unsqueeze(1).to_broadcast([128, 16, 32]), ALU.is_equal, e, t_y))
        t_xl = [tt(rv(XNL + ch * 1024, 1024), fv(XN2 + ch * 1024, 1024), rf(XNH + ch * 1024, 1024), ALU.subtract,
                   t_xh[ch], dil_b_free) for ch in range(2)]
        t_xe = []
        for k in range(8):
            s = (Bank.S, Bank.T)[k % 2].next()
            for ch in range(2):
                c = ch * 1024 + k * 128
                mm(PB[s.at][:, :], rv(XNH + c, 128), rv(PH + ch * 512, 512), ch == 0, False, t_p, t_xh, t_xl, s.free)
                t = mm(PB[s.at][:, :], rv(XNL + c, 128), rv(PH + ch * 512, 512), False, ch == 1)
            if k % 2:
                e = acti(fv(XET + k * 512, 512), PB[s.at][:, :], ACT.Identity, t, t_aff2, t_h_read,
                         bias=fv(mod + 24 + k, 1), scale=fv(scale2 + k, 1))
            else:
                e = ts(fv(XET + k * 512, 512), PB[s.at][:, :], fv(scale2 + k, 1), ALU.mult, t, t_aff2, t_h_read,
                       s2=fv(mod + 24 + k, 1), op1=ALU.add)
            s.free = [e]
            t_xe.append(e)

        while W.hl:
            hi, lo, free = W.hl.popleft()
            give(hi, free)
            give(lo, free)
        give(18, [s.free for s in P_RING.slots])
        give(19, [s.free for s in PT_RING.slots])
        give(3, [t_o])
        give(4, [t_o])
        give(16, [t_y])
        give(17, [s.free for s in part.slots] + [t_dil_a])
        pump()
        for p in (6, 9, 10, 11):
            give(p, [t, t_xl, t_xn, t_xh, t_h2, t_lg])
        pump()

        XY = Ring([2, 3])
        XY.slots[0].free, XY.slots[1].free = Bank.S.slots[0].free, Bank.S.slots[1].free
        acc = [4, 5, 6, 7]
        acc_free = [Bank.T.slots[0].free, Bank.T.slots[1].free, Bank.O.slots[0].free, Bank.O.slots[1].free]
        SG = Ring([page(7), page(7) + 512])
        HID = Ring([page(7) + 1024, page(7) + 1536])
        PG = Ring([page(8) + 512, page(8) + 768])
        AFB = Ring([page(8) + 1024, page(8) + 1280])
        HT = Ring([page(12) + 1024, page(12) + 1536])
        YR = Ring([page(15), page(15) + 1024])
        for r in (SG, HID, PG, AFB, HT, YR):
            for s in r.slots:
                s.free = [t_p, t_slot, t_y]
        scatter = None
        for e in range(NEXP):
            if e == NEXP - 1:
                retire(18, 19, 20, 21, 22, 23, 3, 4, 6, 9, 10, 11, 13)
            gb, ub = Bank.U.next(), Bank.U.next()
            for b in (gb, ub):
                for k in range(8):
                    u = take()
                    for j in range(4):
                        t = mm(PB[b.at][32 * j:32 * j + 32, :], fv(XET + k * 512 + e * 32, 32),
                               fv(page(u.page) + j * 512, 512), k == 0, k == 7, u.loaded, t_xe, b.free)
                    done(u, t)
                if b is gb:
                    t_g = t
                    if scatter:
                        scatter()
                else:
                    t_u = t
            s, af, pg = XY.next(), AFB.next(), PG.next()
            t = mm(PB[s.at][:, :], F[0:16, cc("ident", e):cc("ident", e) + 1].to_broadcast([16, 128]),
                   fv(SLOT, 512, 0, 16), True, True, t_slot, s.free)
            ta = acti(fv(af.at, 256), PB[s.at][:, 256:512], ACT.Copy, t, af.free)
            t_pg = stt(fv(pg.at, 256), PB[s.at][:, 0:256], ccol("pmod"), fv(af.at, 256), ALU.is_equal, ALU.mult,
                       t, ta, pg.free)
            s.free, af.free = [t_pg], [t_pg]

            sg, hid, ht, y = SG.next(), HID.next(), HT.next(), YR.next()
            t = acti(fv(sg.at, 512), PB[gb.at][:, :], ACT.Silu, t_g, sg.free)
            gb.free = [t]
            t = tt(fv(hid.at, 512), fv(sg.at, 512), PB[ub.at][:, :], ALU.mult, t, t_u, hid.free)
            ub.free, sg.free = [t], [t]
            s = XY.next()
            for c in range(4):
                t2 = tr(PB[s.at][:, c * 128:(c + 1) * 128], fv(hid.at + c * 128, 128), t, s.free)
            hid.free = [t2]
            t_ht = cp(fv(ht.at, 512), PB[s.at][:, :], t2, ht.free)
            s.free = [t_ht]
            yb = [XY.next(), XY.next()]
            for c in range(4):
                for j0 in (0, 2):
                    u = take()
                    for n in range(2):
                        for jj in range(2):
                            j = j0 + jj
                            t = mm(PB[yb[n].at][32 * j:32 * j + 32, :], fv(ht.at + c * 128 + 32 * j, 32),
                                   fv(page(u.page) + jj * 1024 + n * 512, 512), c == 0, c == 3, u.loaded, t_ht,
                                   yb[n].free)
                    done(u, t)
            ht.free = [t]
            t_ye = [acti(fv(y.at, 512), PB[yb[0].at][:, :], ACT.Copy, t, y.free),
                    cp(fv(y.at + 512, 512), PB[yb[1].at][:, :], t, y.free)]
            yb[0].free, yb[1].free = [t_ye[0]], [t_ye[1]]

            def scatter(e=e, y=y, pg=pg, t_ye=t_ye, t_pg=t_pg):
                for ch in range(2):
                    for n in range(2):
                        t = mm(PB[acc[2 * ch + n]][:, :], fv(pg.at + ch * 128, 128), fv(y.at + n * 512, 512),
                               e == 0, e == NEXP - 1, t_ye, t_pg, acc_free)
                y.free, pg.free = [t], [t]
                return t

        t_moe = scatter()
        Y = page(15)
        gfin = GT
        t_gf = load("gfin", fv(gfin, 1024), a["rows"][2, :].partition_broadcast(128), t_x1)
        t_x2 = []
        for ch in range(2):
            for n in range(2):
                o = ch * 1024 + n * 512
                e = tt(fv(Y + o, 512), PB[acc[2 * ch + n]][:, :], fv(GT + 1024 + n * 512, 512), ALU.mult, t_moe,
                       t_mod[10], t_mod[11])
                t_x2.append(tt(fv(X1 + o, 512), fv(Y + o, 512), fv(X1 + o, 512), ALU.add, e))
        t_sq = [acti(fv(Y + ch * 1024, 1024), fv(X1 + ch * 1024, 1024), ACT.Square, t_x2, scale=1 / 32,
                     accum=fv(ms + ch, 1)) for ch in range(2)]
        t_rs = rsqrt_small(fv(ms + 2, 2), fv(ms, 2), 2, t_sq)
        t_x = [stt(fv(X1 + ch * 1024, 1024), fv(X1 + ch * 1024, 1024), fv(ms + 2 + ch, 1), fv(gfin, 1024), ALU.mult,
                   ALU.mult, t_rs, t_gf) for ch in range(2)]

        HT_H, HT_L, SCA, SCB = page(1), page(2), page(11), page(13)
        ROW = page(12)

        def norm_fm(g, t_x, free):
            t_sq = [acti(fv(SCB + ch * 1024, 1024), fv(X1 + ch * 1024, 1024), ACT.Square, t_x[ch], free, scale=1 / 32,
                         accum=fv(ms + ch, 1)) for ch in range(2)]
            t_n = []
            for ch in range(2):
                t_rs = rsqrt_small(fv(ms + 2 + ch, 1), fv(ms + ch, 1), 1, t_sq[ch])
                t_n.append(ts(fv(SCA + ch * 1024, 1024), fv(X1 + ch * 1024, 1024), fv(ms + 2 + ch, 1), ALU.mult,
                              t_rs, free))
            toks = []
            for i in range(4):
                s = (Bank.S, Bank.T)[i % 2].next()
                for k in (2 * i, 2 * i + 1):
                    for ch in range(2):
                        o = (k % 2) * 256 + ch * 128
                        t = tr(PB[s.at][:, o:o + 128], fv(SCA + ch * 1024 + k * 128, 128), t_n[ch], s.free)
                th = [acti(rv(HT_H + k * 256, 256), PB[s.at][:, (k % 2) * 256:(k % 2) * 256 + 256], ACT.Copy, t, free,
                           scale=ccol("pre", g * 8 + k)) for k in (2 * i, 2 * i + 1)]
                tl = [stt(rv(HT_L + k * 256, 256), PB[s.at][:, (k % 2) * 256:(k % 2) * 256 + 256],
                          ccol("pre", g * 8 + k), rf(HT_H + k * 256, 256), ALU.mult, ALU.subtract, th, free)
                      for k in (2 * i, 2 * i + 1)]
                s.free = tl
                toks += [[th, tl[0]], [th, tl[1]]]
            return toks

        def post_norm(banks, row, t_m, t_row, free, add=None):
            t_x = []
            src = {}
            for ch in range(2):
                for h in range(2):
                    i = 2 * ch + h
                    src[i] = PB[banks[i]][:, :]
                    if add is not None:
                        src[i] = fv(SCA + i * 512, 512)
                        t_m[i] = tt(src[i], PB[banks[i]][:, :], fv(add + h * 512, 512), ALU.add, t_m[i], t_row, free)
            for ch in range(2):
                t_sq = [acti(fv(SCB + (2 * ch + h) * 512, 512), src[2 * ch + h], ACT.Square, t_m[2 * ch + h], free,
                             scale=1 / 32, accum=fv(ms + 2 * ch + h, 1)) for h in range(2)]
                t = tt(fv(ms + 2 * ch, 1), fv(ms + 2 * ch, 1), fv(ms + 2 * ch + 1, 1), ALU.add, t_sq, q=pool)
                t_rs = rsqrt_small(fv(ms + 4 + ch, 1), fv(ms + 2 * ch, 1), 1, t)
                es = []
                for h in range(2):
                    o = ch * 1024 + h * 512
                    e = stt(fv(SCA + o, 512), src[2 * ch + h], fv(ms + 4 + ch, 1), fv(row + h * 512, 512),
                            ALU.mult, ALU.mult, t_rs, t_sq, t_row, free)
                    es.append(tt(fv(X1 + o, 512), fv(SCA + o, 512), fv(X1 + o, 512), ALU.add, e))
                t_x.append(es)
            return t_x

        def row_load(name, at, r, *after):
            return load(name, fv(at, 1024), a["rows"][r, :].partition_broadcast(128), after)

        C_Q = [0.0] + [1.0 / (2 * k + 1) for k in range(1, 9)]

        def softplus(out, v, ab, n, tmp, t_v, t_ab):
            e_, s_, q_ = (fv(tmp + i * n, n) for i in range(3))
            t = acti(e_, ab, ACT.Exp, t_ab, scale=-1.0)
            t1 = ts(s_, e_, 2.0, ALU.add, t)
            t1 = recip(s_, s_, t1)
            t1 = tt(s_, s_, e_, ALU.mult, t1)
            t2 = tt(e_, s_, s_, ALU.mult, t1)
            t3 = ts(q_, e_, C_Q[8], ALU.mult, t2)
            for k in range(7, 0, -1):
                t3 = stt(q_, q_, C_Q[k], e_, ALU.add, ALU.mult, t3)
            t3 = stt(q_, q_, 1.0, s_, ALU.add, ALU.mult, t3)
            t4 = ts(v, v, 0.0, ALU.max, t_v)
            return stt(out, q_, 2.0, v, ALU.mult, ALU.add, t3, t4)

        BC, XS, XDT, ST = page(3), span(7, 8), span(9, 10), page(11)
        DT, CS, CSR, TM, DEC, E2_, NEG = (page(4) + i for i in (0, 256, 512, 768, 928, 1056, 1312))
        NEGB = page(4) + 1568
        CBT, BTM, XDD = page(6), page(6) + 1024, page(6) + 1536
        idr, idb = small(32), small(64)
        YGH, YGL = span(9, 10), span(13, 14)

        t_old = [t_x, t_moe]
        given = retired(3, 4, 6, 9, 10, 11, 13)
        t_old += given
        give(15, [t_x2, t_sq])
        t_hl = retired(18, 19, 20, 21, 22, 23)
        for i in range(3):
            W.hl.append((18 + 2 * i, 19 + 2 * i, t_hl[2 * i:2 * i + 2]))
        t_idr = [acti(rv(idr, 32, p, p + 32), fv(cc("ident", p), 32, p, p + 32), ACT.Copy, t_cst) for p in (0, 32)]
        t_idb = cp(B16(idb, 128), ident, t_cst)
        t_tri = load("tri", fv(SCB, 512), a["tri"], t_old)
        t_neg = cp(B16(NEG, 512), fv(SCB, 512), t_tri)
        Bank.U.slots[0].free, Bank.U.slots[1].free = gb.free, ub.free
        if Bank.U.i % 2:
            Bank.U.slots.reverse()
            Bank.U.i = 0
        for r, bs in ((Bank.S, XY.slots), ):
            for s, o in zip(r.slots, bs):
                s.free = o.free
        for s in Bank.T.slots + Bank.O.slots:
            s.free = [t_x2]
        t_h = norm_fm(0, [t_x, t_x], [t_old, t_neg])
        pump()
        t_row = row_load("row0", ROW, 3, t_moe)

        CV = Ring([page(12) + 1024, page(12) + 1536])
        for s in CV.slots:
            s.free = [t_old]
        t_bc, t_xs, t_ys, t_xdt = {}, {}, {}, {}
        D_RING = Ring([page(13) + 512 * i for i in range(4)])
        SC_RING = Ring([page(14) + 512 * i for i in range(4)])
        for r in (D_RING, SC_RING):
            for s in r.slots:
                s.free = [t_h, t_neg]
        XDD_RING = Ring([XDD + 128 * i for i in range(4)])
        E2_RING = Ring([E2_, E2_ + 128])
        ss = {}

        def ssd_dt(b, t):
            v, ab, tmp = ST, ST + 256, ST + 512
            t_v = acti(fv(v, 256), PB[b.at][:, 0:256], ACT.Identity, t, t_h, bias=ccol("dt_b"))
            t_ab = acti(fv(ab, 256), PB[b.at][:, 0:256], ACT.Abs, t, t_h, bias=ccol("dt_b"))
            b.free = [t_ab]
            t_a = acti(fv(ms + 6, 1), ccol("a_log"), ACT.Exp, t_cst2)
            t_dt = softplus(fv(DT, 256), fv(v, 256), fv(ab, 256), 256, tmp, t_v, t_ab)
            t = ts(fv(tmp, 256), fv(DT, 256), fv(ms + 6, 1), ALU.mult, t_dt, t_a, s2=-1.0, op1=ALU.mult)
            one = F[:, ones:ones + 1].to_broadcast([128, 128])
            t_cs = []
            for ch in range(2):
                o, i = fv(CS + ch * 128, 128), fv(tmp + ch * 128, 128)
                t_cs.append(dve.do(lambda e, o=o, i=i: e.tensor_tensor_scan(o, one, i, 0.0, ALU.mult, ALU.add), t))
            t_dec = acti(fv(DEC, 128, 0, 32), fv(CS, 128, 0, 32), ACT.Exp, t_cs, scale=-1.0,
                         bias=F[0:32, CS + 127:CS + 128])
            t1 = acti(rv(CSR, 256, 0, 64), fv(CS, 256, 0, 64), ACT.Copy, t_cs)
            ss["csr"] = tt(rv(CSR, 256, 32, 64), fv(CS, 256, 32, 64), rf(CSR, 256, 32, 64), ALU.subtract, t1)
            ss["dt"] = t_cs
            return t_dec, t_cs

        def ssd_tm(t_dec, t_cs):
            yield
            s = Bank.T.next()
            for i, (src, o) in enumerate(((DT, 0), (DT, 128), (CS, 0), (CS, 128), (DEC, 0))):
                t = tr(PB[s.at][:, i * 32:i * 32 + 32], fv(src + o, 128, 0, 32), t_cs, t_dec, s.free, n=32)
            e1 = cp(fv(TM, 64), PB[s.at][:, 0:64], t)
            e2 = ts(fv(TM + 64, 64), PB[s.at][:, 64:128], -1.0, ALU.mult, t)
            e3 = cp(fv(TM + 128, 32), PB[s.at][:, 128:160], t)
            s.free = [e3]
            ss["tm"] = [e1, e2, e3]

        def ssd_bc():
            yield
            s = Bank.T.next()
            for g in range(4):
                t = tr(PB[s.at][:, g * 128:(g + 1) * 128], fv(BC + g * 256, 128), t_bc[g], s.free)
            s.free = [cp(fv(BTM, 512), PB[s.at][:, :], t)]
            ss["btm"] = s.free
            ss["cbt"] = []
            for half in range(2):
                s = Bank.T.next()
                for g in (2 * half, 2 * half + 1):
                    for ch in range(2):
                        o = (g % 2) * 256 + ch * 128
                        t = mm(PB[s.at][:, o:o + 128], fv(BC + g * 256 + ch * 128, 128),
                               fv(BC + (4 + g) * 256 + ch * 128, 128), True, True, t_bc[g], t_bc[4 + g], s.free)
                s.free = [acti(fv(CBT + half * 512, 512), PB[s.at][:, :], ACT.Copy, t)]
                ss["cbt"] += [s.free, s.free]

        def ssd_tiles(tiles):
            yield
            n = len(tiles)
            i0 = tiles[0]
            s = Bank.T.next()
            for k, i in enumerate(tiles):
                for ch in range(2):
                    t = tr(PB[s.at][:, ch * n * 128 + k * 128:ch * n * 128 + k * 128 + 128],
                           fv(XS + i * 256 + ch * 128, 128), t_xs[i], s.free)
            src = PB[s.at][:, 0:n * 256].rearrange("p (c h q) -> p c h q", c=2, q=64)
            dst = fv(XDT, 4096).rearrange("p (c f) -> p c f", c=2)[:, :, i0 * 128:(i0 + n) * 128]
            dst = dst.rearrange("p c (h q) -> p c h q", q=64)
            dtm = fv(TM, 64).rearrange("p (c h) -> p c h", c=2)[:, :, 2 * i0:2 * (i0 + n)]
            t_xdt = tt(dst, src, dtm.unsqueeze(3).to_broadcast([128, 2, 2 * n, 64]), ALU.mult, t, ss["tm"])
            s.free = [t_xdt]
            sc, t_sc = {}, {}
            for i in tiles:
                s, d, c = Bank.S.next(), D_RING.next(), SC_RING.next()
                mm(PB[s.at][:, :], B16(idb, 128), B16(NEG, 512), True, False, t_idb, t_neg, s.free)
                for hh in range(2):
                    h = 2 * i + hh
                    t = mm(PB[s.at][:, hh * 256:(hh + 1) * 256], R[0:64, idr + h:idr + h + 1].to_broadcast([64, 128]),
                           rv(CSR, 256, 0, 64), False, hh == 1, ss["csr"], t_idr)
                es = []
                for hh in range(2):
                    for ch in range(2):
                        o = hh * 256 + ch * 128
                        es.append(acti(fv(d.at + o, 128), PB[s.at][:, o:o + 128], ACT.Exp, t, d.free, ss["tm"],
                                       bias=fv(TM + 64 + ch * 32 + 2 * i + hh, 1)))
                s.free = [es]
                cb = fv(CBT + (i // 4) * 256, 256).unsqueeze(1).to_broadcast([128, 2, 256])
                t_sc[i] = tt(three(fv(c.at, 512), 256), three(fv(d.at, 512), 256), cb, ALU.mult, es, ss["cbt"][i // 4],
                             c.free, q=pool)
                d.free = [t_sc[i]]
                sc[i] = c
            xd, t_xd = {}, {}
            for i in tiles:
                xd[i] = XDD_RING.next()
                dec = fv(TM + 128 + 2 * i, 2).unsqueeze(2).to_broadcast([128, 2, 64])
                t_xd[i] = tt(three(fv(xd[i].at, 128), 64), three(fv(XDT + i * 128, 128), 64), dec, ALU.mult, t_xdt,
                             xd[i].free, ss["tm"], q=pool)
            yield
            s = Bank.T.next()
            for k, i in enumerate(tiles):
                t = mm(PB[s.at][:, k * 128:(k + 1) * 128], fv(BTM + (i // 4) * 128, 128), fv(xd[i].at, 128), True, True,
                       t_xd[i], ss["btm"], s.free)
                xd[i].free = [t]
            t_st = acti(fv(ST + i0 * 128, n * 128), PB[s.at][:, 0:n * 128], ACT.Copy, t, ss["dt"])
            s.free = [t_st]
            s = Bank.T.next()
            for k, i in enumerate(tiles):
                for hh in range(2):
                    h = cc("ident", 2 * i + hh)
                    t = mm(PB[s.at][hh * 64:hh * 64 + 64, k * 128:(k + 1) * 128],
                           F[0:32, h:h + 1].to_broadcast([32, 64]), fv(CS + 128, 128, 0, 32), True, True, s.free)
            e2 = {}
            s_f = []
            for k, i in enumerate(tiles):
                e2[i] = E2_RING.next()
                e2[i].tok = acti(fv(e2[i].at, 128), PB[s.at][:, k * 128:(k + 1) * 128], ACT.Exp, t, e2[i].free)
                s_f.append(e2[i].tok)
            s.free = s_f
            t_y1 = {}
            for i in tiles:
                s = Bank.O.next()
                for ch in range(2):
                    for hh in range(2):
                        t = mm(PB[s.at][hh * 64:hh * 64 + 64, ch * 128:ch * 128 + 128],
                               fv(XDT + ch * 2048 + i * 128 + hh * 64, 64), fv(sc[i].at + hh * 256 + ch * 128, 128),
                               True, True, t_sc[i], t_xdt, s.free)
                sc[i].free = [t]
                ss["xdt_read"] = t
                x = fv(XS + i * 256, 256)
                t_y1[i] = stt(x, x, ccol("d", i), PB[s.at][:, 0:256], ALU.mult, ALU.add, t)
                s.free = [t_y1[i]]
            yield
            s = Bank.T.next()
            for k, i in enumerate(tiles):
                t = mm(PB[s.at][:, k * 128:(k + 1) * 128], fv(ST + i * 128, 128), fv(BC + (4 + i // 4) * 256 + 128, 128),
                       True, True, t_st, s.free)
            es = []
            for k, i in enumerate(tiles):
                e = tt(fv(e2[i].at, 128), PB[s.at][:, k * 128:(k + 1) * 128], fv(e2[i].at, 128), ALU.mult, t, e2[i].tok)
                es.append(e)
                x = fv(XS + i * 256 + 128, 128)
                t_ys[i] = tt(x, x, fv(e2[i].at, 128), ALU.add, e, t_y1[i])
                e2[i].free = [t_ys[i]]
            s.free = es

        def conv(src, w, bias, taps, out, t, *after):
            ta = [acti(o, s, ACT.Identity, t, after, scale=F[:, wc + taps - 1:wc + taps], bias=F[:, bc:bc + 1])
                  for o, s, wc, bc in zip(out, src, w, bias)]
            last = list(ta)
            for k in range(1, taps):
                for i, (o, s, wc) in enumerate(zip(out, src, w)):
                    last[i] = stt(o[:, k:], s[:, :256 - k], F[:, wc + taps - 1 - k:wc + taps - k], o[:, k:], ALU.mult,
                                  ALU.add, ta, last[i])
            return last

        def ssd_z(i, z, t_z):
            x = fv(XS + i * 256, 256)
            t_ys[i] = tt(x, x, z, ALU.mult, t_z, t_ys[i])
            return t_ys[i]

        t_yg = []

        def ssd_group(g):
            x4 = fv(XS + g * 1024, 1024)
            sq = BC
            t = acti(fv(sq, 1024), x4, ACT.Square, [t_ys[i] for i in range(4 * g, 4 * g + 4)], t_sqfree, ss["btm"], ss["cbt"])
            yield
            r = rstd_rows(sq, 4, rcol, inv_n + 2, t, Bank.S, Bank.S)
            next(r)
            yield
            b, t = next(r)
            es = []
            for i in range(4 * g, 4 * g + 4):
                x = fv(XS + i * 256, 256)
                es.append(stt(x, x, ccol("ssd_n", i), PB[b.at][:, 0:256], ALU.mult, ALU.mult, t, t_ys[i]))
            b.free = es
            t_sqfree[:] = es
            th = acti(rv(YGH + g * 1024, 1024), x4, ACT.Copy, es, ss["xdt_read"])
            tl = tt(rv(YGL + g * 1024, 1024), x4, rf(YGH + g * 1024, 1024), ALU.subtract, th, es,
                    [s.free for s in D_RING.slots + SC_RING.slots])
            t_yg.extend([[th, tl]] * 4)

        t_sqfree = []
        pend = []
        for n in range(21):
            u = take()
            b = Bank.U.next()
            tiles = SSD_TILES[2 * n:2 * n + 2]
            t = fm(u, 128 * len(tiles), 8, HT_H, HT_L, b.at, len(tiles), b.free, xtok=t_h if n == 0 else None)
            cv = CV.next()
            src = {k: PB[b.at][:, k * 256:(k + 1) * 256] for k in range(2)}
            b.free = []
            xt = []
            cvk = [k for k, tl in enumerate(tiles) if tl[0] in "bcx"]
            t_bank = t
            if tiles[0] == "dt":
                t_dec, t_cs = ssd_dt(b, t)
                t_bank = b.free
                bg.append(ssd_tm(t_dec, t_cs))
            if cvk:
                chan = [{"x": 0, "b": 16, "c": 20}[tiles[k][0]] + tiles[k][1] for k in cvk]
                out = [fv(cv.at + k * 256, 256) for k in cvk]
                last = conv([src[k] for k in cvk], [cc("conv_w", c * 4) for c in chan], [cc("conv_b", c) for c in chan],
                            4, out, t_bank, t, cv.free, t_cst2)
                b.free = last
                cv.free = []
                for k, o, tk in zip(cvk, out, last):
                    kind, i = tiles[k]
                    dst = fv(XS + i * 256, 256) if kind == "x" else fv(BC + (i + (4 if kind == "c" else 0)) * 256, 256)
                    e = acti(dst, o, ACT.Silu, tk, t_old)
                    cv.free.append(e)
                    if kind == "x":
                        t_xs[i] = e
                        xt.append(i)
                    else:
                        t_bc[i + (4 if kind == "c" else 0)] = e
            zk = [k for k, tl in enumerate(tiles) if tl[0] == "z"]
            zs = []
            if zk:
                k0, k1 = zk[0], zk[-1] + 1
                e = acti(fv(cv.at + k0 * 256, (k1 - k0) * 256), PB[b.at][:, k0 * 256:k1 * 256], ACT.Silu, t, b.free,
                         cv.free)
                b.free = [b.free, e]
                zs = [(tiles[k][1], fv(cv.at + k * 256, 256), e, cv) for k in zk]
                if len(zk) < len(tiles):
                    cv.free = [cv.free]
            done(u, t)
            tick()
            if ("c", 3) in tiles:
                bg.append(ssd_bc())
            if xt:
                bg.append(ssd_tiles(xt))
            pend += zs
            while pend and pend[0][0] in t_ys:
                i, z, e, c = pend.pop(0)
                assert i in t_ys
                c.free = [c.free, ssd_z(i, z, e)]
                if i % 4 == 3:
                    bg.append(ssd_group(i // 4))
        t_hr = t
        while bg:
            tick()
        assert not pend
        banks = [2, 3, 4, 5]
        bank_free = [s.free for s in Bank.S.slots + Bank.T.slots]
        t_m = out_units(8, YGH, YGL, banks, t_yg, bank_free)
        t_x = post_norm(banks, ROW, [t_m] * 4, t_row, [t_yg, t_m])
        for r, i in ((Bank.S, 0), (Bank.T, 2)):
            for k in range(2):
                r.slots[k].free = t_x[(i + k) // 2]

        def ffn(l, t_x, t_row, row, free):
            t_h = norm_fm(2 * l + 1, t_x, free)
            banks = [2, 3, 4, 5]
            UB = Ring([0, 1, 6, 7])
            for s, o in zip(UB.slots, Bank.U.slots + Bank.O.slots):
                s.free = o.free
            CG = Ring([page(3) + 512 * i for i in range(2)])
            CVV = Ring([page(3) + 1024 + 512 * i for i in range(2)])
            GVH = Ring([page(4) + 512 * i for i in range(2)])
            GVL = Ring([page(4) + 1024 + 512 * i for i in range(2)])
            for r in (CG, CVV, GVH, GVL):
                for s in r.slots:
                    s.free = [free]
            bank_free = [s.free for s in Bank.S.slots + Bank.T.slots]
            pend = None

            def down(j, gh, gl, tok):
                u = take()
                for ch in range(2):
                    for half in range(2):
                        for k in range(2):
                            w = k * 1024 + half * 512
                            wh, wl = rv(u.hi + w, 512), rv(u.lo + w, 512)
                            h = rv(gh.at + k * 256 + ch * 128, 128)
                            lo = rv(gl.at + k * 256 + ch * 128, 128)
                            o = PB[banks[2 * ch + half]][:, :]
                            mm(o, h, wh, j == k == 0, False, u.tok, tok, bank_free, t_h)
                            mm(o, h, wl, False, False)
                            t = mm(o, lo, wh, False, j == 15 and k == 1)
                gh.free, gl.free = [t], [t]
                done(u, t)
                return t

            for j in range(16):
                cvs = []
                for part_, ring in ((0, CG), (1, CVV)):
                    u = take()
                    b, c = UB.next(), ring.next()
                    t = fm(u, 256, 8, HT_H, HT_L, b.at, 2, b.free, xtok=t_h if j == 0 else None)
                    tiles = [32 * part_ + 2 * j + k for k in range(2)]
                    out = [fv(c.at + k * 256, 256) for k in range(2)]
                    last = conv([PB[b.at][:, k * 256:(k + 1) * 256] for k in range(2)],
                                [cc("f_cw", l * 192 + x * 3) for x in tiles], [cc("f_cb", l * 64 + x) for x in tiles],
                                3, out, t, c.free)
                    b.free = last
                    cvs.append((c, last))
                    done(u, t)
                (cg, tg), (cv, tv) = cvs
                gh, gl = GVH.next(), GVL.next()
                e = acti(fv(cg.at, 512), fv(cg.at, 512), ACT.Gelu_apprx_tanh, tg)
                e = tt(fv(cg.at, 512), fv(cg.at, 512), fv(cv.at, 512), ALU.mult, e, tv)
                th = acti(rv(gh.at, 512), fv(cg.at, 512), ACT.Copy, e, gh.free)
                tl = tt(rv(gl.at, 512), fv(cg.at, 512), rf(gh.at, 512), ALU.subtract, th, e, gl.free)
                cg.free, cv.free = [th, tl], [e]
                if pend:
                    down(*pend)
                pend = (j, gh, gl, [th, tl])
            t_hr = t
            t_m = down(*pend)
            t_x = post_norm(banks, row, [t_m] * 4, t_row, [t_m, t_h])
            for s, o in zip(UB.slots, Bank.U.slots + Bank.O.slots):
                o.free = s.free
            for r, i in ((Bank.S, 0), (Bank.T, 2)):
                for k in range(2):
                    r.slots[k].free = t_x[(i + k) // 2]
            return t_x, [t_m, t_hr, t_x]

        t_row = row_load("row1", page(12) + 1024, 4, t_m)
        t_x, t_free = ffn(0, t_x, t_row, page(12) + 1024, [t_x, t_yg, t_hr, t_m])

        t_row = [row_load("row2", page(12), 5, t_free), row_load("row3", page(12) + 1024, 7, t_free)]
        t_h = norm_fm(2, t_x, t_free)
        XBP = 259
        XB, XC, GX, GA, YB = span(3, 4), span(6, 11), span(6, 11) + 2560, span(6, 11) + 5120, span(6, 11) + 7680
        AT_, MU = span(13, 14), span(3, 4)
        t_pad = zero(F[:, XB:XB + 10 * XBP].rearrange("p (t c) -> p t c", c=XBP)[:, :, 0:3], 0.0, t_free)
        xb = lambda i: XB + i * XBP
        lam, lab, ltm = small(10), small(10), small(30)
        t_v = ts(fv(lam, 10), fv(cc("lam"), 10), -1.0, ALU.mult, t_cst2)
        t_ab = acti(fv(lab, 10), fv(lam, 10), ACT.Abs, t_v)
        t = softplus(fv(lab, 10), fv(lam, 10), fv(lab, 10), 10, ltm, [t_v, t_ab], t_ab)
        t_lam = ts(fv(lab, 10), fv(lab, 10), -8.0, ALU.mult, t)
        t_lamn = ts(fv(lam, 10), fv(lab, 10), -1.0, ALU.mult, t_lam)

        t_xc = []
        for n in range(5):
            u = take()
            b = Bank.U.next()
            t = fm(u, 256, 8, HT_H, HT_L, b.at, 2, b.free, xtok=t_h if n == 0 else None)
            ts_ = []
            for k in range(2):
                i = 2 * n + k
                ts_.append(acti(fv(xb(i) + 3, 256), PB[b.at][:, k * 256:(k + 1) * 256], ACT.Identity, t, t_free,
                                bias=ccol("l_bin", 10 + i)))
            b.free = ts_
            last = []
            for k in range(2):
                i = 2 * n + k
                last.append(ts(fv(XC + i * 256, 256), fv(xb(i) + 3, 256), ccol("l_cw", i * 4 + 3), ALU.mult, ts_[k],
                               t_free, s2=ccol("l_cb", i), op1=ALU.add))
            for j in range(1, 4):
                for k in range(2):
                    i = 2 * n + k
                    o = fv(XC + i * 256, 256)
                    last[k] = stt(o, fv(xb(i) + 3 - j, 256), ccol("l_cw", i * 4 + 3 - j), o, ALU.mult, ALU.add, last[k],
                                  t_pad)
            t_xc += last
            done(u, t)
        t_g = {}
        t_yb = []
        for gi, (dst, bn) in enumerate(((GX, "l_bgx"), (GA, "l_bga"))):
            u = take()
            for n in range(5):
                b = Bank.O.next()
                for k in range(2):
                    i = 2 * n + k
                    t = mm(PB[b.at][:, k * 256:(k + 1) * 256], fv(page(u.page) + i * 128, 128), fv(XC + i * 256, 256),
                           True, True, u.loaded, t_xc[i], b.free)
                b.free = []
                for k in range(2):
                    i = 2 * n + k
                    e = acti(fv(dst + i * 256, 256), PB[b.at][:, k * 256:(k + 1) * 256], ACT.Sigmoid, t, t_free,
                             bias=ccol(bn, i))
                    b.free.append(e)
                    t_g[gi, i] = e
            done(u, t)
        t_at = []
        for i in range(10):
            g = fv(GA + i * 256, 256)
            e = acti(fv(AT_ + i * 256, 256), g, ACT.Exp, t_g[1, i], t_lam, t_h, scale=fv(lab + i, 1))
            e2 = acti(g, g, ACT.Tanh, e, t_lamn, scale=fv(lam + i, 1))
            t_at.append([e, e2])
        e = tt(fv(MU, 2560), fv(AT_, 2560), fv(AT_, 2560), ALU.mult, t_at, t_xc)
        e = stt(fv(MU, 2560), fv(MU, 2560), 1.0, fv(GA, 2560), ALU.add, ALU.mult, e)
        e = acti(fv(MU, 2560), fv(MU, 2560), ACT.Sqrt, e)
        e1 = tt(fv(GX, 2560), fv(GX, 2560), fv(XC, 2560), ALU.mult, [t_g[0, i] for i in range(10)], q=pool)
        t_b = tt(fv(MU, 2560), fv(MU, 2560), fv(GX, 2560), ALU.mult, e, e1)
        t_hl = []
        for i in range(10):
            o, at_, bt = fv(GA + i * 256, 256), fv(AT_ + i * 256, 256), fv(MU + i * 256, 256)
            t_hl.append(dve.do(lambda e, o=o, at_=at_, bt=bt: e.tensor_tensor_scan(o, at_, bt, 0.0, ALU.mult, ALU.add),
                               t_b))
        for n in range(5):
            u = take()
            b = Bank.U.next()
            t = fm(u, 256, 8, HT_H, HT_L, b.at, 2, b.free)
            b.free = []
            for k in range(2):
                i = 2 * n + k
                e = acti(fv(YB + i * 256, 256), PB[b.at][:, k * 256:(k + 1) * 256], ACT.Gelu_apprx_tanh, t, t_free,
                         bias=ccol("l_bin", i))
                b.free.append(e)
                t_yb.append(e)
            done(u, t)
        t_hr = t
        YLH, YLL = XC, AT_
        t_yl = []
        for i in range(10):
            f = fv(GA + i * 256, 256)
            e = tt(f, f, fv(YB + i * 256, 256), ALU.mult, t_yb[i], t_hl[i])
            th = acti(rv(YLH + i * 256, 256), f, ACT.Copy, e, e1, t_xc)
            tl = tt(rv(YLL + i * 256, 256), f, rf(YLH + i * 256, 256), ALU.subtract, th, t_hl)
            t_yl.append([th, tl])
        bank_free = [s.free for s in Bank.S.slots + Bank.T.slots]
        t_m = out_units(5, YLH, YLL, banks, t_yl, bank_free)
        t_x = post_norm(banks, page(12), [t_m] * 4, t_row, [t_m, t_yl], add=page(12) + 1024)
        for r, i in ((Bank.S, 0), (Bank.T, 2)):
            for k in range(2):
                r.slots[k].free = t_x[(i + k) // 2]
        t_row = row_load("row4", page(12), 6, t_x)
        t_x, t_free = ffn(1, t_x, t_row, page(12), [t_x, t_m, t_hr])
        ov = a["out"].rearrange("(c p) d -> p c d", p=128)
        for ch in range(2):
            load(f"out{ch}", ov[:, ch, :], fv(X1 + ch * 1024, 1024), t_x[ch])
        assert W.taken == len(units)

        queues = (pe, act, dve, pool, sp)
        all_sems = page_sem + list(misc.values())
        ends = [(s.handle, s.count) for s in all_sems if s.count]
        for q in queues:
            q.number()
        with nc.Block() as block:
            @block.tensor
            def _(e):
                pe.emit(e)

            @block.scalar
            def _(e):
                act.emit(e)

            @block.vector
            def _(e):
                dve.emit(e)

            @block.gpsimd
            def _(e):
                pool.emit(e)

            @block.sync
            def _(e):
                sp.emit(e)
                for handle, count in ends:
                    e.wait_ge(handle, count)



def kernel(**inputs):
    import numpy as _np
    import concourse.bacc as _bacc
    from concourse import mybir as _mybir
    from concourse.bass_utils import run_bass_kernel_spmd as _run

    arrays = lay_out({k: _np.asarray(v) for k, v in inputs.items()})
    nc = _bacc.Bacc("TRN2", target_bir_lowering=False, num_devices=1)
    a = {k: nc.dram_tensor(k, v.shape, _mybir.dt.from_np(v.dtype), kind="ExternalInput").ap()
         for k, v in arrays.items()}
    a["out"] = nc.dram_tensor("out", (SEQ, DM), F32, kind="ExternalOutput").ap()
    program(nc, a)
    r = _run(nc, [arrays], core_ids=[0])
    return r.results[0]["out"].reshape(1, SEQ, DM)
```

```python
import concourse.bass as bass
from concourse import mybir
from contextlib import ExitStack
from collections import deque
import numpy as np

F32 = mybir.dt.float32
F32R = mybir.dt.float32r
BF16 = mybir.dt.bfloat16
I32 = mybir.dt.int32
ALU = mybir.AluOpType
ACT = mybir.ActivationFunctionType
AX = mybir.AxisListType

SEQ = 256
DM = 1024
EPS = 1e-6
BIG = 1e30
NEXP = 16

PAGE = 2048
NPAGE = 25
CONST = 1952

TAG = 1 << 20
SPANS = [(1, 2), (3, 4), (3, 6), (6, 11), (7, 8), (9, 10), (9, 11), (13, 14), (15, 17)]

THRESH = ([-BIG, -558, -304, -165, -90, -49, -26, -14] + list(range(-7, 1))
          + list(range(1, 8)) + [8, 15, 27, 50, 91, 166, 305, 559] + [BIG])
BUCKET = [15, 14, 13, 12, 11, 10, 9, 8, 7, 6, 5, 4, 3, 2, 1, 0] + list(range(17, 32)) + [None]

ADA_FIRST = [2, 0, 3, 1]
ADA_LATER = [4, 5, 6, 7, 8, 9, 10, 11]
DIL0 = 704
DIL_AHEAD = 3
GATE0 = 704 + 9216
SSD_TILES = ["dt"] + [("b", i) for i in range(4)] + [("c", i) for i in range(4)] \
    + [("x", i) for i in range(16)] + [("z", i) for i in range(16)]


def token_order():
    return [16 * l + 4 * j + c for c in range(4) for j in range(4) for l in range(16)]


def ada_after(i):
    return ADA_LATER[i // 4] if i % 4 == 3 and i // 4 < 8 else None



CONST_COLS = {}


def const_layout():
    at = 0
    for name, n in [("ident", 128), ("iota", 32), ("thr", 1), ("invf", 1), ("sgn", 1), ("pmod", 1), ("sel4", 1),
                    ("c", 8), ("g_mix", 8), ("g_ffn", 8), ("b_ada", 48), ("g_q", 3), ("g_kv", 2), ("w_router", 128),
                    ("pre", 32), ("conv_w", 96), ("conv_b", 24), ("dt_b", 1), ("a_log", 1), ("d", 16), ("ssd_n", 16),
                    ("l_bin", 20), ("l_cw", 40), ("l_cb", 10), ("l_bgx", 10), ("l_bga", 10), ("lam", 10),
                    ("f_cw", 384), ("f_cb", 128)]:
        CONST_COLS[name] = (at, n)
        at += n
    return at


NCST = const_layout()
NCST1 = CONST_COLS["pre"][0]


def cols(v):
    return np.ascontiguousarray(np.reshape(v, (-1, 128)).T)


def lay_out(i):
    f32 = np.float32
    order = token_order()
    out = {}
    p = np.arange(128)
    cst = np.zeros((128, NCST), f32)

    def put(name, v):
        at, n = CONST_COLS[name]
        cst[:, at:at + n] = np.reshape(v, (128, n))

    put("ident", np.eye(128, dtype=f32))
    put("iota", np.tile(np.arange(32, dtype=f32), (128, 1)))
    put("thr", np.array(THRESH, f32)[p % 32])
    inv = (10000.0 ** (-np.arange(0, 64, 2, dtype=np.float64) / 64)).astype(f32)
    put("invf", inv[p % 32])
    put("sgn", np.where(p % 64 < 32, -1, 1).astype(f32))
    put("pmod", (p % 32).astype(f32))
    put("sel4", (p % 32 == 0).astype(f32))
    put("c", cols(i["c"][0]))
    put("g_mix", cols(i["g_norm_mix"][0]))
    put("g_ffn", cols(i["g_norm_ffn"][0]))
    put("b_ada", cols(i["b_ada"][0]))
    put("g_q", cols(i["g_q_lat"][0]))
    put("g_kv", cols(i["g_kv_lat"][0]))
    put("w_router", i["w_router"][0].reshape(8, 128, 16).transpose(1, 0, 2))
    put("pre", np.concatenate([cols(i["norm_mix_pre_2"][0]), cols(i["norm_ffn_pre_2"][0]),
                               cols(i["norm_mix_pre_2"][1]), cols(i["norm_ffn_pre_2"][1])], 1))
    put("conv_w", i["ssd_conv_w_2"][0].reshape(4, 24, 128).transpose(2, 1, 0))
    put("conv_b", cols(i["ssd_conv_b_2"][0]))
    put("dt_b", np.tile(i["ssd_dt_bias_2"][0], 4))
    put("a_log", np.tile(i["ssd_a_log_2"][0], 4))
    put("d", cols(np.repeat(i["ssd_d_2"][0], 64)))
    put("ssd_n", cols(i["ssd_norm_2"][0]))
    put("l_bin", cols(i["lru_b_in_2"][0]))
    put("l_cw", i["lru_conv_w_2"][0].reshape(4, 10, 128).transpose(2, 1, 0))
    put("l_cb", cols(i["lru_conv_b_2"][0]))
    put("l_bgx", cols(i["lru_b_gx_2"][0]))
    put("l_bga", cols(i["lru_b_ga_2"][0]))
    put("lam", cols(i["lru_lambda_2"][0]))
    put("f_cw", i["ffn_conv_w_2"].reshape(2, 3, 64, 128).transpose(3, 0, 2, 1))
    put("f_cb", i["ffn_conv_b_2"].reshape(2, 64, 128).transpose(2, 0, 1))
    out["cst"] = cst

    q = np.array(order)
    mask = np.zeros((128, 768), f32)
    for ch in range(2):
        tq = q[ch * 128:(ch + 1) * 128, None]
        mask[:, ch * 256:ch * 256 + 256] = np.where(np.abs(tq - q[None, :]) <= 64, 0, BIG)
    for r, at in ((4, 512), (16, 640)):
        mask[:, at:at + 128] = np.where(q[:128, None] % r == q[None, :128] % r, 0, BIG)
    out["mask"] = mask
    tri = np.where(np.arange(128)[:, None] <= np.arange(128)[None, :], 0, -BIG).astype(f32)
    out["tri"] = np.tile(tri, (1, 4))

    pos = i["positions"][0]
    posi = np.zeros((128, 321), np.int32)
    posi[:, 0:64] = pos[q].reshape(64, 4)[:, p // 32].T
    posi[:, 64:320] = pos[q][None, :]
    posi[:, 320] = pos[0]
    out["posi"] = posi
    rb = i["rel_bias"]
    tab = np.zeros((128, 2, 96), f32)
    for kk in range(4):
        for j in range(31):
            tab[kk * 32 + j, 0, kk * 24:kk * 24 + 24] = rb[BUCKET[j]]
            if j:
                tab[kk * 32 + j, 1, kk * 24:kk * 24 + 24] = rb[BUCKET[j - 1]]
    out["tab"] = tab.reshape(128, 192)

    x = i["x"][0]
    out["xp"] = np.ascontiguousarray(x[q].reshape(2, 128, 1024).transpose(1, 0, 2)).reshape(128, 2048)
    out["xn"] = np.ascontiguousarray(x.reshape(2, 128, 1024).transpose(1, 0, 2)).reshape(128, 2048)
    ba = i["b_ada"][0].reshape(6, 1024)
    out["rows"] = np.stack([ba[2], ba[5], i["g_final"], i["norm_mix_post_2"][0], i["norm_ffn_post_2"][0],
                            i["norm_mix_post_2"][1], i["norm_ffn_post_2"][1], i["lru_b_out_2"][0]])

    units = []

    def by_cols(w, n):
        k = w.shape[0] // 128
        a = w.reshape(k, 128, w.shape[1] // n, n).transpose(2, 1, 0, 3)
        return [u.reshape(128, k * n) for u in a]

    def by_rows(w, k):
        a = w.reshape(w.shape[0] // (128 * k), k, 128, w.shape[1]).transpose(0, 2, 1, 3)
        return [u.reshape(128, -1) for u in a]

    ada = i["w_ada"][0]

    def ada_units(cb):
        return by_rows(ada[:, cb * 512:(cb + 1) * 512], 4)

    win = i["w_in"][0]
    kpe = np.arange(640, 704)
    sw = np.concatenate([kpe[32:], kpe[:32]])
    lat = by_cols(win[:, np.concatenate([np.arange(640), kpe, kpe])], 256)
    lat += by_cols(win[:, np.concatenate([sw, sw])], 128)
    for cb in ADA_FIRST[:3]:
        units += ada_units(cb)
    units += lat[:1] + ada_units(ADA_FIRST[3]) + lat[1:]
    uq = i["w_uq"][0].reshape(384, 8, 192)
    up = by_cols(uq[:, :, :128].reshape(384, 1024), 512)
    pe = uq[:, :, 128:]
    up += by_cols(pe.reshape(384, 512), 512)
    up += by_cols(np.concatenate([pe[:, :, 32:], pe[:, :, :32]], 2).reshape(384, 512), 512)
    ukv = i["w_ukv"][0].reshape(256, 8, 256)
    up += by_cols(ukv[:, :, :128].reshape(256, 1024), 1024)
    up += by_cols(ukv[:, :, 128:].reshape(256, 1024), 1024)
    for n in range(36):
        hp, (t, g) = n // 9, DIL_UNITS[n % 9]
        at = DIL0 + ((g * 3 + t) * 8 + 2 * hp) * 128
        units += (up if n == DIL_AHEAD else []) + by_cols(win[:, at:at + 256], 256)
        if ada_after(n) is not None:
            units += ada_units(ada_after(n))
    for j in range(8):
        a = win[:, GATE0 + j * 128:GATE0 + (j + 1) * 128]
        b = win[:, GATE0 + 1024 + j * 128:GATE0 + 1024 + (j + 1) * 128]
        units += by_cols(np.concatenate([a, b], 1), 256)
    units += by_rows(i["w_out"][0], 2)

    sw_in = i["ssd_w_in_2"][0]
    z, xs, b, c, dt = (sw_in[:, s] for s in (slice(0, 2048), slice(2048, 4096), slice(4096, 4608),
                                             slice(4608, 5120), slice(5120, 5152)))
    allc = np.concatenate([dt, dt, dt, dt, b, c, xs, z], 1)
    units += by_cols(allc[:, :5120], 256) + by_cols(allc[:, 5120:], 128)
    units += by_rows(i["ssd_w_out_2"][0], 2)

    def ffn(l):
        up, down = i["ffn_w_up_2"][l], by_rows(i["ffn_w_down_2"][l], 2)
        g, v = by_cols(up[:, :4096], 256), by_cols(up[:, 4096:], 256)
        out = []
        for j in range(16):
            out += [g[j], v[j]] + ([down[j - 1]] if j else [])
        return out + [down[15]]

    units += ffn(0)
    lw = i["lru_w_in_2"][0]
    units += by_cols(lw[:, 1280:], 256)
    units += [i[k][0].transpose(1, 0, 2).reshape(128, 1280) for k in ("lru_w_gx_2", "lru_w_ga_2")]
    units += by_cols(lw[:, :1280], 256)
    units += by_rows(i["lru_w_out_2"][0], 2)
    units += ffn(1)
    out["dense"] = np.concatenate([np.ascontiguousarray(u, dtype=f32).reshape(-1) for u in units])
    for k in ("w_gate", "w_up", "w_down"):
        out[k] = i[k][0]
    return out


DIL_UNITS = [(0, 0), (1, 0), (0, 1), (1, 1), (0, 2), (1, 2), (2, 0), (2, 1), (2, 2)]


def unit_plan():
    ada = [(2048, False)] * 2
    block1 = ada * 3 + [(2048, True)] + ada + [(2048, True)] * 2 + [(1024, True)]
    for n in range(36):
        block1 += [(1536, True)] * 4 + [(2048, True)] * 2 if n == DIL_AHEAD else []
        block1 += [(2048, True)] + (ada if ada_after(n) is not None else [])
    block1 += [(2048, True)] * 12
    ffn = [(2048, True)] * 48
    block2 = [(2048, True)] * 20 + [(1024, True)] + [(2048, True)] * 8 + ffn
    block2 += [(2048, True)] * 5 + [(1280, False)] * 2 + [(2048, True)] * 10 + ffn
    return block1, block2


def dense_size():
    return 128 * sum(n for b in unit_plan() for n, _ in b)



class Tok:

    def __init__(self, sem, val=0):
        self.sem, self.val, self.used = sem, val, False


def flat(xs):
    for x in xs:
        if isinstance(x, Tok):
            yield x
        elif x is not None:
            yield from flat(x)


class Queue:

    def __init__(self, sem):
        self.sem, self.ops = sem, []

    def do(self, fn, *after):
        tok = Tok(self.sem)
        self.ops.append((fn, list(flat(after)), tok, 1))
        for t in self.ops[-1][1]:
            t.used = True
        return tok

    def dma(self, out, in_, sem, *after):
        sem.count += 16
        tok = Tok(sem.handle, sem.count)
        tok.used = True
        self.ops.append((lambda e: e.dma_start(out, in_), list(flat(after)), tok, 16))
        for t in self.ops[-1][1]:
            t.used = True
        return tok

    def number(self):
        n = 0
        for _, _, tok, inc in self.ops:
            if inc == 1 and tok.used:
                n += 1
                tok.val = n

    def emit(self, e):
        seen = {}
        for fn, after, tok, inc in self.ops:
            need = {}
            for t in after:
                need[t.sem] = max(need.get(t.sem, 0), t.val)
            for sem, val in need.items():
                if seen.get(sem, 0) < val:
                    e.wait_ge(sem, val)
                    seen[sem] = val
            ins = fn(e)
            if tok.used:
                ins.then_inc(tok.sem, inc)


class Arena:

    def __init__(self, nc, name, dt, per=1):
        self.per, self.tensors = per, []
        with ExitStack() as ctx:
            for lo, n in [(0, CONST)] + [(CONST + i * PAGE, PAGE) for i in range(NPAGE)]:
                self.tensors.append((lo, ctx.enter_context(nc.sbuf_tensor(f"{name}_{lo}", [128, n * per], dt))))
        for a, b in SPANS:
            lo, n = CONST + a * PAGE, (b - a + 1) * PAGE
            with nc.sbuf_tensor(f"{name}_below_{a}_{b}", [128, lo * per], dt):
                with nc.sbuf_tensor(f"{name}_span_{a}_{b}", [128, n * per], dt) as t:
                    self.tensors.append((lo, t))

    def __getitem__(self, at):
        p, c = at
        tag, lo = divmod(c.start, TAG)
        i = (NPAGE + tag if tag else 0 if lo < CONST else 1 + (lo - CONST) // PAGE)
        base, t = self.tensors[i]
        lo -= base
        return t[p, lo * self.per:(lo + c.stop - c.start) * self.per]


def page(i):
    return CONST + i * PAGE


def span(a, b):
    return (SPANS.index((a, b)) + 1) * TAG + page(a)


class Slot:

    def __init__(self, at):
        self.at, self.free = at, []


class Ring:
    def __init__(self, ats):
        self.slots, self.i = [a if isinstance(a, Slot) else Slot(a) for a in ats], 0

    def next(self):
        s = self.slots[self.i % len(self.slots)]
        self.i += 1
        return s


class DmaSem:
    def __init__(self, handle):
        self.handle, self.count = handle, 0


class Unit:
    def __init__(self, src, n, split):
        self.src, self.n, self.split = src, n, split
        self.page = self.loaded = self.tok = self.hl = None




def program(nc, a):
    ctx = ExitStack()
    with ctx:
        F, R, I = (Arena(nc, name, dt) for name, dt in (("F", F32), ("R", F32R), ("I", I32)))
        B = Arena(nc, "B", BF16, 2)
        PB = [ctx.enter_context(nc.psum_tensor(f"ps{i}", [128, 512], F32)) for i in range(8)]

        def sem(name):
            return ctx.enter_context(nc.semaphore(name))

        pe, act, dve, pool, sp = (Queue(sem(f"s_{n}")) for n in ("pe", "act", "dve", "pool", "sp"))
        page_sem = [DmaSem(sem(f"s_page{i}")) for i in range(NPAGE)]

        def fv(at, n, p0=0, p1=128):
            return F[p0:p1, at:at + n]

        def rv(at, n, p0=0, p1=128):
            return R[p0:p1, at:at + n]

        def rf(at, n, p0=0, p1=128):
            return R[p0:p1, at:at + n].bitcast(F32)

        def B16(at, n):
            return B[:, at:at + n // 2]

        def three(ap, n):
            return ap.rearrange("p (a b) -> p a b", b=n)

        def cc(name, i=0, n=1):
            at, _ = CONST_COLS[name]
            return at + i

        def ccol(name, i=0, p0=0, p1=128):
            at = cc(name, i)
            return F[p0:p1, at:at + 1]

        free_at = [NCST]

        def small(n):
            at = free_at[0]
            free_at[0] += n
            assert free_at[0] <= CONST
            return at

        ident = fv(cc("ident"), 128)

        plan1, plan2 = unit_plan()
        units = []
        at = 0
        for n, split in plan1:
            units.append(Unit(a["dense"][at:at + 128 * n].rearrange("(p n) -> p n", p=128), n, split))
            at += 128 * n
        for e in range(NEXP):
            for w in ("w_gate", "w_up"):
                for k in range(8):
                    units.append(Unit(a[w][e, k * 128:(k + 1) * 128, :], 2048, False))
            for c in range(4):
                down = a["w_down"][e].rearrange("(j c p) n -> p j c n", j=4, c=4)
                for j in (0, 2):
                    units.append(Unit(down[:, j:j + 2, c, :], 2048, False))
        for n, split in plan2:
            units.append(Unit(a["dense"][at:at + 128 * n].rearrange("(p n) -> p n", p=128), n, split))
            at += 128 * n

        class W:
            issued = split = taken = 0
            pages, retiring, given = deque(), set(), {}
            hl = deque()
            pool_share = 0

        def pump():
            while W.issued < len(units) and W.pages:
                u = units[W.issued]
                u.page, after = W.pages.popleft()
                W.issued += 1
                dst = fv(page(u.page), u.n)
                if len(u.src.shape) == 3:
                    dst = three(dst, 1024)
                u.loaded = sp.dma(dst, u.src, page_sem[u.page], after)
            while W.split < W.issued:
                u = units[W.split]
                if u.split:
                    if not W.hl:
                        break
                    split_unit(u)
                W.split += 1

        def split_unit(u):
            hi, lo, free = W.hl.popleft()
            u.hl = (hi, lo)
            u.hi, u.lo = page(hi), page(lo)
            src, n = page(u.page), u.n
            th = act.do(lambda e: e.activation(rv(u.hi, n), fv(src, n), ACT.Copy), u.loaded, free)
            u.tok = []
            for q, c0, c1 in ((pool, 0, W.pool_share), (dve, W.pool_share, n)):
                if c0 < c1:
                    out, a_, b_ = rv(u.lo + c0, c1 - c0), fv(src + c0, c1 - c0), rf(u.hi + c0, c1 - c0)
                    u.tok.append(tt(out, a_, b_, ALU.subtract, th, u.loaded, free, q=q))
            give(u.page, [th, u.tok])

        def give(p, toks):
            if p in W.retiring:
                W.retiring.remove(p)
                W.given[p] = toks
            else:
                W.pages.append((p, toks))

        def retire(*ps):
            for p in ps:
                for item in list(W.pages):
                    if item[0] == p:
                        W.pages.remove(item)
                        W.given[p] = item[1]
                        break
                else:
                    W.retiring.add(p)

        def retired(*ps):
            return [W.given.pop(p) for p in ps]

        def take():
            u = units[W.taken]
            assert u.loaded is not None, "not issued"
            assert u.split == (u.tok is not None)
            W.taken += 1
            return u

        def done(u, tok):
            if u.split:
                W.hl.append((*u.hl, [tok]))
            else:
                give(u.page, [tok])
            pump()

        def mm(out, lhsT, rhs, start, stop, *after):
            return pe.do(lambda e: e.matmul(out, lhsT, rhs, start=start, stop=stop), *after)

        def tr(out, in_, *after, n=128):
            return pe.do(lambda e: e.transpose(out, in_, ident if n == 128 else F[0:n, cc("ident"):cc("ident") + n]),
                         *after)

        def acti(out, in_, func, *after, bias=0.0, scale=1.0, accum=None):
            if accum is None:
                return act.do(lambda e: e.activation(out, in_, func, bias=bias, scale=scale), *after)
            return act.do(lambda e: e.activation(out, in_, func, bias=bias, scale=scale, accum_out=accum), *after)

        def tt(out, in0, in1, op, *after, q=None):
            return (q or dve).do(lambda e: e.tensor_tensor(out, in0, in1, op), *after)

        def ts(out, in0, s1, op0, *after, s2=None, op1=None, q=None):
            if op1 is None:
                return (q or dve).do(lambda e: e.tensor_scalar(out, in0, s1, None, op0), *after)
            return (q or dve).do(lambda e: e.tensor_scalar(out, in0, s1, s2, op0, op1), *after)

        def stt(out, in0, s, in1, op0, op1, *after, q=None):
            return (q or dve).do(lambda e: e.scalar_tensor_tensor(out=out, in0=in0, scalar=s, in1=in1, op0=op0, op1=op1),
                          *after)

        def cp(out, in_, *after, q=None):
            return (q or dve).do(lambda e: e.tensor_copy(out, in_), *after)

        def red(out, in_, op, *after):
            return dve.do(lambda e: e.tensor_reduce(out, in_, AX.X, op), *after)

        def recip(out, in_, *after):
            return dve.do(lambda e: e.reciprocal(out, in_), *after)

        def zero(out, v, *after, q=None):
            return (q or pool).do(lambda e: e.memset(out, v), *after)

        misc = {}

        def load(name, out, in_, *after):
            if name not in misc:
                misc[name] = DmaSem(sem("s_" + name))
            return sp.dma(out, in_, misc[name], after)

        def fm(u, ncol, nk, xh, xl, bank, tiles, *after, xtok=None, t0=0, k0=0, k1=None):
            first = [u.tok, after]
            for t in range(tiles):
                o = PB[bank][:, t * 256:(t + 1) * 256]
                for k in range(k0, k1 or nk):
                    w = k * ncol + (t0 + t) * 128
                    wh, wl = rv(u.hi + w, 128), rv(u.lo + w, 128)
                    h, l = rv(xh + k * 256, 256), rv(xl + k * 256, 256)
                    mm(o, wh, h, k == 0, False, first, xtok[k] if xtok and t == 0 else None)
                    mm(o, wh, l, False, False)
                    tok = mm(o, wl, h, False, k == nk - 1)
                    first = None
            return tok

        def tm(u, ncol, c0, n, nk, xh, xl, out, ch, start, stop, *after):
            first = [u.tok, after]
            for k in range(nk):
                w = k * ncol + c0
                wh, wl = rv(u.hi + w, n), rv(u.lo + w, n)
                h, l = rv(xh + k * 256 + ch * 128, 128), rv(xl + k * 256 + ch * 128, 128)
                mm(out, h, wh, start and k == 0, False, first)
                mm(out, h, wl, False, False)
                tok = mm(out, l, wh, False, stop and k == nk - 1)
                first = None
            return tok

        bg = []

        def tick():
            for g in list(bg):
                try:
                    next(g)
                except StopIteration:
                    bg.remove(g)

        class Bank:
            U, S, T, O = Ring([0, 1]), Ring([2, 3]), Ring([4, 5]), Ring([6, 7])

        ms = small(8)
        eps_half = small(4)
        t_eps = [zero(fv(eps_half, 2), -0.5)]

        def rsqrt_small(out, in_, n, *after):
            t = ts(out, in_, EPS, ALU.add, after, q=pool)
            return tt(out, out, F[0:128, eps_half:eps_half + 1].to_broadcast([128, n]), ALU.pow, t, t_eps, q=pool)


        X, HTH, HTL, BIAS = page(0), page(1), page(2), span(3, 6)
        OA, OB, QN, QPE, KN, VM = page(7), page(8), page(9), page(10), page(11), page(12)
        COS, SIN, KPA, KPB = (QPE + 1024 + 256 * i for i in range(4))
        CF, CH, CL = span(13, 14), span(13, 14) + 1280, span(13, 14) + 2560
        XNT, HF = page(18), page(19)

        W.pages.extend([(24, []), (12, [])])

        mod = small(48)
        scale1, scale2 = small(8), small(8)
        cond = small(256)
        ones = small(1)
        t_ones = zero(fv(ones, 1), 1.0)
        inv_n, rcol = small(3), small(4)
        t_inv = [zero(fv(inv_n + i, 1), 1.0 / n) for i, n in enumerate((384, 256, 512))]

        t_cst = load("cst", fv(0, NCST1), a["cst"][:, 0:NCST1])
        posi = page(11)
        t_pos = load("pos", I[:, posi:posi + 321], a["posi"])
        maskat, rel, thr_k, tab = page(8), page(8) + 768, page(8) + 1088, page(8) + 1152
        t_tab = load("tab", fv(tab + 96, 192), a["tab"])
        pump()
        t_mask = load("mask", fv(maskat, 768), a["mask"])
        t_x = load("x", fv(X, 2048), a["xp"])
        W.pages.extend([(p, []) for p in (7, 15, 16)])
        pump()
        retire(15, 16)

        t_cond = acti(three(fv(cond, 256), 32), fv(cc("c"), 8).unsqueeze(2).to_broadcast([128, 8, 32]), ACT.Silu, t_cst)

        hi_i, lo_i, hi_f, lo_f = (page(13) + 321 * k for k in range(4))
        posf = page(14)
        iv = lambda at: I[:, at:at + 321]
        ta = t_hi = ts(iv(hi_i), iv(posi), 16, ALU.arith_shift_right, t_pos)
        tb = t_lo = ts(iv(lo_i), iv(posi), 65535, ALU.bitwise_and, t_pos)
        t_posf = cp(fv(posf, 256), I[:, posi + 64:posi + 320], t_pos)
        give(11, [t_posf, t_hi, t_lo])
        pump()
        ta = cp(fv(hi_f, 321), iv(hi_i), ta)
        tb = cp(fv(lo_f, 321), iv(lo_i), tb)
        ta = ts(fv(hi_f, 320), fv(hi_f, 320), fv(hi_f + 320, 1), ALU.subtract, ta)
        tb = ts(fv(lo_f, 320), fv(lo_f, 320), fv(lo_f + 320, 1), ALU.subtract, tb)
        t_rel = stt(fv(rel, 320), fv(hi_f, 320), 65536.0, fv(lo_f, 320), ALU.mult, ALU.add, ta, tb)
        t_thr = ts(fv(thr_k, 64), fv(rel, 64), ccol("thr"), ALU.subtract, t_rel, t_cst)
        tparts = [tab + 288 + 48 * i for i in range(3)]
        t = tt(fv(tab, 96), fv(tab + 96, 96), fv(tab + 192, 96), ALU.subtract, t_tab)
        t = cp(B16(tparts[0], 96), fv(tab, 96), t)
        t = tt(fv(tab, 96), fv(tab, 96), B16(tparts[0], 96), ALU.subtract, t)
        t = cp(B16(tparts[1], 96), fv(tab, 96), t)
        t = tt(fv(tab, 96), fv(tab, 96), B16(tparts[1], 96), ALU.subtract, t)
        t_tab = cp(B16(tparts[2], 96), fv(tab, 96), t)

        IND = [Ring([p + 512 * i for i in range(4)]) for p in (page(9), XNT)]
        bias_banks = Ring(Bank.S.slots)
        bias_toks, bias_reads = [], []
        t_h = []

        def bias_view(ch, at, n):
            return three(fv(BIAS + ch * 4096, 4096), 512)[:, :, at:at + n]

        def bias_start(g):
            s = IND[len(t_h) == 8].next()
            s.tok = []
            for i in range(4):
                s.tok.append(ts(B16(s.at + i * 128, 256), fv(rel + 64, 256), fv(thr_k + 4 * g + i, 1), ALU.is_le,
                                t_rel, t_thr, s.free, q=dve if i < (2 if g < 6 else 1) else pool))
            bias_reads.append(s.tok)
            return s

        def bias_sums(g, s):
            own = g // 8
            b = bias_banks.next()
            for i in range(4):
                for other in range(2):
                    ind = B16(s.at + i * 128 + 64 * (own ^ other), 128)
                    for j, at in enumerate(tparts):
                        if other:
                            o, w = PB[b.at][:, 384 + i * 32:416 + i * 32], B16(at, 96)
                            w = w.rearrange("p (k h) -> p k h", k=4)[:, :, 0:8]
                        else:
                            o, w = PB[b.at][:, i * 96:(i + 1) * 96], B16(at, 96)
                        t = mm(o, ind, w, j == 0, j == 2, s.tok, t_tab, b.free)
            s.free = [t]
            bias_reads.append(t)
            return b, t

        def bias_end(g, b, t):
            own = g // 8
            src = PB[b.at][:, 0:384].rearrange("p (k g h) -> p g h k", g=3, h=8)
            src0 = PB[b.at][:, 384:512].rearrange("p (k h) -> p h k", h=8)
            b.free = []
            for ch, ps in ((own, src[:, 0]), (1 - own, src0)):
                m = fv(maskat + ch * 256 + 16 * g, 16).unsqueeze(1).to_broadcast([128, 8, 16])
                b.free.append(tt(bias_view(ch, 16 * g, 16), m, ps, ALU.subtract, t, t_mask))
            for i in range(2):
                m = fv(maskat + 512 + i * 128 + 16 * (g % 8), 16).unsqueeze(1).to_broadcast([128, 8, 16])
                b.free.append(tt(bias_view(own, 256 + i * 128 + 16 * (g % 8), 16), m, src[:, 1 + i], ALU.subtract, t,
                                 t_mask))
            bias_toks.append(b.free[-1])

        def bias_all():
            s = {g: bias_start(g) for g in range(3)}
            p = {}
            yield
            for g in range(17):
                if g < 13:
                    s[g + 3] = bias_start(g + 3)
                if g < 16:
                    p[g] = bias_sums(g, s[g])
                if g:
                    bias_end(g - 1, *p[g - 1])
                yield
            give(8, [bias_toks, bias_reads])
            pump()

        bias = bias_all()

        part = Ring([page(17) + 512, page(17) + 1024])
        t_mod = {}
        GT = page(14)
        t_gt = {}

        def ada_block(cb):
            b = Bank.U.next()
            for half in range(2):
                u = take()
                for k in range(4):
                    t = mm(PB[b.at][32 * k:32 * k + 32, :], fv(cond + (4 * half + k) * 32, 32),
                           fv(page(u.page) + k * 512, 512), half == 0, half == 1, u.loaded, t_cond, b.free)
                done(u, t)
            s = part.next()
            e = acti(fv(s.at, 512), PB[b.at][:, :], ACT.Copy, t, s.free)
            b.free = [e]
            yield
            b = Bank.T.next()
            if cb in (4, 5, 10, 11):
                t = mm(PB[b.at][:, :], F[:, cc("sel4"):cc("sel4") + 1].to_broadcast([128, 128]), fv(s.at, 512),
                       True, True, e, b.free)
                at = GT + (cb // 10) * 1024 + (cb % 2) * 512
                t_mod[cb] = tt(fv(at, 512), PB[b.at][:, :], fv(at, 512), ALU.add, t, t_gt["rows"])
            else:
                for i in range(4):
                    t = tr(PB[b.at][:, i * 128:(i + 1) * 128], fv(s.at + i * 128, 128), e, b.free)
                m = fv(mod + cb * 4, 4)
                e = red(m, PB[b.at][:, :].rearrange("p (i k r) -> p i k r", k=4, r=32)[:, :, :, 0], ALU.add, t)
                t_mod[cb] = tt(m, m, fv(cc("b_ada", cb * 4), 4), ALU.add, e)
            s.free = [t]
            b.free = [t_mod[cb]]

        next(bias)

        TWO_PI = 6.283185307179586
        P1 = 6.28125
        P2 = float(np.float32(TWO_PI - P1))
        P3 = float(np.float32(TWO_PI - P1 - float(np.float32(TWO_PI - P1))))
        MAGIC = 12582912.0
        ang, kk, rr = (page(14) + 512 + 256 * i for i in range(3))
        t_ang = ts(fv(ang, 256), fv(posf, 256), ccol("invf"), ALU.mult, t_posf, t_cst)

        def rope_table(out, quarter):
            t = ts(fv(kk, 256), fv(ang, 256), 1 / TWO_PI, ALU.mult, t_ang, t_rope, s2=quarter, op1=ALU.add)
            t = ts(fv(kk, 256), fv(kk, 256), MAGIC, ALU.add, t)
            t = ts(fv(kk, 256), fv(kk, 256), MAGIC, ALU.subtract, t)
            t = stt(fv(rr, 256), fv(kk, 256), -P1, fv(ang, 256), ALU.mult, ALU.add, t)
            t = stt(fv(rr, 256), fv(kk, 256), -P2, fv(rr, 256), ALU.mult, ALU.add, t)
            t = stt(fv(rr, 256), fv(kk, 256), -P3, fv(rr, 256), ALU.mult, ALU.add, t)
            if quarter:
                t = ts(fv(rr, 256), fv(rr, 256), TWO_PI / 4, ALU.add, t)
            t = ts(fv(rr, 256), fv(rr, 256), 3.1415925, ALU.min, t, s2=-3.1415925, op1=ALU.max)
            t = acti(fv(out, 256), fv(rr, 256), ACT.Sin, t)
            if not quarter:
                t = ts(fv(out, 256), fv(out, 256), ccol("sgn"), ALU.mult, t)
            t_rope.append(t)

        t_rope = []

        ada = [ada_block(cb) for cb in ADA_FIRST]
        next(ada[0])
        for _ in range(2):
            next(bias)
        next(ada[0], None)

        t_sq = [acti(fv(HF + ch * 1024, 1024), fv(X + ch * 1024, 1024), ACT.Square, t_x, scale=1 / 32,
                     accum=fv(ms + ch, 1)) for ch in range(2)]
        t_rs = rsqrt_small(fv(ms + 2, 2), fv(ms, 2), 2, t_sq)
        t_xn = [ts(fv(X + ch * 1024, 1024), fv(X + ch * 1024, 1024), fv(ms + 2 + ch, 1), ALU.mult, t_rs)
                for ch in range(2)]
        t_xnt = []

        def x_half(half):
            for b in (2 * half, 2 * half + 1):
                s = (Bank.O, Bank.T)[b % 2].next()
                for k in (2 * b, 2 * b + 1):
                    for ch in range(2):
                        t = tr(PB[s.at][:, (k % 2) * 256 + ch * 128:(k % 2) * 256 + ch * 128 + 128],
                               fv(X + ch * 1024 + k * 128, 128), t_xn[ch], s.free)
                e = acti(fv(XNT + b * 512, 512), PB[s.at][:, :], ACT.Copy, t)
                s.free = [e]
                t_xnt.extend([e, e])
            return t

        t_hf, t_s1 = [], []

        def h_half(half):
            o = 4 * half
            t_s1.append(stt(fv(scale1 + o, 4), fv(mod + 8 + o, 4), 1.0, fv(cc("g_mix", o), 4), ALU.add, ALU.mult,
                            t_mod[2 + half]))
            mods = [t_s1[half], t_mod[half]]
            for k in range(o, o + 4):
                col = dict(scale=fv(scale1 + k, 1), bias=fv(mod + k, 1))
                th = acti(rv(HTH + k * 256, 256), fv(XNT + k * 256, 256), ACT.Identity, t_xnt[k], mods, **col)
                e = ts(fv(HF + k * 256, 256), fv(XNT + k * 256, 256), col["scale"], ALU.mult, t_xnt[k], mods,
                       s2=col["bias"], op1=ALU.add, q=pool if k % 2 else dve)
                t_hf.append(e)
                tl = tt(rv(HTL + k * 256, 256), fv(HF + k * 256, 256), rf(HTH + k * 256, 256), ALU.subtract, th, e)
                t_h.append([th, tl])

        next(ada[1])
        x_half(0)
        next(ada[1], None)
        h_half(0)
        give(0, [x_half(1)])
        next(bias)
        next(bias)
        next(ada[2])
        W.hl.append((20, 21, []))
        pump()
        next(bias)
        next(ada[2], None)
        u0, b0 = take(), [Bank.O.next(), Bank.O.next()]
        next(ada[3])
        for i, b in enumerate(b0):
            fm(u0, 256, 8, HTH, HTL, b.at, 1, b.free, xtok=t_h, t0=i, k1=4)
            next(ada[3], None)
        h_half(1)
        W.hl.append((22, 23, []))
        pump()
        t0 = [fm(u0, 256, 8, HTH, HTL, b.at, 1, xtok=[None] * 4 + t_h[4:], t0=i, k0=4) for i, b in enumerate(b0)]
        for s in IND[1].slots:
            s.free = [t_h, t_hf]
        bg.append(bias)

        UO = Ring(Bank.U.slots + Bank.O.slots)

        def next_unit_fm(ncol, nk, xh, xl, tiles, t0=0, u=None, after=None):
            u = u or take()
            b = UO.next()
            t = fm(u, ncol, nk, xh, xl, b.at, tiles, b.free, after, t0=t0)
            return u, b, t

        t_c = []
        startup = [t_rel, t_thr]
        SQ = page(19)
        t_sq = []

        def squares(n, w, e):
            t_sq.append(acti(fv(SQ + n * 512, w), fv(CF + n * 512, w), ACT.Square, e, t_hf, t_h))

        for i, b in enumerate(b0):
            e = acti(fv(CF + i * 256, 256), PB[b.at][:, 0:256], ACT.Copy, t0[i], startup)
            b.free = [e]
            t_c.append(e)
        done(u0, t0[1])
        squares(0, 512, t_c)
        rope_table(COS, 0.25)
        tick()
        for n in range(1, 3):
            u, b, t = next_unit_fm(256, 8, HTH, HTL, 2)
            w = 512 if n < 2 else 256
            e = acti(fv(CF + n * 512, w), PB[b.at][:, 0:w], ACT.Copy, t, startup)
            b.free = [e]
            if n == 2:
                e2 = tt(fv(KPA, 256), PB[b.at][:, 256:512], fv(COS, 256), ALU.mult, e, t_rope[0])
                b.free = [e2]
            t_c.append(e)
            done(u, t)
            squares(n, w, e)
            if n == 1:
                rope_table(SIN, 0.0)
            tick()
        def latent_norm():
            sq = lambda k: fv(SQ + k * 256, 256)
            e = tt(sq(0), sq(0), sq(1), ALU.add, t_sq)
            e = tt(sq(0), sq(0), sq(2), ALU.add, e)
            e2 = tt(sq(3), sq(3), sq(4), ALU.add, t_sq)
            yield
            b = Bank.T.next()
            for i, k in ((0, 0), (1, 3)):
                for ch in range(2):
                    t = mm(PB[b.at][:, 2 * i + ch:2 * i + ch + 1], fv(SQ + k * 256 + ch * 128, 128),
                           fv(inv_n + i, 1), True, True, e, e2, t_inv, b.free)
            r4 = fv(rcol, 4)
            e = ts(r4, PB[b.at][:, 0:4], EPS, ALU.add, t)
            b.free = [e]
            t = tt(r4, r4, F[0:128, eps_half:eps_half + 1].to_broadcast([128, 4]), ALU.pow, e, t_eps, q=pool)
            yield
            b = Bank.T.next()
            for i in range(4):
                t2 = mm(PB[b.at][:, i * 128:i * 128 + 128], F[:, rcol + i:rcol + i + 1].to_broadcast([128, 128]), ident,
                        True, True, t, b.free)
            es = []
            for k in range(5):
                c = fv(CF + k * 256, 256)
                w = ccol("g_q", k) if k < 3 else ccol("g_kv", k - 3)
                r = PB[b.at][:, 0:256] if k < 3 else PB[b.at][:, 256:512]
                es.append(stt(c, c, w, r, ALU.mult, ALU.mult, t2, t_sq))
            for k, e in enumerate(es):
                c = fv(CF + k * 256, 256)
                th = acti(rv(CH + k * 256, 256), c, ACT.Copy, e, t_rope)
                tl = tt(rv(CL + k * 256, 256), c, rf(CH + k * 256, 256), ALU.subtract, th, e)
                t_cn.append([th, tl])
            b.free = [e]

        t_cn = []
        bg.append(latent_norm())
        retire(12)
        u, b, t = next_unit_fm(128, 8, HTH, HTL, 1)
        tmp = page(14) + 1792
        e = tt(fv(tmp, 256), PB[b.at][:, 0:256], fv(SIN, 256), ALU.mult, t, t_rope[1], startup)
        b.free = [e]
        done(u, t)
        e = tt(fv(KPA, 256), fv(KPA, 256), fv(tmp, 256), ALU.add, e, e2)
        t_kp = [zero(fv(KPB, 256, 0, 64), 0.0, q=dve)]
        t_kp.append(ts(fv(KPB, 256, 64, 128), fv(KPA, 256, 64, 128), -(192.0 ** -0.5), ALU.mult, e))
        t_kp.append(ts(fv(KPA, 256, 0, 64), fv(KPA, 256, 0, 64), -(192.0 ** -0.5), ALU.mult, e))
        t_kp.append(zero(fv(KPA, 256, 64, 128), 0.0, t_kp[1], q=dve))
        tick()

        DIL = [span(15, 17), span(9, 11)]
        dil_free = [[], []]
        t_dil_pages = retired(15, 16)
        dil_n = [0]

        def dil_unit(hp, free, t_qk, t_vv):
            n = dil_n[0]
            t_, g = DIL_UNITS[n % 9]
            dil_n[0] += 1
            u = take()
            b = Bank.U.next()
            dst = fv(DIL[hp % 2] + t_ * 1536 + g * 512, 512)
            if t_ < 2:
                t = fm(u, 256, 8, HTH, HTL, b.at, 2, b.free)
            else:
                for ch in range(2):
                    t = tm(u, 256, 0, 256, 8, HTH, HTL, PB[b.at][:, ch * 256:(ch + 1) * 256], ch, True, True, b.free)
            if t_ == 0:
                e = acti(dst, PB[b.at][:, :], ACT.Copy, t, free, scale=-(128.0 ** -0.5))
            elif t_ == 1 or g == 0:
                e = cp(dst, PB[b.at][:, :], t, free)
            else:
                e = acti(dst, PB[b.at][:, :], ACT.Copy, t, free)
            (t_vv if t_ == 2 else t_qk).append(e)
            b.free = [e]
            done(u, t)
            if ada_after(n) is not None:
                bg.append(ada_block(ada_after(n)))
            tick()

        dil_toks = ([], [])
        for _ in range(DIL_AHEAD):
            dil_unit(0, t_dil_pages, *dil_toks)
        t_cst2 = load("cst2", fv(NCST1, NCST - NCST1), a["cst"][:, NCST1:NCST])
        retire(11)
        t_ind = [s.free for s in IND[0].slots]

        t_qn, t_qp = [], []
        for n in range(2):
            u = take()
            for half in range(2):
                _, b, t = next_unit_fm(512, 3, CH, CL, 2, t0=2 * half, u=u, after=t_cn)
                h = 4 * n + 2 * half
                e = cp(fv(QN + h * 256, 512), PB[b.at][:, :], t, t_ind) if half else \
                    acti(fv(QN + h * 256, 512), PB[b.at][:, :], ACT.Copy, t, t_ind)
                b.free = [e]
                t_qn += [e, e]
            done(u, t)
            tick()
        for n in range(2):
            u = take()
            for half in range(2):
                _, b, t = next_unit_fm(512, 3, CH, CL, 2, t0=2 * half, u=u)
                d = three(fv(QPE + half * 512, 512), 256)
                table = fv((COS, SIN)[n], 256).unsqueeze(1).to_broadcast([128, 2, 256])
                src = three(PB[b.at][:, :], 256)
                if n == 0:
                    e = tt(d, src, table, ALU.mult, t, t_rope)
                    b.free = [e]
                    t_qp.append(e)
                else:
                    e = tt(src, src, table, ALU.mult, t, t_rope)
                    e = tt(d, src, d, ALU.add, e, t_qp[half])
                    b.free = [e]
                    t_qp[half] = e
            done(u, t)
            tick()
        t_qp = [t_qp[0]] * 4 + [t_qp[1]] * 4

        P_RING = Ring([page(18) + 512 * i for i in range(4)])
        PT_RING = Ring([page(19) + 512 * i for i in range(4)])
        st_at = small(32)
        ST_RING = Ring([st_at + 8 * i for i in range(4)])
        t_oa, t_ob = [], []
        assert len(bias_toks) >= 15
        t_p0 = [t_h, t_hf, t_cn, t_sq, [s.free for s in IND[1].slots]]
        for r in (P_RING, PT_RING):
            for s in r.slots:
                s.free = t_p0
        t7 = []

        def mla_head(h):
            s, p, st = Bank.S.next(), P_RING.next(), ST_RING.next()
            for ch in range(2):
                o = PB[s.at][:, ch * 256:(ch + 1) * 256]
                mm(o, fv(QN + h * 256 + ch * 128, 128), fv(KN + h * 256, 256), True, False, s.free, t_qn[h], t_kn[h])
                t = mm(o, fv(QPE + (h // 2) * 256 + ch * 128, 128), fv(KPB if h % 2 else KPA, 256), False, True,
                       t_qp[h], t_kp)
            nmx, den, rd = (fv(st.at + 2 * i, 2) for i in range(3))
            t1 = red(nmx, three(PB[s.at][:, :], 256), ALU.min, t, st.free)
            t2 = [acti(fv(p.at + ch * 256, 256), PB[s.at][:, ch * 256:(ch + 1) * 256], ACT.Exp, t, t1, p.free, st.free,
                       bias=fv(st.at + ch, 1), scale=-1.0, accum=fv(st.at + 2 + ch, 1)) for ch in range(2)]
            s.free = t2
            t3 = recip(rd, den, t2)
            t4 = [ts(fv(p.at + ch * 256, 256), fv(p.at + ch * 256, 256), fv(st.at + 4 + ch, 1), ALU.mult, t3)
                  for ch in range(2)]
            st.free = t4
            yield
            s, pt = Bank.T.next(), PT_RING.next()
            for k in range(2):
                for ch in range(2):
                    t = tr(PB[s.at][:, k * 256 + ch * 128:k * 256 + ch * 128 + 128], fv(p.at + ch * 256 + k * 128, 128),
                           t4, s.free)
            p.free = [t]
            e = acti(fv(pt.at, 512), PB[s.at][:, :], ACT.Copy, t, pt.free)
            s.free = [e]
            yield
            s = Bank.O.next()
            if h == 0:
                t7.extend(retired(7))
            for k in range(2):
                t = mm(PB[s.at][:, 0:256], fv(VM + k * 1024 + h * 128, 128), fv(pt.at + k * 256, 256), k == 0, k == 1,
                       e, t_v, s.free)
            pt.free = [t]
            e = acti(fv(OA + h * 256, 256), PB[s.at][:, 0:256], ACT.Copy, t, t7)
            s.free = [e]
            t_oa.append(e)

        def mla_heads():
            live, h = [], 0
            for n in (2, 1, 2, 1, 1, 1, 0, 0):
                for _ in range(n):
                    live.append(mla_head(h))
                    h += 1
                for g in list(live):
                    if next(g, "end") == "end":
                        live.remove(g)
                yield

        t_kn, t_v = [], []
        retire(7)
        u = take()
        t11 = retired(11)
        for n in range(4):
            _, b, t = next_unit_fm(1024, 2, CH + 768, CL + 768, 2, t0=2 * n, u=u)
            e = acti(fv(KN + n * 512, 512), PB[b.at][:, :], ACT.Copy, t, t11, scale=-(192.0 ** -0.5))
            b.free = [e]
            t_kn += [e, e]
        done(u, t)
        bg.append(mla_heads())
        tick()
        u = take()
        t12 = retired(12)
        for ch in range(2):
            for n in range(2):
                b = UO.next()
                t = tm(u, 1024, n * 512, 512, 2, CH + 768, CL + 768, PB[b.at][:, :], ch, True, True, b.free)
                e = cp(fv(VM + ch * 1024 + n * 512, 512), PB[b.at][:, :], t, t12)
                b.free = [e]
                t_v.append(e)
        done(u, t)
        tick()
        t_lat = t
        give(13, [t_lat, t_cn])
        pump()
        t_gt["rows"] = [load("rows", fv(GT + r * 1024, 1024), a["rows"][r, :].partition_broadcast(128), t_lat, t_cn,
                             t_kp) for r in range(2)][-1]

        assert len(bias_toks) == 16
        t_bias_read, t_ob_free = [], []

        def dil_item(hp, hh, ch, t_qk, t_vv, pair):
            at = DIL[hp % 2]
            h = 2 * hp + hh
            q = lambda g: fv(at + g * 512 + hh * 256 + ch * 128, 128)
            k = lambda g, c0, n: fv(at + 1536 + g * 512 + hh * 256 + c0, n)
            v = lambda g, c: fv(at + 3072 + g * 512 + c * 256 + hh * 128, 128)
            s, p, st = Bank.S.next(), P_RING.next(), ST_RING.next()
            mm(PB[s.at][:, 0:256], q(0), k(0, 0, 256), True, True, s.free, t_qk)
            mm(PB[s.at][:, 256:384], q(1), k(1, ch * 128, 128), True, True)
            t = mm(PB[s.at][:, 384:512], q(2), k(2, ch * 128, 128), True, True)
            dil_free[hp % 2].append(t)
            nmx, den, rd = (fv(st.at + i, 1) for i in range(3))
            sc, pv, bias = PB[s.at][:, :], fv(p.at, 512), fv(BIAS + ch * 4096 + h * 512, 512)
            t1 = dve.do(lambda e: e.tensor_tensor_reduce(out=pv, in0=sc, in1=bias, scale=1.0, scalar=3e38,
                                                         op0=ALU.add, op1=ALU.min, accum_out=nmx),
                        t, p.free, st.free, bias_toks)
            s.free = [t1]
            t2 = acti(pv, pv, ACT.Exp, t1, bias=nmx, scale=-1.0, accum=den)
            t3 = recip(rd, den, t2)
            t4 = ts(pv, pv, rd, ALU.mult, t3, t2)
            st.free = [t4]
            t_bias_read.append(t1)
            yield
            s, pt = Bank.T.next(), PT_RING.next()
            for i in range(4):
                t = tr(PB[s.at][:, i * 128:(i + 1) * 128], fv(p.at + i * 128, 128), t4, s.free)
            p.free = [t]
            if ch:
                e = acti(fv(pt.at, 512), PB[s.at][:, :], ACT.Copy, t, pt.free)
            else:
                e = cp(fv(pt.at, 512), PB[s.at][:, :], t, pt.free)
            s.free = [e]
            yield
            if "bank" not in pair:
                pair["bank"] = Bank.O.next()
            s = pair["bank"]
            o = PB[s.at][:, hh * 256 + ch * 128:hh * 256 + ch * 128 + 128]
            for i, (g, c) in enumerate(((0, 0), (0, 1), (1, ch), (2, ch))):
                t = mm(o, v(g, c), fv(pt.at + i * 128, 128), i == 0, i == 3, e, t_vv, s.free)
            pt.free = [t]
            dil_free[hp % 2].append(t)
            pair["n"] = pair.get("n", 0) + 1
            if pair["n"] == 4:
                if hp == 0:
                    t_ob_free.extend(retired(8))
                e = cp(fv(OB + hp * 512, 512), PB[s.at][:, :], t, t_ob_free)
                s.free = [e]
                t_ob.append(e)

        def dil_pair(hp, t_qk, t_vv):
            pair = {}
            live = []
            for hh, ch in ((0, 0), (0, 1), (1, 0), (1, 1), (None, None), (None, None)):
                if hh is not None:
                    live.append(dil_item(hp, hh, ch, t_qk, t_vv, pair))
                for g in list(live):
                    if next(g, "end") == "end":
                        live.remove(g)
                yield

        for hp in range(4):
            free = [dil_free[hp % 2], t_dil_pages if hp == 0 else None, t_oa if hp == 1 else None]
            if hp:
                dil_toks = ([], [])
            dil_free[hp % 2] = []
            while dil_n[0] < 9 * hp + 9:
                dil_unit(hp, free, *dil_toks)
            if hp == 0:
                assert len(t_oa) == 8
                give(12, [t_oa])
                retire(8)
            bg.append(dil_pair(hp, *dil_toks))

        YH, YL, X1 = page(3), page(4), page(5)
        YF_RING = Ring([span(15, 17) + 2 * PAGE, span(15, 17) + 2 * PAGE + 256])
        nat = lambda ap: ap.rearrange("p (l j c) -> p c j l", l=16, j=4)
        perm = lambda ap: ap.rearrange("p (c j l) -> p c j l", c=4, j=4)
        t_y = []

        def gate_mix(j, g, t_g):
            e1 = tt(fv(g, 256), fv(g, 256), fv(OA + j * 256, 256), ALU.mult, t_g, t_oa)
            e2 = tt(fv(g + 256, 256), fv(g + 256, 256), fv(OB + j * 256, 256), ALU.mult, t_g, t_ob)
            f = YF_RING.next()
            e = tt(nat(fv(f.at, 256)), perm(fv(g, 256)), perm(fv(g + 256, 256)), ALU.add, e1, e2, f.free,
                   t_dil_a)
            th = acti(rv(YH + j * 256, 256), fv(f.at, 256), ACT.Copy, e, t_bias_read)
            tl = tt(rv(YL + j * 256, 256), fv(f.at, 256), rf(YH + j * 256, 256), ALU.subtract, th, e)
            f.free = [th, tl]
            t_y.append([th, tl])

        t_dil_a = dil_free[0]
        gates = []
        for j in range(8):
            u = take()
            b = Bank.U.next()
            t = fm(u, 256, 8, HTH, HTL, b.at, 2, b.free)
            tick()
            g = span(15, 17) + j * 512
            e = acti(fv(g, 512), PB[b.at][:, :], ACT.Sigmoid, t, t_dil_a)
            b.free = [e]
            gates.append((j, g, e))
            done(u, t)
            if j == 5:
                retire(12)
                assert len(t_ob) == 4
                t_xr = load("xr", fv(X1, 2048), a["xn"], t_bias_read)
            if j >= 4:
                gate_mix(*gates[j - 4])
        t_h_read = t
        for j in range(4, 8):
            gate_mix(*gates[j])

        def out_units(n, xh, xl, banks, xtok, free, after_each=lambda: None):
            for i in range(n):
                u = take()
                for ch in range(2):
                    for half in range(2):
                        for k in range(2):
                            w = k * 1024 + half * 512
                            wh, wl = rv(u.hi + w, 512), rv(u.lo + w, 512)
                            h = rv(xh + (2 * i + k) * 256 + ch * 128, 128)
                            l = rv(xl + (2 * i + k) * 256 + ch * 128, 128)
                            o = PB[banks[2 * ch + half]][:, :]
                            mm(o, h, wh, i == k == 0, False, u.tok, xtok[2 * i + k], free)
                            mm(o, h, wl, False, False)
                            t = mm(o, l, wh, False, i == n - 1 and k == 1)
                after_each()
                done(u, t)
            return t

        banks = [2, 3, 4, 5]
        bank_free = [Bank.S.slots[0].free, Bank.S.slots[1].free, Bank.T.slots[0].free, Bank.T.slots[1].free]
        t_o = out_units(4, YH, YL, banks, t_y, bank_free)
        SC = page(6)
        t_x1 = []
        for ch in range(2):
            for half in range(2):
                o = ch * 1024 + half * 512
                bk = PB[banks[2 * ch + half]][:, :]
                e = tt(fv(SC + o, 512), bk, fv(GT + half * 512, 512), ALU.mult, t_o, t_mod[4], t_mod[5], t_bias_read)
                bank_free[2 * ch + half] = [e]
                t_x1.append(tt(fv(X1 + o, 512), fv(SC + o, 512), fv(X1 + o, 512), ALU.add, e, t_xr))
        for r, i in ((Bank.S, 0), (Bank.T, 2)):
            for k in range(2):
                r.slots[k].free = bank_free[i + k]

        XN2, XNH, XNL, H2T, XET = page(6), page(9), page(10), page(11), span(1, 2)
        t_sq = [acti(fv(XN2 + ch * 1024, 1024), fv(X1 + ch * 1024, 1024), ACT.Square, t_x1, scale=1 / 32,
                     accum=fv(ms + ch, 1)) for ch in range(2)]
        t_rs = rsqrt_small(fv(ms + 2, 2), fv(ms, 2), 2, t_sq)
        t_xn = [ts(fv(XN2 + ch * 1024, 1024), fv(X1 + ch * 1024, 1024), fv(ms + 2 + ch, 1), ALU.mult, t_rs)
                for ch in range(2)]
        t_s2 = stt(fv(scale2, 8), fv(mod + 32, 8), 1.0, fv(cc("g_ffn"), 8), ALU.add, ALU.mult, t_mod[8], t_mod[9])
        t_aff2 = [t_s2, t_mod[6], t_mod[7]]
        t_h2 = []
        dil_b_free = dil_free[1]
        for i in range(4):
            s = (Bank.S, Bank.T)[i % 2].next()
            for k in (2 * i, 2 * i + 1):
                for ch in range(2):
                    o = (k % 2) * 256 + ch * 128
                    t = tr(PB[s.at][:, o:o + 128], fv(XN2 + ch * 1024 + k * 128, 128), t_xn[ch], s.free)
            s.free = []
            for k in (2 * i, 2 * i + 1):
                src = PB[s.at][:, (k % 2) * 256:(k % 2) * 256 + 256]
                if i % 2:
                    e = acti(fv(H2T + k * 256, 256), src, ACT.Identity, t, t_aff2, dil_b_free,
                             bias=fv(mod + 24 + k, 1), scale=fv(scale2 + k, 1))
                else:
                    e = ts(fv(H2T + k * 256, 256), src, fv(scale2 + k, 1), ALU.mult, t, t_aff2, dil_b_free,
                           s2=fv(mod + 24 + k, 1), op1=ALU.add)
                s.free.append(e)
                t_h2.append(e)
        t_xh = [acti(rv(XNH + ch * 1024, 1024), fv(XN2 + ch * 1024, 1024), ACT.Copy, t_xn[ch], dil_b_free)
                for ch in range(2)]

        b = Bank.O.next()
        for ch in range(2):
            for k in range(8):
                t = mm(PB[b.at][:, ch * 16:ch * 16 + 16], fv(H2T + k * 256 + ch * 128, 128),
                       fv(cc("w_router", k * 16), 16), k == 0, k == 7, t_h2, b.free)
        t_lg = t
        RT = page(7)
        lg, aff, mx, sm, rsm = RT, RT + 32, RT + 64, RT + 66, RT + 68
        SLOT, AT, WK, T8, CUM, SEL = (page(8) + 256 * i for i in range(6))
        thr8, nrest = RT + 72, RT + 72 + 32
        t_gm = t_y
        bc = lambda at: fv(at, 2).unsqueeze(2).to_broadcast([128, 2, 16])
        e = red(fv(mx, 2), three(PB[b.at][:, 0:32], 16), ALU.max, t, t_gm)
        e = tt(three(fv(lg, 32), 16), three(PB[b.at][:, 0:32], 16), bc(mx), ALU.subtract, e)
        b.free = [e]
        e = acti(fv(lg, 32), fv(lg, 32), ACT.Exp, e)
        e1 = red(fv(sm, 2), three(fv(lg, 32), 16), ALU.add, e)
        e1 = recip(fv(rsm, 2), fv(sm, 2), e1)
        t_af = tt(three(fv(aff, 32), 16), three(fv(lg, 32), 16), bc(rsm), ALU.mult, e1)
        s = Bank.S.next()
        for ch in range(2):
            t = tr(PB[s.at][0:16, ch * 128:ch * 128 + 128], fv(aff + ch * 16, 16), t_af, s.free)
        w16 = lambda at, n=256: fv(at, n, 0, 16)
        t_at = cp(w16(AT), PB[s.at][0:16, 0:256], t, t_gm)
        s.free = [t_at]
        e = cp(w16(WK), w16(AT), t_at)
        for i in range(4):
            m8 = w16(thr8 + 8 * i, 8)
            e = dve.do(lambda e_, o=m8: e_.max(o, w16(WK)), e)
            if i < 3:
                e = dve.do(lambda e_, o=m8: e_.match_replace(w16(WK), o, w16(WK), -1.0), e)
        thr = w16(thr8 + 31, 1)
        e1 = dve.do(lambda e_: e_.tensor_scalar(w16(SEL), w16(AT), thr, None, ALU.is_gt), e)
        e2 = ts(w16(T8), w16(AT), thr, ALU.is_equal, e)
        e3 = red(w16(nrest, 1), w16(SEL), ALU.add, e1)
        e3 = ts(w16(nrest, 1), w16(nrest, 1), -1.0, ALU.mult, e3, s2=32.0, op1=ALU.add)
        one16 = F[0:16, ones:ones + 1].to_broadcast([16, 256])

        def cumsum(out, in_, *after):
            return dve.do(lambda e_: e_.tensor_tensor_scan(out, one16, in_, 0.0, ALU.mult, ALU.add), after)

        e4 = cumsum(w16(CUM), w16(T8), e2, t_ones)
        e = stt(w16(T8), w16(CUM), w16(nrest, 1), w16(T8), ALU.is_le, ALU.mult, e4, e3)
        e = tt(w16(SEL), w16(SEL), w16(T8), ALU.add, e, e1, e3)
        e1 = cumsum(w16(CUM), w16(SEL), e)
        e = tt(w16(SLOT), w16(CUM), w16(SEL), ALU.mult, e1)
        t_slot = ts(w16(SLOT), w16(SLOT), -1.0, ALU.add, e)

        ST = RT + 160
        s = Bank.S.next()
        for ch in range(2):
            t = tr(PB[s.at][:, ch * 16:ch * 16 + 16], w16(SLOT + ch * 128, 128), t_slot, s.free, n=16)
        e = cp(fv(ST, 32), PB[s.at][:, 0:32], t)
        s.free = [e]
        PH = page(12)
        t_p = []
        t12 = retired(12)
        iota = fv(cc("iota"), 32)
        for ch in range(2):
            o = rv(PH + ch * 512, 512).rearrange("p (e s) -> p e s", s=32)
            t_p.append(tt(o, fv(ST + ch * 16, 16).unsqueeze(2).to_broadcast([128, 16, 32]),
                          iota.unsqueeze(1).to_broadcast([128, 16, 32]), ALU.is_equal, e, t12))
        t_xl = [tt(rv(XNL + ch * 1024, 1024), fv(XN2 + ch * 1024, 1024), rf(XNH + ch * 1024, 1024), ALU.subtract,
                   t_xh[ch], dil_b_free) for ch in range(2)]
        t_xe = []
        for k in range(8):
            s = (Bank.S, Bank.T)[k % 2].next()
            for ch in range(2):
                c = ch * 1024 + k * 128
                mm(PB[s.at][:, :], rv(XNH + c, 128), rv(PH + ch * 512, 512), ch == 0, False, t_p, t_xh, t_xl, s.free)
                t = mm(PB[s.at][:, :], rv(XNL + c, 128), rv(PH + ch * 512, 512), False, ch == 1)
            if k % 2:
                e = acti(fv(XET + k * 512, 512), PB[s.at][:, :], ACT.Identity, t, t_aff2, t_h_read,
                         bias=fv(mod + 24 + k, 1), scale=fv(scale2 + k, 1))
            else:
                e = ts(fv(XET + k * 512, 512), PB[s.at][:, :], fv(scale2 + k, 1), ALU.mult, t, t_aff2, t_h_read,
                       s2=fv(mod + 24 + k, 1), op1=ALU.add)
            s.free = [e]
            t_xe.append(e)

        while W.hl:
            hi, lo, free = W.hl.popleft()
            give(hi, free)
            give(lo, free)
        give(18, [s.free for s in P_RING.slots])
        give(19, [s.free for s in PT_RING.slots])
        give(3, [t_o])
        give(4, [t_o])
        give(16, [t_y])
        give(17, [s.free for s in part.slots] + [t_dil_a])
        pump()
        for p in (6, 9, 10, 11):
            give(p, [t, t_xl, t_xn, t_xh, t_h2, t_lg])
        pump()

        XY = Ring([2, 3])
        XY.slots[0].free, XY.slots[1].free = Bank.S.slots[0].free, Bank.S.slots[1].free
        acc = [4, 5, 6, 7]
        acc_free = [Bank.T.slots[0].free, Bank.T.slots[1].free, Bank.O.slots[0].free, Bank.O.slots[1].free]
        SG = Ring([page(7), page(7) + 512])
        HID = Ring([page(7) + 1024, page(7) + 1536])
        PG = Ring([page(8) + 512, page(8) + 768])
        AFB = Ring([page(8) + 1024, page(8) + 1280])
        HT = Ring([page(12) + 1024, page(12) + 1536])
        YR = Ring([page(15), page(15) + 1024])
        for r in (SG, HID, PG, AFB, HT, YR):
            for s in r.slots:
                s.free = [t_p, t_slot, t_y, t12]
        scatter = None
        for e in range(NEXP):
            if e == NEXP - 1:
                retire(18, 19, 20, 21, 22, 23, 3, 4, 6, 9, 10, 11, 13, 17)
            gb, ub = Bank.U.next(), Bank.U.next()
            for b in (gb, ub):
                for k in range(8):
                    u = take()
                    for j in range(4):
                        t = mm(PB[b.at][32 * j:32 * j + 32, :], fv(XET + k * 512 + e * 32, 32),
                               fv(page(u.page) + j * 512, 512), k == 0, k == 7, u.loaded, t_xe, b.free)
                    done(u, t)
                if b is gb:
                    t_g = t
                    if scatter:
                        scatter()
                else:
                    t_u = t
            s, af, pg = XY.next(), AFB.next(), PG.next()
            t = mm(PB[s.at][:, :], F[0:16, cc("ident", e):cc("ident", e) + 1].to_broadcast([16, 128]),
                   fv(SLOT, 512, 0, 16), True, True, t_slot, s.free)
            ta = acti(fv(af.at, 256), PB[s.at][:, 256:512], ACT.Copy, t, af.free)
            t_pg = stt(fv(pg.at, 256), PB[s.at][:, 0:256], ccol("pmod"), fv(af.at, 256), ALU.is_equal, ALU.mult,
                       t, ta, pg.free)
            s.free, af.free = [t_pg], [t_pg]

            sg, hid, ht, y = SG.next(), HID.next(), HT.next(), YR.next()
            t = acti(fv(sg.at, 512), PB[gb.at][:, :], ACT.Silu, t_g, sg.free)
            gb.free = [t]
            t = tt(fv(hid.at, 512), fv(sg.at, 512), PB[ub.at][:, :], ALU.mult, t, t_u, hid.free)
            ub.free, sg.free = [t], [t]
            s = XY.next()
            for c in range(4):
                t2 = tr(PB[s.at][:, c * 128:(c + 1) * 128], fv(hid.at + c * 128, 128), t, s.free)
            hid.free = [t2]
            t_ht = cp(fv(ht.at, 512), PB[s.at][:, :], t2, ht.free)
            s.free = [t_ht]
            yb = [XY.next(), XY.next()]
            for c in range(4):
                for j0 in (0, 2):
                    u = take()
                    for n in range(2):
                        for jj in range(2):
                            j = j0 + jj
                            t = mm(PB[yb[n].at][32 * j:32 * j + 32, :], fv(ht.at + c * 128 + 32 * j, 32),
                                   fv(page(u.page) + jj * 1024 + n * 512, 512), c == 0, c == 3, u.loaded, t_ht,
                                   yb[n].free)
                    done(u, t)
            ht.free = [t]
            t_ye = [acti(fv(y.at, 512), PB[yb[0].at][:, :], ACT.Copy, t, y.free),
                    cp(fv(y.at + 512, 512), PB[yb[1].at][:, :], t, y.free)]
            yb[0].free, yb[1].free = [t_ye[0]], [t_ye[1]]

            def scatter(e=e, y=y, pg=pg, t_ye=t_ye, t_pg=t_pg):
                for ch in range(2):
                    for n in range(2):
                        t = mm(PB[acc[2 * ch + n]][:, :], fv(pg.at + ch * 128, 128), fv(y.at + n * 512, 512),
                               e == 0, e == NEXP - 1, t_ye, t_pg, acc_free)
                y.free, pg.free = [t], [t]
                return t

        t_moe = scatter()
        Y = page(15)
        gfin = GT
        t_gf = load("gfin", fv(gfin, 1024), a["rows"][2, :].partition_broadcast(128), t_x1)
        t_x2 = []
        for ch in range(2):
            for n in range(2):
                o = ch * 1024 + n * 512
                e = tt(fv(Y + o, 512), PB[acc[2 * ch + n]][:, :], fv(GT + 1024 + n * 512, 512), ALU.mult, t_moe,
                       t_mod[10], t_mod[11])
                t_x2.append(tt(fv(X1 + o, 512), fv(Y + o, 512), fv(X1 + o, 512), ALU.add, e))
        t_sq = [acti(fv(Y + ch * 1024, 1024), fv(X1 + ch * 1024, 1024), ACT.Square, t_x2, scale=1 / 32,
                     accum=fv(ms + ch, 1)) for ch in range(2)]
        t_rs = rsqrt_small(fv(ms + 2, 2), fv(ms, 2), 2, t_sq)
        t_x = [stt(fv(X1 + ch * 1024, 1024), fv(X1 + ch * 1024, 1024), fv(ms + 2 + ch, 1), fv(gfin, 1024), ALU.mult,
                   ALU.mult, t_rs, t_gf) for ch in range(2)]

        HT_H, HT_L, SCA, SCB = page(1), page(2), page(11), page(13)
        ROW = page(12)

        def norm_fm(g, t_x, free):
            t_sq = [acti(fv(SCB + ch * 1024, 1024), fv(X1 + ch * 1024, 1024), ACT.Square, t_x[ch], free, scale=1 / 32,
                         accum=fv(ms + ch, 1)) for ch in range(2)]
            t_n = []
            for ch in range(2):
                t_rs = rsqrt_small(fv(ms + 2 + ch, 1), fv(ms + ch, 1), 1, t_sq[ch])
                t_n.append(ts(fv(SCA + ch * 1024, 1024), fv(X1 + ch * 1024, 1024), fv(ms + 2 + ch, 1), ALU.mult,
                              t_rs, free))
            toks = []
            for i in range(4):
                s = (Bank.S, Bank.T)[i % 2].next()
                for k in (2 * i, 2 * i + 1):
                    for ch in range(2):
                        o = (k % 2) * 256 + ch * 128
                        t = tr(PB[s.at][:, o:o + 128], fv(SCA + ch * 1024 + k * 128, 128), t_n[ch], s.free)
                th = [acti(rv(HT_H + k * 256, 256), PB[s.at][:, (k % 2) * 256:(k % 2) * 256 + 256], ACT.Copy, t, free,
                           scale=ccol("pre", g * 8 + k)) for k in (2 * i, 2 * i + 1)]
                tl = [stt(rv(HT_L + k * 256, 256), PB[s.at][:, (k % 2) * 256:(k % 2) * 256 + 256],
                          ccol("pre", g * 8 + k), rf(HT_H + k * 256, 256), ALU.mult, ALU.subtract, th, free)
                      for k in (2 * i, 2 * i + 1)]
                s.free = tl
                toks += [[th, tl[0]], [th, tl[1]]]
            return toks

        def post_norm(banks, row, t_m, t_row, free, add=None):
            t_x = []
            src = {}
            for ch in range(2):
                for h in range(2):
                    i = 2 * ch + h
                    src[i] = PB[banks[i]][:, :]
                    if add is not None:
                        src[i] = fv(SCA + i * 512, 512)
                        t_m[i] = tt(src[i], PB[banks[i]][:, :], fv(add + h * 512, 512), ALU.add, t_m[i], t_row, free)
            for ch in range(2):
                t_sq = [acti(fv(SCB + (2 * ch + h) * 512, 512), src[2 * ch + h], ACT.Square, t_m[2 * ch + h], free,
                             scale=1 / 32, accum=fv(ms + 2 * ch + h, 1)) for h in range(2)]
                t = tt(fv(ms + 2 * ch, 1), fv(ms + 2 * ch, 1), fv(ms + 2 * ch + 1, 1), ALU.add, t_sq, q=pool)
                t_rs = rsqrt_small(fv(ms + 4 + ch, 1), fv(ms + 2 * ch, 1), 1, t)
                es = []
                for h in range(2):
                    o = ch * 1024 + h * 512
                    e = stt(fv(SCA + o, 512), src[2 * ch + h], fv(ms + 4 + ch, 1), fv(row + h * 512, 512),
                            ALU.mult, ALU.mult, t_rs, t_sq, t_row, free)
                    es.append(tt(fv(X1 + o, 512), fv(SCA + o, 512), fv(X1 + o, 512), ALU.add, e))
                t_x.append(es)
            return t_x

        def row_load(name, at, r, *after):
            return load(name, fv(at, 1024), a["rows"][r, :].partition_broadcast(128), after)

        C_Q = [0.0] + [1.0 / (2 * k + 1) for k in range(1, 8)]

        def softplus(out, v, ab, n, tmp, t_v, t_ab, q=None):
            e_, s_, q_ = (fv(tmp + i * n, n) for i in range(3))
            t = acti(e_, ab, ACT.Exp, t_ab, scale=-1.0)
            def add_mult(x, c, y, *after):
                if q is None:
                    return stt(x, x, c, y, ALU.add, ALU.mult, after)
                return tt(x, x, y, ALU.mult, ts(x, x, c, ALU.add, after, q=q), after, q=q)

            t1 = ts(s_, e_, 2.0, ALU.add, t, q=q)
            t1 = recip(s_, s_, t1)
            t1 = tt(s_, s_, e_, ALU.mult, t1, q=q)
            t2 = tt(e_, s_, s_, ALU.mult, t1, q=q)
            t3 = ts(q_, e_, C_Q[7], ALU.mult, t2, q=q)
            for k in range(6, 0, -1):
                t3 = add_mult(q_, C_Q[k], e_, t3)
            t3 = add_mult(q_, 1.0, s_, t3)
            t4 = ts(v, v, 0.0, ALU.max, t_v, q=q)
            return lambda: stt(out, q_, 2.0, v, ALU.mult, ALU.add, t3, t4)

        BC, XS, XDT, ST = page(3), span(7, 8), span(9, 10), page(11)
        DT, CS, CSR, TM, DEC, NEG = (page(4) + i for i in (0, 256, 512, 768, 928, 1056))
        E2_ = page(17) + 768
        CBT, BTM, XDD = page(6), page(6) + 1024, page(17)
        idr, idb = small(32), small(64)
        YGH, YGL = span(9, 10), span(13, 14)

        t_old = [t_x, t_moe]
        given = retired(3, 4, 6, 9, 10, 11, 13, 17)
        t_old += given
        give(15, [t_x2, t_sq])
        t_hl = retired(18, 19, 20, 21, 22, 23)
        for i in range(3):
            W.hl.append((18 + 2 * i, 19 + 2 * i, t_hl[2 * i:2 * i + 2]))
        t_idr = [acti(rv(idr, 32, p, p + 32), fv(cc("ident", p), 32, p, p + 32), ACT.Copy, t_cst) for p in (0, 32)]
        t_idb = cp(B16(idb, 128), ident, t_cst)
        t_tri = load("tri", fv(SCB, 512), a["tri"], t_old)
        t_neg = cp(B16(NEG, 512), fv(SCB, 512), t_tri)
        Bank.U.slots[0].free, Bank.U.slots[1].free = gb.free, ub.free
        if Bank.U.i % 2:
            Bank.U.slots.reverse()
            Bank.U.i = 0
        for r, bs in ((Bank.S, XY.slots), ):
            for s, o in zip(r.slots, bs):
                s.free = o.free
        for s in Bank.T.slots + Bank.O.slots:
            s.free = [t_x2]
        t_h = norm_fm(0, [t_x, t_x], [t_old, t_neg])
        pump()
        t_row = row_load("row0", ROW, 3, t_moe)

        CV = Ring([page(12) + 1024, page(12) + 1536, page(17) + 1280])
        for s in CV.slots:
            s.free = [t_old]
        t_bc, t_xs, t_ys, t_xdt = {}, {}, {}, {}
        D_RING = Ring([page(13) + 512 * i for i in range(2)])
        SC_RING = Ring([page(13) + 1024, page(13) + 1536] + [page(14) + 512 * i for i in range(4)])
        for r in (D_RING, SC_RING):
            for s in r.slots:
                s.free = [t_h, t_neg]
        XDD_RING = Ring([XDD + 128 * i for i in range(6)])
        E2_RING = Ring([E2_ + 128 * i for i in range(4)])
        ss = {}
        t_half = [ts(fv(cc(k), n), fv(cc(k), n), 0.5, ALU.mult, t_cst2) for k, n in (("conv_w", 96), ("conv_b", 24))]

        def ssd_dt(b, t):
            v, ab, tmp = ST, ST + 256, ST + 512
            t_v = acti(fv(v, 256), PB[b.at][:, 0:256], ACT.Identity, t, t_h, bias=ccol("dt_b"))
            t_ab = acti(fv(ab, 256), PB[b.at][:, 0:256], ACT.Abs, t, t_h, bias=ccol("dt_b"))
            b.free = [t_ab]
            t_a = acti(fv(ms + 6, 1), ccol("a_log"), ACT.Exp, t_cst2)
            end = softplus(fv(DT, 256), fv(v, 256), fv(ab, 256), 256, tmp, t_v, t_ab, q=pool)
            for _ in range(4):
                yield
            t = ts(fv(tmp, 256), fv(DT, 256), fv(ms + 6, 1), ALU.mult, end(), t_a, s2=-1.0, op1=ALU.mult)
            one = F[:, ones:ones + 1].to_broadcast([128, 128])
            t_cs = []
            for ch in range(2):
                o, i = fv(CS + ch * 128, 128), fv(tmp + ch * 128, 128)
                t_cs.append(dve.do(lambda e, o=o, i=i: e.tensor_tensor_scan(o, one, i, 0.0, ALU.mult, ALU.add), t))
            t_dec = acti(fv(DEC, 128, 0, 32), fv(CS, 128, 0, 32), ACT.Exp, t_cs, scale=-1.0,
                         bias=F[0:32, CS + 127:CS + 128])
            t1 = acti(rv(CSR, 256, 0, 64), fv(CS, 256, 0, 64), ACT.Copy, t_cs)
            ss["csr"] = tt(rv(CSR, 256, 32, 64), fv(CS, 256, 32, 64), rf(CSR, 256, 32, 64), ALU.subtract, t1)
            ss["dt"] = t_cs
            yield
            s = Bank.T.next()
            for i, (src, o) in enumerate(((DT, 0), (DT, 128), (CS, 0), (CS, 128), (DEC, 0))):
                t = tr(PB[s.at][:, i * 32:i * 32 + 32], fv(src + o, 128, 0, 32), t_cs, t_dec, s.free, n=32)
            e1 = cp(fv(TM, 64), PB[s.at][:, 0:64], t)
            e2 = ts(fv(TM + 64, 64), PB[s.at][:, 64:128], -1.0, ALU.mult, t)
            e3 = cp(fv(TM + 128, 32), PB[s.at][:, 128:160], t)
            s.free = [e3]
            ss["tm"] = [e1, e2, e3]

        def ssd_bc():
            yield
            s = Bank.O.next()
            for g in range(4):
                t = tr(PB[s.at][:, g * 128:(g + 1) * 128], fv(BC + g * 256, 128), t_bc[g], s.free)
            s.free = [cp(fv(BTM, 512), PB[s.at][:, :], t)]
            ss["btm"] = s.free
            ss["cbt"] = []
            for half in range(2):
                if half:
                    yield
                s = (Bank.T, Bank.O)[half].next()
                for g in (2 * half, 2 * half + 1):
                    for ch in range(2):
                        o = (g % 2) * 256 + ch * 128
                        t = mm(PB[s.at][:, o:o + 128], fv(BC + g * 256 + ch * 128, 128),
                               fv(BC + (4 + g) * 256 + ch * 128, 128), True, True, t_bc[g], t_bc[4 + g], s.free)
                s.free = [acti(fv(CBT + half * 512, 512), PB[s.at][:, :], ACT.Copy, t)]
                ss["cbt"] += [s.free, s.free]

        def ssd_tiles(tiles):
            yield
            n = len(tiles)
            i0 = tiles[0]
            s = Bank.T.next()
            for k, i in enumerate(tiles):
                for ch in range(2):
                    t = tr(PB[s.at][:, ch * n * 128 + k * 128:ch * n * 128 + k * 128 + 128],
                           fv(XS + i * 256 + ch * 128, 128), t_xs[i], s.free)
            src = PB[s.at][:, 0:n * 256].rearrange("p (c h q) -> p c h q", c=2, q=64)
            dst = fv(XDT, 4096).rearrange("p (c f) -> p c f", c=2)[:, :, i0 * 128:(i0 + n) * 128]
            dst = dst.rearrange("p c (h q) -> p c h q", q=64)
            dtm = fv(TM, 64).rearrange("p (c h) -> p c h", c=2)[:, :, 2 * i0:2 * (i0 + n)]
            t_xdt = tt(dst, src, dtm.unsqueeze(3).to_broadcast([128, 2, 2 * n, 64]), ALU.mult, t, ss["tm"])
            s.free = [t_xdt]
            sc, t_sc = {}, {}
            for i in tiles:
                s, d, c = Bank.S.next(), D_RING.next(), SC_RING.next()
                mm(PB[s.at][:, :], B16(idb, 128), B16(NEG, 512), True, False, t_idb, t_neg, s.free)
                for hh in range(2):
                    h = 2 * i + hh
                    t = mm(PB[s.at][:, hh * 256:(hh + 1) * 256], R[0:64, idr + h:idr + h + 1].to_broadcast([64, 128]),
                           rv(CSR, 256, 0, 64), False, hh == 1, ss["csr"], t_idr)
                es = []
                for hh in range(2):
                    for ch in range(2):
                        o = hh * 256 + ch * 128
                        es.append(acti(fv(d.at + o, 128), PB[s.at][:, o:o + 128], ACT.Exp, t, d.free, ss["tm"],
                                       bias=fv(TM + 64 + ch * 32 + 2 * i + hh, 1)))
                s.free = [es]
                cb = fv(CBT + (i // 4) * 256, 256).unsqueeze(1).to_broadcast([128, 2, 256])
                t_sc[i] = tt(three(fv(c.at, 512), 256), three(fv(d.at, 512), 256), cb, ALU.mult, es, ss["cbt"][i // 4],
                             c.free, q=pool)
                d.free = [t_sc[i]]
                sc[i] = c
            xd, t_xd = {}, {}
            for i in tiles:
                xd[i] = XDD_RING.next()
                dec = fv(TM + 128 + 2 * i, 2).unsqueeze(2).to_broadcast([128, 2, 64])
                t_xd[i] = tt(three(fv(xd[i].at, 128), 64), three(fv(XDT + i * 128, 128), 64), dec, ALU.mult, t_xdt,
                             xd[i].free, ss["tm"], q=pool)
            yield
            yield
            s = Bank.T.next()
            for k, i in enumerate(tiles):
                t = mm(PB[s.at][:, k * 128:(k + 1) * 128], fv(BTM + (i // 4) * 128, 128), fv(xd[i].at, 128), True, True,
                       t_xd[i], ss["btm"], s.free)
                xd[i].free = [t]
            e2 = {}
            for k, i in enumerate(tiles):
                for hh in range(2):
                    h = cc("ident", 2 * i + hh)
                    t = mm(PB[s.at][hh * 64:hh * 64 + 64, 256 + k * 128:256 + (k + 1) * 128],
                           F[0:32, h:h + 1].to_broadcast([32, 64]), fv(CS + 128, 128, 0, 32), True, True)
            t_st = acti(fv(ST + i0 * 128, n * 128), PB[s.at][:, 0:n * 128], ACT.Copy, t, ss["dt"])
            s.free = [t_st]
            for k, i in enumerate(tiles):
                e2[i] = E2_RING.next()
                e2[i].tok = acti(fv(e2[i].at, 128), PB[s.at][:, 256 + k * 128:256 + (k + 1) * 128], ACT.Exp, t,
                                 e2[i].free)
                s.free.append(e2[i].tok)
            s = Bank.O.next()
            for k, i in enumerate(tiles):
                for ch in range(2):
                    for hh in range(2):
                        o = k * 256 + ch * 128
                        t = mm(PB[s.at][hh * 64:hh * 64 + 64, o:o + 128],
                               fv(XDT + ch * 2048 + i * 128 + hh * 64, 64), fv(sc[i].at + hh * 256 + ch * 128, 128),
                               True, True, t_sc[i], t_xdt, s.free)
                sc[i].free = [t]
            ss["xdt_read"] = t
            t_y1 = {}
            for k, i in enumerate(tiles):
                x = fv(XS + i * 256, 256)
                t_y1[i] = stt(x, x, ccol("d", i), PB[s.at][:, k * 256:(k + 1) * 256], ALU.mult, ALU.add, t)
            s.free = [t_y1[i] for i in tiles]
            yield
            s = Bank.O.next()
            for k, i in enumerate(tiles):
                t = mm(PB[s.at][:, k * 128:(k + 1) * 128], fv(ST + i * 128, 128), fv(BC + (4 + i // 4) * 256 + 128, 128),
                       True, True, t_st, s.free)
            es = []
            for k, i in enumerate(tiles):
                e = tt(fv(e2[i].at, 128), PB[s.at][:, k * 128:(k + 1) * 128], fv(e2[i].at, 128), ALU.mult, t, e2[i].tok)
                es.append(e)
                x = fv(XS + i * 256 + 128, 128)
                t_ys[i] = tt(x, x, fv(e2[i].at, 128), ALU.add, e, t_y1[i])
                e2[i].free = [t_ys[i]]
            s.free = es

        def conv(src, w, bias, taps, out, t, *after):
            ta = [acti(o, s, ACT.Identity, t, after, scale=F[:, wc + taps - 1:wc + taps], bias=F[:, bc:bc + 1])
                  for o, s, wc, bc in zip(out, src, w, bias)]
            last = list(ta)
            for k in range(1, taps):
                for i, (o, s, wc) in enumerate(zip(out, src, w)):
                    last[i] = stt(o[:, k:], s[:, :256 - k], F[:, wc + taps - 1 - k:wc + taps - k], o[:, k:], ALU.mult,
                                  ALU.add, ta, last[i])
            return last

        def ssd_z(i, z, t_z):
            x = fv(XS + i * 256, 256)
            t_ys[i] = stt(x, x, 0.5, z, ALU.mult, ALU.mult, t_z, t_ys[i])
            return t_ys[i]

        t_yg = []

        def ssd_group(g):
            x4 = fv(XS + g * 1024, 1024)
            sq = BC
            t = acti(fv(sq, 1024), x4, ACT.Square, [t_ys[i] for i in range(4 * g, 4 * g + 4)], t_sqfree, ss["btm"], ss["cbt"])
            yield
            t = tt(fv(sq, 512), fv(sq, 512), fv(sq + 512, 512), ALU.add, t)
            t = tt(fv(sq, 256), fv(sq, 256), fv(sq + 256, 256), ALU.add, t)
            yield
            b = Bank.O.next()
            for ch in range(2):
                t2 = mm(PB[b.at][:, ch:ch + 1], fv(sq + ch * 128, 128), fv(inv_n + 2, 1), True, True, t, t_inv, b.free)
            t_sqfree[:] = [t2]
            r2 = fv(rcol + 2 * (g % 2), 2)
            e = ts(r2, PB[b.at][:, 0:2], EPS, ALU.add, t2)
            b.free = [e]
            e = tt(r2, r2, F[0:128, eps_half:eps_half + 1].to_broadcast([128, 2]), ALU.pow, e, t_eps, q=pool)
            yield
            b = Bank.O.next()
            for ch in range(2):
                r = rcol + 2 * (g % 2) + ch
                t = mm(PB[b.at][:, ch * 128:ch * 128 + 128], F[:, r:r + 1].to_broadcast([128, 128]), ident, True, True, e,
                       b.free)
            es = []
            for i in range(4 * g, 4 * g + 4):
                x = fv(XS + i * 256, 256)
                es.append(stt(x, x, ccol("ssd_n", i), PB[b.at][:, 0:256], ALU.mult, ALU.mult, t, t_ys[i]))
            b.free = es
            th = acti(rv(YGH + g * 1024, 1024), x4, ACT.Copy, es, ss["xdt_read"])
            tl = tt(rv(YGL + g * 1024, 1024), x4, rf(YGH + g * 1024, 1024), ALU.subtract, th, es,
                    [s.free for s in D_RING.slots + SC_RING.slots])
            t_yg.extend([[th, tl]] * 4)

        t_sqfree = []
        pend = []
        for n in range(21):
            W.pool_share = 512 if 3 <= n < 14 else 0
            u = take()
            b = Bank.U.next()
            tiles = SSD_TILES[2 * n:2 * n + 2]
            t = fm(u, 128 * len(tiles), 8, HT_H, HT_L, b.at, len(tiles), b.free, xtok=t_h if n == 0 else None)
            cv = CV.next()
            assert all(p[3] is not cv for p in pend)
            src = {k: PB[b.at][:, k * 256:(k + 1) * 256] for k in range(2)}
            b.free = []
            xt, cvf = [], []
            cvk = [k for k, tl in enumerate(tiles) if tl[0] in "bcx"]
            t_bank = t
            if tiles[0] == "dt":
                bg.append(ssd_dt(b, t))
                next(bg[-1])
                t_bank = b.free
            if cvk:
                chan = [{"x": 0, "b": 16, "c": 20}[tiles[k][0]] + tiles[k][1] for k in cvk]
                dst = [fv(XS + tiles[k][1] * 256, 256) if tiles[k][0] == "x" else
                       fv(BC + (tiles[k][1] + (4 if tiles[k][0] == "c" else 0)) * 256, 256) for k in cvk]
                last = conv([src[k] for k in cvk], [cc("conv_w", c * 4) for c in chan], [cc("conv_b", c) for c in chan],
                            4, dst, t_bank, t, t_half, t_old)
                b.free = last
                for k, o, tk in zip(cvk, dst, last):
                    kind, i = tiles[k]
                    th = fv(cv.at + k * 256, 256)
                    e = acti(th, o, ACT.Tanh, tk, cv.free)
                    e = stt(o, th, 1.0, o, ALU.add, ALU.mult, e)
                    cvf.append(e)
                    if kind == "x":
                        t_xs[i] = e
                        xt.append(i)
                    else:
                        t_bc[i + (4 if kind == "c" else 0)] = e
            zk = [k for k, tl in enumerate(tiles) if tl[0] == "z"]
            zs = []
            if zk:
                o, n_ = zk[0] * 256, len(zk) * 256
                g, ps = fv(cv.at + o, n_), PB[b.at][:, o:o + n_]
                e = acti(g, ps, ACT.Tanh, t, b.free, cv.free, scale=0.5)
                e = stt(g, g, 1.0, ps, ALU.add, ALU.mult, e)
                b.free = [b.free, e]
                zs = [(tiles[k][1], fv(cv.at + k * 256, 256), e, cv) for k in zk]
            cv.free = cvf
            tick()
            done(u, t)
            if ("c", 3) in tiles:
                bg.append(ssd_bc())
            if xt:
                bg.append(ssd_tiles(xt))
            pend += zs
            while pend and pend[0][0] in t_ys:
                i, z, e, c = pend.pop(0)
                assert i in t_ys
                c.free = [c.free, ssd_z(i, z, e)]
                if i % 4 == 3:
                    bg.append(ssd_group(i // 4))
        t_hr = t
        assert not pend
        banks = [2, 3, 4, 5]
        bank_free = [s.free for s in Bank.S.slots + Bank.T.slots]
        t_m = out_units(8, YGH, YGL, banks, t_yg, bank_free, tick)
        t_x = post_norm(banks, ROW, [t_m] * 4, t_row, [t_yg, t_m])
        for r, i in ((Bank.S, 0), (Bank.T, 2)):
            for k in range(2):
                r.slots[k].free = t_x[(i + k) // 2]

        def ffn(l, t_x, t_row, row, free):
            t_h = norm_fm(2 * l + 1, t_x, free)
            banks = [2, 3, 4, 5]
            UB = Ring([0, 1, 6, 7])
            for s, o in zip(UB.slots, Bank.U.slots + Bank.O.slots):
                s.free = o.free
            CG = Ring([page(3) + 512 * i for i in range(2)])
            CVV = Ring([page(3) + 1024 + 512 * i for i in range(2)])
            GVH = Ring([page(4) + 512 * i for i in range(2)])
            GVL = Ring([page(4) + 1024 + 512 * i for i in range(2)])
            for r in (CG, CVV, GVH, GVL):
                for s in r.slots:
                    s.free = [free]
            bank_free = [s.free for s in Bank.S.slots + Bank.T.slots]
            pend = None

            def down(j, gh, gl, tok):
                u = take()
                for ch in range(2):
                    for half in range(2):
                        for k in range(2):
                            w = k * 1024 + half * 512
                            wh, wl = rv(u.hi + w, 512), rv(u.lo + w, 512)
                            h = rv(gh.at + k * 256 + ch * 128, 128)
                            lo = rv(gl.at + k * 256 + ch * 128, 128)
                            o = PB[banks[2 * ch + half]][:, :]
                            mm(o, h, wh, j == k == 0, False, u.tok, tok, bank_free, t_h)
                            mm(o, h, wl, False, False)
                            t = mm(o, lo, wh, False, j == 15 and k == 1)
                gh.free, gl.free = [t], [t]
                done(u, t)
                return t

            for j in range(16):
                cvs = []
                for part_, ring in ((0, CG), (1, CVV)):
                    u = take()
                    b, c = UB.next(), ring.next()
                    t = fm(u, 256, 8, HT_H, HT_L, b.at, 2, b.free, xtok=t_h if j == 0 else None)
                    tiles = [32 * part_ + 2 * j + k for k in range(2)]
                    out = [fv(c.at + k * 256, 256) for k in range(2)]
                    last = conv([PB[b.at][:, k * 256:(k + 1) * 256] for k in range(2)],
                                [cc("f_cw", l * 192 + x * 3) for x in tiles], [cc("f_cb", l * 64 + x) for x in tiles],
                                3, out, t, c.free)
                    b.free = last
                    cvs.append((c, last))
                    done(u, t)
                (cg, tg), (cv, tv) = cvs
                gh, gl = GVH.next(), GVL.next()
                e = acti(fv(cg.at, 512), fv(cg.at, 512), ACT.Gelu_apprx_tanh, tg)
                e = tt(fv(cg.at, 512), fv(cg.at, 512), fv(cv.at, 512), ALU.mult, e, tv)
                th = acti(rv(gh.at, 512), fv(cg.at, 512), ACT.Copy, e, gh.free)
                tl = tt(rv(gl.at, 512), fv(cg.at, 512), rf(gh.at, 512), ALU.subtract, th, e, gl.free)
                cg.free, cv.free = [th, tl], [e]
                if pend:
                    down(*pend)
                pend = (j, gh, gl, [th, tl])
            t_hr = t
            t_m = down(*pend)
            t_x = post_norm(banks, row, [t_m] * 4, t_row, [t_m, t_h])
            for s, o in zip(UB.slots, Bank.U.slots + Bank.O.slots):
                o.free = s.free
            for r, i in ((Bank.S, 0), (Bank.T, 2)):
                for k in range(2):
                    r.slots[k].free = t_x[(i + k) // 2]
            return t_x, [t_m, t_hr, t_x]

        t_row = row_load("row1", page(12) + 1024, 4, t_m)
        t_x, t_free = ffn(0, t_x, t_row, page(12) + 1024, [t_x, t_yg, t_hr, t_m])

        t_row = [row_load("row2", page(12), 5, t_free), row_load("row3", page(12) + 1024, 7, t_free)]
        t_h = norm_fm(2, t_x, t_free)
        XBP = 259
        XB, XC, GX, GA, YB = span(3, 4), span(6, 11), span(6, 11) + 2560, span(6, 11) + 5120, span(6, 11) + 7680
        AT_, MU = span(13, 14), span(3, 4)
        t_pad = zero(F[:, XB:XB + 10 * XBP].rearrange("p (t c) -> p t c", c=XBP)[:, :, 0:3], 0.0, t_free)
        xb = lambda i: XB + i * XBP
        lam, lab, ltm = small(10), small(10), small(30)
        t_v = ts(fv(lam, 10), fv(cc("lam"), 10), -1.0, ALU.mult, t_cst2)
        t_ab = acti(fv(lab, 10), fv(lam, 10), ACT.Abs, t_v)
        t = softplus(fv(lab, 10), fv(lam, 10), fv(lab, 10), 10, ltm, [t_v, t_ab], t_ab)()
        t_lam = ts(fv(lab, 10), fv(lab, 10), -8.0, ALU.mult, t)
        t_lamn = ts(fv(lam, 10), fv(lab, 10), -1.0, ALU.mult, t_lam)

        t_xc = []
        for n in range(5):
            u = take()
            b = Bank.U.next()
            t = fm(u, 256, 8, HT_H, HT_L, b.at, 2, b.free, xtok=t_h if n == 0 else None)
            ts_ = []
            for k in range(2):
                i = 2 * n + k
                ts_.append(acti(fv(xb(i) + 3, 256), PB[b.at][:, k * 256:(k + 1) * 256], ACT.Identity, t, t_free,
                                bias=ccol("l_bin", 10 + i)))
            b.free = ts_
            last = []
            for k in range(2):
                i = 2 * n + k
                last.append(ts(fv(XC + i * 256, 256), fv(xb(i) + 3, 256), ccol("l_cw", i * 4 + 3), ALU.mult, ts_[k],
                               t_free, s2=ccol("l_cb", i), op1=ALU.add))
            for j in range(1, 4):
                for k in range(2):
                    i = 2 * n + k
                    o = fv(XC + i * 256, 256)
                    last[k] = stt(o, fv(xb(i) + 3 - j, 256), ccol("l_cw", i * 4 + 3 - j), o, ALU.mult, ALU.add, last[k],
                                  t_pad)
            t_xc += last
            done(u, t)
        t_g = {}
        t_yb = []
        for gi, (dst, bn) in enumerate(((GX, "l_bgx"), (GA, "l_bga"))):
            u = take()
            for n in range(5):
                b = Bank.O.next()
                for k in range(2):
                    i = 2 * n + k
                    t = mm(PB[b.at][:, k * 256:(k + 1) * 256], fv(page(u.page) + i * 128, 128), fv(XC + i * 256, 256),
                           True, True, u.loaded, t_xc[i], b.free)
                b.free = []
                for k in range(2):
                    i = 2 * n + k
                    e = acti(fv(dst + i * 256, 256), PB[b.at][:, k * 256:(k + 1) * 256], ACT.Sigmoid, t, t_free,
                             bias=ccol(bn, i))
                    b.free.append(e)
                    t_g[gi, i] = e
            done(u, t)
        t_at = []
        for i in range(10):
            g = fv(GA + i * 256, 256)
            e = acti(fv(AT_ + i * 256, 256), g, ACT.Exp, t_g[1, i], t_lam, t_h, scale=fv(lab + i, 1))
            e2 = acti(g, g, ACT.Tanh, e, t_lamn, scale=fv(lam + i, 1))
            t_at.append([e, e2])
        e = tt(fv(MU, 2560), fv(AT_, 2560), fv(AT_, 2560), ALU.mult, t_at, t_xc)
        e = stt(fv(MU, 2560), fv(MU, 2560), 1.0, fv(GA, 2560), ALU.add, ALU.mult, e)
        e = acti(fv(MU, 2560), fv(MU, 2560), ACT.Sqrt, e)
        e1 = tt(fv(GX, 2560), fv(GX, 2560), fv(XC, 2560), ALU.mult, [t_g[0, i] for i in range(10)], q=pool)
        t_b = tt(fv(MU, 2560), fv(MU, 2560), fv(GX, 2560), ALU.mult, e, e1)
        t_hl = []
        for i in range(10):
            o, at_, bt = fv(GA + i * 256, 256), fv(AT_ + i * 256, 256), fv(MU + i * 256, 256)
            t_hl.append(dve.do(lambda e, o=o, at_=at_, bt=bt: e.tensor_tensor_scan(o, at_, bt, 0.0, ALU.mult, ALU.add),
                               t_b))
        for n in range(5):
            u = take()
            b = Bank.U.next()
            t = fm(u, 256, 8, HT_H, HT_L, b.at, 2, b.free)
            b.free = []
            for k in range(2):
                i = 2 * n + k
                e = acti(fv(YB + i * 256, 256), PB[b.at][:, k * 256:(k + 1) * 256], ACT.Gelu_apprx_tanh, t, t_free,
                         bias=ccol("l_bin", i))
                b.free.append(e)
                t_yb.append(e)
            done(u, t)
        t_hr = t
        YLH, YLL = XC, AT_
        t_yl = []
        for i in range(10):
            f = fv(GA + i * 256, 256)
            e = tt(f, f, fv(YB + i * 256, 256), ALU.mult, t_yb[i], t_hl[i])
            th = acti(rv(YLH + i * 256, 256), f, ACT.Copy, e, e1, t_xc)
            tl = tt(rv(YLL + i * 256, 256), f, rf(YLH + i * 256, 256), ALU.subtract, th, t_hl)
            t_yl.append([th, tl])
        bank_free = [s.free for s in Bank.S.slots + Bank.T.slots]
        t_m = out_units(5, YLH, YLL, banks, t_yl, bank_free)
        t_x = post_norm(banks, page(12), [t_m] * 4, t_row, [t_m, t_yl], add=page(12) + 1024)
        for r, i in ((Bank.S, 0), (Bank.T, 2)):
            for k in range(2):
                r.slots[k].free = t_x[(i + k) // 2]
        t_row = row_load("row4", page(12), 6, t_x)
        t_x, t_free = ffn(1, t_x, t_row, page(12), [t_x, t_m, t_hr])
        ov = a["out"].rearrange("(c p) d -> p c d", p=128)
        for ch in range(2):
            load(f"out{ch}", ov[:, ch, :], fv(X1 + ch * 1024, 1024), t_x[ch])
        assert W.taken == len(units)

        queues = (pe, act, dve, pool, sp)
        all_sems = page_sem + list(misc.values())
        ends = [(s.handle, s.count) for s in all_sems if s.count]
        for q in queues:
            q.number()
        with nc.Block() as block:
            @block.tensor
            def _(e):
                pe.emit(e)

            @block.scalar
            def _(e):
                act.emit(e)

            @block.vector
            def _(e):
                dve.emit(e)

            @block.gpsimd
            def _(e):
                pool.emit(e)

            @block.sync
            def _(e):
                sp.emit(e)
                for handle, count in ends:
                    e.wait_ge(handle, count)



def kernel(**inputs):
    import numpy as _np
    import concourse.bacc as _bacc
    from concourse import mybir as _mybir
    from concourse.bass_utils import run_bass_kernel_spmd as _run

    arrays = lay_out({k: _np.asarray(v) for k, v in inputs.items()})
    nc = _bacc.Bacc("TRN2", target_bir_lowering=False, num_devices=1)
    a = {k: nc.dram_tensor(k, v.shape, _mybir.dt.from_np(v.dtype), kind="ExternalInput").ap()
         for k, v in arrays.items()}
    a["out"] = nc.dram_tensor("out", (SEQ, DM), F32, kind="ExternalOutput").ap()
    program(nc, a)
    r = _run(nc, [arrays], core_ids=[0])
    return r.results[0]["out"].reshape(1, SEQ, DM)
```

```python
import concourse.bass as bass
from concourse import mybir
from contextlib import ExitStack
from collections import deque
import numpy as np

F32 = mybir.dt.float32
F32R = mybir.dt.float32r
BF16 = mybir.dt.bfloat16
I32 = mybir.dt.int32
ALU = mybir.AluOpType
ACT = mybir.ActivationFunctionType
AX = mybir.AxisListType

SEQ = 256
DM = 1024
EPS = 1e-6
BIG = 1e30
NEXP = 16

PAGE = 2048
NPAGE = 25
CONST = 1952

TAG = 1 << 20
SPANS = [(1, 2), (3, 4), (3, 6), (6, 11), (7, 8), (9, 10), (9, 11), (13, 14), (15, 17)]

THRESH = ([-BIG, -558, -304, -165, -90, -49, -26, -14] + list(range(-7, 1))
          + list(range(1, 8)) + [8, 15, 27, 50, 91, 166, 305, 559] + [BIG])
BUCKET = [15, 14, 13, 12, 11, 10, 9, 8, 7, 6, 5, 4, 3, 2, 1, 0] + list(range(17, 32)) + [None]

ADA_FIRST = [2, 0, 3, 1]
ADA_LATER = [4, 5, 6, 7, 8, 9, 10, 11]
DIL0 = 704
DIL_AHEAD = 3
GATE0 = 704 + 9216
SSD_TILES = ["dt", ("b", 0), ("b", 1), ("b", 2), ("z", 0), ("z", 1), ("b", 3), ("c", 0), ("z", 2), ("z", 3), ("c", 1),
             ("c", 2), ("z", 4), ("z", 5), ("c", 3)] + [("x", i) for i in range(16)] + [("z", i) for i in range(6, 16)]


def token_order():
    return [16 * l + 4 * j + c for c in range(4) for j in range(4) for l in range(16)]


def ada_after(i):
    return ADA_LATER[i // 4] if i % 4 == 3 and i // 4 < 8 else None



CONST_COLS = {}


def const_layout():
    at = 0
    for name, n in [("ident", 128), ("iota", 32), ("thr", 1), ("invf", 1), ("sgn", 1), ("pmod", 1), ("sel4", 1),
                    ("c", 8), ("g_mix", 8), ("g_ffn", 8), ("b_ada", 48), ("g_q", 3), ("g_kv", 2), ("w_router", 128),
                    ("pre", 32), ("conv_w", 96), ("conv_b", 24), ("dt_b", 1), ("a_log", 1), ("d", 16), ("ssd_n", 16),
                    ("l_bin", 20), ("l_cw", 40), ("l_cb", 10), ("l_bgx", 10), ("l_bga", 10), ("lam", 10),
                    ("f_cw", 384), ("f_cb", 128)]:
        CONST_COLS[name] = (at, n)
        at += n
    return at


NCST = const_layout()
NCST1 = CONST_COLS["pre"][0]


def cols(v):
    return np.ascontiguousarray(np.reshape(v, (-1, 128)).T)


def lay_out(i):
    f32 = np.float32
    order = token_order()
    out = {}
    p = np.arange(128)
    cst = np.zeros((128, NCST), f32)

    def put(name, v):
        at, n = CONST_COLS[name]
        cst[:, at:at + n] = np.reshape(v, (128, n))

    put("ident", np.eye(128, dtype=f32))
    put("iota", np.tile(np.arange(32, dtype=f32), (128, 1)))
    put("thr", np.array(THRESH, f32)[p % 32])
    inv = (10000.0 ** (-np.arange(0, 64, 2, dtype=np.float64) / 64)).astype(f32)
    put("invf", inv[p % 32])
    put("sgn", np.where(p % 64 < 32, -1, 1).astype(f32))
    put("pmod", (p % 32).astype(f32))
    put("sel4", (p % 32 == 0).astype(f32))
    put("c", cols(i["c"][0]))
    put("g_mix", cols(i["g_norm_mix"][0]))
    put("g_ffn", cols(i["g_norm_ffn"][0]))
    put("b_ada", cols(i["b_ada"][0]))
    put("g_q", cols(i["g_q_lat"][0]))
    put("g_kv", cols(i["g_kv_lat"][0]))
    put("w_router", i["w_router"][0].reshape(8, 128, 16).transpose(1, 0, 2))
    put("pre", np.concatenate([cols(i["norm_mix_pre_2"][0]), cols(i["norm_ffn_pre_2"][0]),
                               cols(i["norm_mix_pre_2"][1]), cols(i["norm_ffn_pre_2"][1])], 1))
    put("conv_w", i["ssd_conv_w_2"][0].reshape(4, 24, 128).transpose(2, 1, 0))
    put("conv_b", cols(i["ssd_conv_b_2"][0]))
    put("dt_b", np.tile(i["ssd_dt_bias_2"][0], 4))
    put("a_log", np.tile(i["ssd_a_log_2"][0], 4))
    put("d", cols(np.repeat(i["ssd_d_2"][0], 64)))
    put("ssd_n", cols(i["ssd_norm_2"][0]))
    put("l_bin", cols(i["lru_b_in_2"][0]))
    put("l_cw", i["lru_conv_w_2"][0].reshape(4, 10, 128).transpose(2, 1, 0))
    put("l_cb", cols(i["lru_conv_b_2"][0]))
    put("l_bgx", cols(i["lru_b_gx_2"][0]))
    put("l_bga", cols(i["lru_b_ga_2"][0]))
    put("lam", cols(i["lru_lambda_2"][0]))
    put("f_cw", i["ffn_conv_w_2"].reshape(2, 3, 64, 128).transpose(3, 0, 2, 1))
    put("f_cb", i["ffn_conv_b_2"].reshape(2, 64, 128).transpose(2, 0, 1))
    out["cst"] = cst

    q = np.array(order)
    mask = np.zeros((128, 768), f32)
    for ch in range(2):
        tq = q[ch * 128:(ch + 1) * 128, None]
        mask[:, ch * 256:ch * 256 + 256] = np.where(np.abs(tq - q[None, :]) <= 64, 0, BIG)
    for r, at in ((4, 512), (16, 640)):
        mask[:, at:at + 128] = np.where(q[:128, None] % r == q[None, :128] % r, 0, BIG)
    out["mask"] = mask
    tri = np.where(np.arange(128)[:, None] <= np.arange(128)[None, :], 0, -BIG).astype(f32)
    out["tri"] = tri

    pos = i["positions"][0]
    posi = np.zeros((128, 321), np.int32)
    posi[:, 0:64] = pos[q].reshape(64, 4)[:, p // 32].T
    posi[:, 64:320] = pos[q][None, :]
    posi[:, 320] = pos[0]
    out["posi"] = posi
    rb = i["rel_bias"]
    tab = np.zeros((128, 2, 96), f32)
    for kk in range(4):
        for j in range(31):
            tab[kk * 32 + j, 0, kk * 24:kk * 24 + 24] = rb[BUCKET[j]]
            if j:
                tab[kk * 32 + j, 1, kk * 24:kk * 24 + 24] = rb[BUCKET[j - 1]]
    out["tab"] = tab.reshape(128, 192)

    x = i["x"][0]
    out["xp"] = np.ascontiguousarray(x[q].reshape(2, 128, 1024).transpose(1, 0, 2)).reshape(128, 2048)
    out["xn"] = np.ascontiguousarray(x.reshape(2, 128, 1024).transpose(1, 0, 2)).reshape(128, 2048)
    ba = i["b_ada"][0].reshape(6, 1024)
    out["rows"] = np.stack([ba[2], ba[5], i["g_final"], i["norm_mix_post_2"][0], i["norm_ffn_post_2"][0],
                            i["norm_mix_post_2"][1], i["norm_ffn_post_2"][1], i["lru_b_out_2"][0]])

    units = []

    def by_cols(w, n):
        k = w.shape[0] // 128
        a = w.reshape(k, 128, w.shape[1] // n, n).transpose(2, 1, 0, 3)
        return [u.reshape(128, k * n) for u in a]

    def by_rows(w, k):
        a = w.reshape(w.shape[0] // (128 * k), k, 128, w.shape[1]).transpose(0, 2, 1, 3)
        return [u.reshape(128, -1) for u in a]

    ada = i["w_ada"][0]

    def ada_units(cb):
        return by_rows(ada[:, cb * 512:(cb + 1) * 512], 4)

    win = i["w_in"][0]
    kpe = np.arange(640, 704)
    sw = np.concatenate([kpe[32:], kpe[:32]])
    lat = by_cols(win[:, np.concatenate([np.arange(640), kpe, kpe])], 256)
    lat += by_cols(win[:, np.concatenate([sw, sw])], 128)
    for cb in ADA_FIRST[:3]:
        units += ada_units(cb)
    units += lat[:1] + ada_units(ADA_FIRST[3]) + lat[1:]
    uq = i["w_uq"][0].reshape(384, 8, 192)
    up = by_cols(uq[:, :, :128].reshape(384, 1024), 512)
    pe = uq[:, :, 128:]
    up += by_cols(pe.reshape(384, 512), 512)
    up += by_cols(np.concatenate([pe[:, :, 32:], pe[:, :, :32]], 2).reshape(384, 512), 512)
    ukv = i["w_ukv"][0].reshape(256, 8, 256)
    up += by_cols(ukv[:, :, :128].reshape(256, 1024), 1024)
    up += by_cols(ukv[:, :, 128:].reshape(256, 1024), 1024)
    for n in range(36):
        hp, (t, g) = n // 9, DIL_UNITS[n % 9]
        at = DIL0 + ((g * 3 + t) * 8 + 2 * hp) * 128
        units += (up if n == DIL_AHEAD else []) + by_cols(win[:, at:at + 256], 256)
        if ada_after(n) is not None:
            units += ada_units(ada_after(n))
    for j in range(8):
        a = win[:, GATE0 + j * 128:GATE0 + (j + 1) * 128]
        b = win[:, GATE0 + 1024 + j * 128:GATE0 + 1024 + (j + 1) * 128]
        units += by_cols(np.concatenate([a, b], 1), 256)
    units += by_rows(i["w_out"][0], 2)

    sw_in = i["ssd_w_in_2"][0]
    z, xs, b, c, dt = (sw_in[:, s] for s in (slice(0, 2048), slice(2048, 4096), slice(4096, 4608),
                                             slice(4608, 5120), slice(5120, 5152)))
    part = {"b": b, "c": c, "x": xs, "z": z}
    allc = np.concatenate([np.concatenate([dt] * 4, 1) if t == "dt" else part[t[0]][:, t[1] * 128:t[1] * 128 + 128]
                           for t in SSD_TILES], 1)
    units += by_cols(allc[:, :5120], 256) + by_cols(allc[:, 5120:], 128)
    units += by_rows(i["ssd_w_out_2"][0], 2)

    def ffn(l):
        up, down = i["ffn_w_up_2"][l], by_rows(i["ffn_w_down_2"][l], 2)
        g, v = by_cols(up[:, :4096], 256), by_cols(up[:, 4096:], 256)
        out = []
        for j in range(16):
            out += [g[j], v[j]] + ([down[j - 2]] if 1 < j < 15 else [])
        return out + down[13:]

    units += ffn(0)
    lw = i["lru_w_in_2"][0]
    units += by_cols(lw[:, 1280:], 256)
    units += by_cols(lw[:, :1280], 256)
    units += by_rows(i["lru_w_out_2"][0], 2)
    units += ffn(1)
    out["gates"] = np.stack([i[k][0].transpose(1, 0, 2).reshape(128, 1280) for k in ("lru_w_gx_2", "lru_w_ga_2")])
    out["dense"] = np.concatenate([np.ascontiguousarray(u, dtype=f32).reshape(-1) for u in units])
    for k in ("w_gate", "w_up", "w_down"):
        out[k] = i[k][0]
    return out


DIL_UNITS = [(0, 0), (1, 0), (0, 1), (1, 1), (0, 2), (1, 2), (2, 0), (2, 1), (2, 2)]


def unit_plan():
    ada = [(2048, False)] * 2
    block1 = ada * 3 + [(2048, True)] + ada + [(2048, True)] * 2 + [(1024, True)]
    for n in range(36):
        block1 += [(1536, True)] * 4 + [(2048, True)] * 2 if n == DIL_AHEAD else []
        block1 += [(2048, True)] + (ada if ada_after(n) is not None else [])
    block1 += [(2048, True)] * 12
    ffn = [(2048, True)] * 48
    block2 = [(2048, True)] * 20 + [(1024, True)] + [(2048, True)] * 8 + ffn
    block2 += [(2048, True)] * 15 + ffn
    return block1, block2



class Tok:

    def __init__(self, sem, val=0):
        self.sem, self.val, self.used = sem, val, False


def flat(xs):
    for x in xs:
        if isinstance(x, Tok):
            yield x
        elif x is not None:
            yield from flat(x)


class Queue:

    def __init__(self, sem):
        self.sem, self.ops = sem, []

    def do(self, fn, *after):
        tok = Tok(self.sem)
        self.ops.append((fn, list(flat(after)), tok, 1))
        for t in self.ops[-1][1]:
            t.used = True
        return tok

    def dma(self, out, in_, sem, *after):
        sem.count += 16
        tok = Tok(sem.handle, sem.count)
        tok.used = True
        self.ops.append((lambda e: e.dma_start(out, in_), list(flat(after)), tok, 16))
        for t in self.ops[-1][1]:
            t.used = True
        return tok

    def number(self):
        n = 0
        for _, _, tok, inc in self.ops:
            if inc == 1 and tok.used:
                n += 1
                tok.val = n

    def emit(self, e):
        seen = {}
        for fn, after, tok, inc in self.ops:
            need = {}
            for t in after:
                need[t.sem] = max(need.get(t.sem, 0), t.val)
            for sem, val in need.items():
                if seen.get(sem, 0) < val:
                    e.wait_ge(sem, val)
                    seen[sem] = val
            ins = fn(e)
            if tok.used:
                ins.then_inc(tok.sem, inc)


class Arena:

    def __init__(self, nc, name, dt, per=1):
        self.per, self.tensors = per, []
        with ExitStack() as ctx:
            for lo, n in [(0, CONST)] + [(CONST + i * PAGE, PAGE) for i in range(NPAGE)]:
                self.tensors.append((lo, ctx.enter_context(nc.sbuf_tensor(f"{name}_{lo}", [128, n * per], dt))))
        for a, b in SPANS:
            lo, n = CONST + a * PAGE, (b - a + 1) * PAGE
            with nc.sbuf_tensor(f"{name}_below_{a}_{b}", [128, lo * per], dt):
                with nc.sbuf_tensor(f"{name}_span_{a}_{b}", [128, n * per], dt) as t:
                    self.tensors.append((lo, t))

    def __getitem__(self, at):
        p, c = at
        tag, lo = divmod(c.start, TAG)
        i = (NPAGE + tag if tag else 0 if lo < CONST else 1 + (lo - CONST) // PAGE)
        base, t = self.tensors[i]
        lo -= base
        return t[p, lo * self.per:(lo + c.stop - c.start) * self.per]


def page(i):
    return CONST + i * PAGE


def span(a, b):
    return (SPANS.index((a, b)) + 1) * TAG + page(a)


class Slot:

    def __init__(self, at):
        self.at, self.free = at, []


class Ring:
    def __init__(self, ats):
        self.slots, self.i = [a if isinstance(a, Slot) else Slot(a) for a in ats], 0

    def next(self):
        s = self.slots[self.i % len(self.slots)]
        self.i += 1
        return s


class DmaSem:
    def __init__(self, handle):
        self.handle, self.count = handle, 0


class Unit:
    def __init__(self, src, n, split):
        self.src, self.n, self.split = src, n, split
        self.page = self.loaded = self.tok = self.hl = self.bank = None
        self.read = self.owed = self.over = None




def program(nc, a):
    ctx = ExitStack()
    with ctx:
        F, R, I = (Arena(nc, name, dt) for name, dt in (("F", F32), ("R", F32R), ("I", I32)))
        B = Arena(nc, "B", BF16, 2)
        PB = [ctx.enter_context(nc.psum_tensor(f"ps{i}", [128, 512], F32)) for i in range(8)]

        def sem(name):
            return ctx.enter_context(nc.semaphore(name))

        pe, act, dve, pool, sp = (Queue(sem(f"s_{n}")) for n in ("pe", "act", "dve", "pool", "sp"))
        page_sem = [DmaSem(sem(f"s_page{i}")) for i in range(NPAGE)]

        def fv(at, n, p0=0, p1=128):
            return F[p0:p1, at:at + n]

        def rv(at, n, p0=0, p1=128):
            return R[p0:p1, at:at + n]

        def rf(at, n, p0=0, p1=128):
            return R[p0:p1, at:at + n].bitcast(F32)

        def B16(at, n):
            return B[:, at:at + n // 2]

        def three(ap, n):
            return ap.rearrange("p (a b) -> p a b", b=n)

        def cc(name, i=0, n=1):
            at, _ = CONST_COLS[name]
            return at + i

        def ccol(name, i=0, p0=0, p1=128):
            at = cc(name, i)
            return F[p0:p1, at:at + 1]

        free_at = [NCST]

        def small(n):
            at = free_at[0]
            free_at[0] += n
            assert free_at[0] <= CONST
            return at

        ident = fv(cc("ident"), 128)

        plan1, plan2 = unit_plan()
        units = []
        at = 0
        for n, split in plan1:
            units.append(Unit(a["dense"][at:at + 128 * n].rearrange("(p n) -> p n", p=128), n, split))
            at += 128 * n
        for e in range(NEXP + 1):
            for w in ("w_gate", "w_up") if e < NEXP else ():
                for k in range(8):
                    units.append(Unit(a[w][e, k * 128:(k + 1) * 128, :], 2048, False))
            for c in range(4) if e else ():
                down = a["w_down"][e - 1].rearrange("(j c p) n -> p j c n", j=4, c=4)
                for j in (0, 2):
                    units.append(Unit(down[:, j:j + 2, c, :], 2048, False))
        moe_end = len(units)
        for n, split in plan2:
            units.append(Unit(a["dense"][at:at + 128 * n].rearrange("(p n) -> p n", p=128), n, split))
            at += 128 * n

        class W:
            issued = split = taken = 0
            pages, retiring, given = deque(), set(), {}
            hl = deque()
            dropping, dropped = set(), {}
            pool_share = dve_hi = turn = 0
            late = after_moe = None

        def pump():
            while W.issued < len(units) and W.pages:
                u = units[W.issued]
                u.page, after = W.pages.popleft()
                W.issued += 1
                dst = fv(page(u.page), u.n)
                if len(u.src.shape) == 3:
                    dst = three(dst, 1024)
                u.loaded = sp.dma(dst, u.src, page_sem[u.page], after)
                if W.issued == moe_end:
                    W.after_moe()
            while W.split < W.issued:
                u = units[W.split]
                if u.split:
                    if not W.hl:
                        return
                    split_unit(u)
                W.split += 1
                if W.pages and W.split == W.issued:
                    pump()

        def split_unit(u):
            hi, lo, free = W.hl.popleft()
            u.hl = (hi, lo)
            u.hi, u.lo = page(hi), page(lo)
            src, n = page(u.page), u.n
            W.turn += W.dve_hi
            if W.turn >= 1:
                W.turn -= 1
                th = cp(rv(u.hi, n), fv(src, n), u.loaded, free)
            else:
                th = acti(rv(u.hi, n), fv(src, n), ACT.Copy, u.loaded, free)

            def low():
                u.tok = []
                for q, c0, c1 in ((pool, 0, W.pool_share), (dve, W.pool_share, n)):
                    if c0 < c1:
                        out, a_, b_ = rv(u.lo + c0, c1 - c0), fv(src + c0, c1 - c0), rf(u.hi + c0, c1 - c0)
                        u.tok.append(tt(out, a_, b_, ALU.subtract, th, u.loaded, free, q=q))
                give(u.page, [th, u.tok])

            if W.late is None:
                low()
            else:
                W.late.append(low)

        def split_late(hi, lo, free):
            W.hl.append((hi, lo, free))
            W.late = []
            pump()
            late, W.late = W.late, None
            assert len(late) == 1

            def end():
                late[0]()
                pump()

            return end

        def give(p, toks):
            if p in W.retiring:
                W.retiring.remove(p)
                W.given[p] = toks
            else:
                W.pages.append((p, toks))

        def retire(*ps):
            for p in ps:
                for item in list(W.pages):
                    if item[0] == p:
                        W.pages.remove(item)
                        W.given[p] = item[1]
                        break
                else:
                    W.retiring.add(p)

        def retired(*ps):
            return [W.given.pop(p) for p in ps]

        def take():
            u = units[W.taken]
            assert u.loaded is not None, "not issued"
            assert u.split == (u.tok is not None)
            W.taken += 1
            return u

        def done(u, tok):
            if u.split and u.hl in W.dropping:
                W.dropped[u.hl] = [tok]
            elif u.split:
                W.hl.append((*u.hl, [tok]))
            else:
                give(u.page, [tok])
            pump()

        def through(u, tok):
            if u.owed:
                done(*u.owed)
            if not u.over:
                done(u, u.read or tok)

        def mm(out, lhsT, rhs, start, stop, *after):
            return pe.do(lambda e: e.matmul(out, lhsT, rhs, start=start, stop=stop), *after)

        def tr(out, in_, *after, n=128):
            return pe.do(lambda e: e.transpose(out, in_, ident if n == 128 else F[0:n, cc("ident"):cc("ident") + n]),
                         *after)

        def acti(out, in_, func, *after, bias=0.0, scale=1.0, accum=None):
            if accum is None:
                return act.do(lambda e: e.activation(out, in_, func, bias=bias, scale=scale), *after)
            return act.do(lambda e: e.activation(out, in_, func, bias=bias, scale=scale, accum_out=accum), *after)

        def tt(out, in0, in1, op, *after, q=None):
            return (q or dve).do(lambda e: e.tensor_tensor(out, in0, in1, op), *after)

        def ts(out, in0, s1, op0, *after, s2=None, op1=None, q=None):
            if op1 is None:
                return (q or dve).do(lambda e: e.tensor_scalar(out, in0, s1, None, op0), *after)
            return (q or dve).do(lambda e: e.tensor_scalar(out, in0, s1, s2, op0, op1), *after)

        def stt(out, in0, s, in1, op0, op1, *after, q=None):
            return (q or dve).do(lambda e: e.scalar_tensor_tensor(out=out, in0=in0, scalar=s, in1=in1, op0=op0, op1=op1),
                          *after)

        def cp(out, in_, *after, q=None):
            return (q or dve).do(lambda e: e.tensor_copy(out, in_), *after)

        def red(out, in_, op, *after):
            return dve.do(lambda e: e.tensor_reduce(out, in_, AX.X, op), *after)

        def recip(out, in_, *after):
            return dve.do(lambda e: e.reciprocal(out, in_), *after)

        def zero(out, v, *after, q=None):
            return (q or pool).do(lambda e: e.memset(out, v), *after)

        misc = {}

        def load(name, out, in_, *after):
            if name not in misc:
                misc[name] = DmaSem(sem("s_" + name))
            return sp.dma(out, in_, misc[name], after)

        def fm(u, ncol, nk, xh, xl, bank, tiles, *after, xtok=None, t0=0, k0=0, k1=None):
            first = [u.tok, after]
            for t in range(tiles):
                o = PB[bank][:, t * 256:(t + 1) * 256]
                for k in range(k0, k1 or nk):
                    w = k * ncol + (t0 + t) * 128
                    wh, wl = rv(u.hi + w, 128), rv(u.lo + w, 128)
                    h, l = rv(xh + k * 256, 256), rv(xl + k * 256, 256)
                    mm(o, wh, h, k == 0, False, first, xtok[k] if xtok and t == 0 else None)
                    mm(o, wh, l, False, False)
                    tok = mm(o, wl, h, False, k == nk - 1)
                    first = None
            return tok

        def tm(u, ncol, c0, n, nk, xh, xl, out, ch, start, stop, *after):
            first = [u.tok, after]
            for k in range(nk):
                w = k * ncol + c0
                wh, wl = rv(u.hi + w, n), rv(u.lo + w, n)
                h, l = rv(xh + k * 256 + ch * 128, 128), rv(xl + k * 256 + ch * 128, 128)
                mm(out, h, wh, start and k == 0, False, first)
                mm(out, h, wl, False, False)
                tok = mm(out, l, wh, False, stop and k == nk - 1)
                first = None
            return tok

        bg = []

        def tick():
            for g in list(bg):
                try:
                    next(g)
                except StopIteration:
                    bg.remove(g)

        class Bank:
            U, S, T, O = Ring([0, 1]), Ring([2, 3]), Ring([4, 5]), Ring([6, 7])

        ms = small(8)
        eps_half = small(4)
        t_eps = [zero(fv(eps_half, 2), -0.5)]

        def rsqrt_small(out, in_, n, *after):
            t = ts(out, in_, EPS, ALU.add, after, q=pool)
            return tt(out, out, F[0:128, eps_half:eps_half + 1].to_broadcast([128, n]), ALU.pow, t, t_eps, q=pool)


        X, HTH, HTL, BIAS = page(0), page(1), page(2), span(3, 6)
        OA, OB, QN, QPE, KN, VM = page(7), page(8), page(9), page(10), page(11), page(12)
        COS, SIN, KPA, KPB = (QPE + 1024 + 256 * i for i in range(4))
        CF, CH, CL = span(13, 14), span(13, 14) + 1280, span(13, 14) + 2560
        XNT, HF = page(18), page(19)

        W.pages.extend([(24, []), (12, [])])

        mod = small(48)
        scale1, scale2 = small(8), small(8)
        cond = small(256)
        ones = small(1)
        t_ones = zero(fv(ones, 1), 1.0)
        inv_n, rcol = small(3), small(4)
        t_inv = [zero(fv(inv_n + i, 1), 1.0 / n) for i, n in enumerate((384, 256, 512))]

        t_cst = load("cst", fv(0, NCST1), a["cst"][:, 0:NCST1])
        posi = page(11)
        t_pos = load("pos", I[:, posi:posi + 321], a["posi"])
        maskat, rel, thr_k, tab = page(8), page(8) + 768, page(8) + 1088, page(8) + 1152
        t_tab = load("tab", fv(tab + 96, 192), a["tab"])
        pump()
        t_mask = load("mask", fv(maskat, 768), a["mask"])
        t_x = load("x", fv(X, 2048), a["xp"])
        W.pages.extend([(p, []) for p in (7, 15, 16)])
        pump()
        retire(15, 16)

        t_cond = acti(three(fv(cond, 256), 32), fv(cc("c"), 8).unsqueeze(2).to_broadcast([128, 8, 32]), ACT.Silu, t_cst)

        hi_i, lo_i, hi_f, lo_f = (page(13) + 321 * k for k in range(4))
        posf = page(14)
        iv = lambda at: I[:, at:at + 321]
        ta = t_hi = ts(iv(hi_i), iv(posi), 16, ALU.arith_shift_right, t_pos)
        tb = t_lo = ts(iv(lo_i), iv(posi), 65535, ALU.bitwise_and, t_pos)
        t_posf = cp(fv(posf, 256), I[:, posi + 64:posi + 320], t_pos)
        give(11, [t_posf, t_hi, t_lo])
        pump()
        ta = cp(fv(hi_f, 321), iv(hi_i), ta)
        tb = cp(fv(lo_f, 321), iv(lo_i), tb)
        ta = ts(fv(hi_f, 320), fv(hi_f, 320), fv(hi_f + 320, 1), ALU.subtract, ta)
        tb = ts(fv(lo_f, 320), fv(lo_f, 320), fv(lo_f + 320, 1), ALU.subtract, tb)
        t_rel = stt(fv(rel, 320), fv(hi_f, 320), 65536.0, fv(lo_f, 320), ALU.mult, ALU.add, ta, tb)
        t_thr = ts(fv(thr_k, 64), fv(rel, 64), ccol("thr"), ALU.subtract, t_rel, t_cst)
        tparts = [tab + 288 + 48 * i for i in range(3)]
        t = tt(fv(tab, 96), fv(tab + 96, 96), fv(tab + 192, 96), ALU.subtract, t_tab)
        t = cp(B16(tparts[0], 96), fv(tab, 96), t)
        t = tt(fv(tab, 96), fv(tab, 96), B16(tparts[0], 96), ALU.subtract, t)
        t = cp(B16(tparts[1], 96), fv(tab, 96), t)
        t = tt(fv(tab, 96), fv(tab, 96), B16(tparts[1], 96), ALU.subtract, t)
        t_tab = cp(B16(tparts[2], 96), fv(tab, 96), t)

        IND = [Ring([p + 512 * i for i in range(4)]) for p in (page(9), XNT)]
        bias_banks = Ring(Bank.S.slots)
        bias_toks, bias_reads = [], []
        t_h = []

        def bias_view(ch, at, n):
            return three(fv(BIAS + ch * 4096, 4096), 512)[:, :, at:at + n]

        def bias_start(g):
            s = IND[len(t_h) == 8].next()
            s.tok = []
            for i in range(4):
                s.tok.append(ts(B16(s.at + i * 128, 256), fv(rel + 64, 256), fv(thr_k + 4 * g + i, 1), ALU.is_le,
                                t_rel, t_thr, s.free, q=dve if i < (2 if g < 6 else 1) else pool))
            bias_reads.append(s.tok)
            return s

        def bias_sums(g, s):
            own = g // 8
            b = bias_banks.next()
            for i in range(4):
                for other in range(2):
                    ind = B16(s.at + i * 128 + 64 * (own ^ other), 128)
                    for j, at in enumerate(tparts):
                        if other:
                            o, w = PB[b.at][:, 384 + i * 32:416 + i * 32], B16(at, 96)
                            w = w.rearrange("p (k h) -> p k h", k=4)[:, :, 0:8]
                        else:
                            o, w = PB[b.at][:, i * 96:(i + 1) * 96], B16(at, 96)
                        t = mm(o, ind, w, j == 0, j == 2, s.tok, t_tab, b.free)
            s.free = [t]
            bias_reads.append(t)
            return b, t

        def bias_end(g, b, t):
            own = g // 8
            src = PB[b.at][:, 0:384].rearrange("p (k g h) -> p g h k", g=3, h=8)
            src0 = PB[b.at][:, 384:512].rearrange("p (k h) -> p h k", h=8)
            b.free = []
            for ch, ps in ((own, src[:, 0]), (1 - own, src0)):
                m = fv(maskat + ch * 256 + 16 * g, 16).unsqueeze(1).to_broadcast([128, 8, 16])
                b.free.append(tt(bias_view(ch, 16 * g, 16), m, ps, ALU.subtract, t, t_mask))
            for i in range(2):
                m = fv(maskat + 512 + i * 128 + 16 * (g % 8), 16).unsqueeze(1).to_broadcast([128, 8, 16])
                b.free.append(tt(bias_view(own, 256 + i * 128 + 16 * (g % 8), 16), m, src[:, 1 + i], ALU.subtract, t,
                                 t_mask))
            bias_toks.append(b.free[-1])

        def bias_all():
            s = {g: bias_start(g) for g in range(3)}
            p = {}
            yield
            for g in range(17):
                if g < 13:
                    s[g + 3] = bias_start(g + 3)
                if g < 16:
                    p[g] = bias_sums(g, s[g])
                if g:
                    bias_end(g - 1, *p[g - 1])
                yield
            give(8, [bias_toks, bias_reads])
            pump()

        bias = bias_all()

        part = Ring([page(17) + 512, page(17) + 1024])
        t_mod = {}
        GT = page(14)
        t_gt = {}

        def ada_block(cb):
            b = Bank.U.next()
            for half in range(2):
                u = take()
                for k in range(4):
                    t = mm(PB[b.at][32 * k:32 * k + 32, :], fv(cond + (4 * half + k) * 32, 32),
                           fv(page(u.page) + k * 512, 512), half == 0, half == 1, u.loaded, t_cond, b.free)
                done(u, t)
            s = part.next()
            e = acti(fv(s.at, 512), PB[b.at][:, :], ACT.Copy, t, s.free)
            b.free = [e]
            yield
            b = Bank.T.next()
            if cb in (4, 5, 10, 11):
                t = mm(PB[b.at][:, :], F[:, cc("sel4"):cc("sel4") + 1].to_broadcast([128, 128]), fv(s.at, 512),
                       True, True, e, b.free)
                at = GT + (cb // 10) * 1024 + (cb % 2) * 512
                t_mod[cb] = tt(fv(at, 512), PB[b.at][:, :], fv(at, 512), ALU.add, t, t_gt["rows"])
            else:
                for i in range(4):
                    t = tr(PB[b.at][:, i * 128:(i + 1) * 128], fv(s.at + i * 128, 128), e, b.free)
                m = fv(mod + cb * 4, 4)
                e = red(m, PB[b.at][:, :].rearrange("p (i k r) -> p i k r", k=4, r=32)[:, :, :, 0], ALU.add, t)
                t_mod[cb] = tt(m, m, fv(cc("b_ada", cb * 4), 4), ALU.add, e)
            s.free = [t]
            b.free = [t_mod[cb]]

        def ada_rest(cb):
            us, s = [take(), take()], part.next()
            acc_ = fv(s.at, 512)
            t = None
            for half, u in enumerate(us):
                for k in range(4):
                    w, c = fv(page(u.page) + k * 512, 512), fv(cond + (4 * half + k) * 32, 1)
                    if t is None:
                        t = ts(acc_, w, c, ALU.mult, u.loaded, t_cond, s.free)
                    else:
                        t = stt(acc_, w, c, acc_, ALU.mult, ALU.add, u.loaded, t)
                done(u, t)
                yield
            yield
            b = Bank.T.next()
            if cb in (4, 5, 10, 11):
                t = mm(PB[b.at][:, :], F[:, ones:ones + 1].to_broadcast([128, 128]), acc_, True, True, t, t_ones, b.free)
                at = GT + (cb // 10) * 1024 + (cb % 2) * 512
                t_mod[cb] = tt(fv(at, 512), PB[b.at][:, :], fv(at, 512), ALU.add, t, t_gt["rows"])
            else:
                for i in range(4):
                    t2 = mm(PB[b.at][:, i:i + 1], fv(s.at + i * 128, 128), fv(ones, 1), True, True, t, t_ones, b.free)
                t = t2
                t_mod[cb] = tt(fv(mod + cb * 4, 4), PB[b.at][:, 0:4], fv(cc("b_ada", cb * 4), 4), ALU.add, t)
            s.free = [t]
            b.free = [t_mod[cb]]

        next(bias)

        TWO_PI = 6.283185307179586
        P1 = 6.28125
        P2 = float(np.float32(TWO_PI - P1))
        P3 = float(np.float32(TWO_PI - P1 - float(np.float32(TWO_PI - P1))))
        MAGIC = 12582912.0
        ang, kk, rr = (page(14) + 512 + 256 * i for i in range(3))
        t_ang = ts(fv(ang, 256), fv(posf, 256), ccol("invf"), ALU.mult, t_posf, t_cst)

        def rope_table(out, quarter):
            t = ts(fv(kk, 256), fv(ang, 256), 1 / TWO_PI, ALU.mult, t_ang, t_rope, s2=quarter, op1=ALU.add)
            t = ts(fv(kk, 256), fv(kk, 256), MAGIC, ALU.add, t)
            t = ts(fv(kk, 256), fv(kk, 256), MAGIC, ALU.subtract, t)
            t = stt(fv(rr, 256), fv(kk, 256), -P1, fv(ang, 256), ALU.mult, ALU.add, t)
            t = stt(fv(rr, 256), fv(kk, 256), -P2, fv(rr, 256), ALU.mult, ALU.add, t)
            t = stt(fv(rr, 256), fv(kk, 256), -P3, fv(rr, 256), ALU.mult, ALU.add, t)
            if quarter:
                t = ts(fv(rr, 256), fv(rr, 256), TWO_PI / 4, ALU.add, t)
            t = ts(fv(rr, 256), fv(rr, 256), 3.1415925, ALU.min, t, s2=-3.1415925, op1=ALU.max)
            t = acti(fv(out, 256), fv(rr, 256), ACT.Sin, t)
            if not quarter:
                t = ts(fv(out, 256), fv(out, 256), ccol("sgn"), ALU.mult, t)
            t_rope.append(t)

        t_rope = []

        ada = [ada_block(cb) for cb in ADA_FIRST]
        next(ada[0])
        for _ in range(2):
            next(bias)
        next(ada[0], None)

        t_sq = [acti(fv(HF + ch * 1024, 1024), fv(X + ch * 1024, 1024), ACT.Square, t_x, scale=1 / 32,
                     accum=fv(ms + ch, 1)) for ch in range(2)]
        t_rs = rsqrt_small(fv(ms + 2, 2), fv(ms, 2), 2, t_sq)
        t_xn = [ts(fv(X + ch * 1024, 1024), fv(X + ch * 1024, 1024), fv(ms + 2 + ch, 1), ALU.mult, t_rs)
                for ch in range(2)]
        t_xnt = []

        def x_half(half):
            for b in (2 * half, 2 * half + 1):
                s = (Bank.O, Bank.T)[b % 2].next()
                for k in (2 * b, 2 * b + 1):
                    for ch in range(2):
                        t = tr(PB[s.at][:, (k % 2) * 256 + ch * 128:(k % 2) * 256 + ch * 128 + 128],
                               fv(X + ch * 1024 + k * 128, 128), t_xn[ch], s.free)
                e = acti(fv(XNT + b * 512, 512), PB[s.at][:, :], ACT.Copy, t)
                s.free = [e]
                t_xnt.extend([e, e])
            return t

        t_hf, t_s1 = [], []

        def h_half(half):
            o = 4 * half
            t_s1.append(stt(fv(scale1 + o, 4), fv(mod + 8 + o, 4), 1.0, fv(cc("g_mix", o), 4), ALU.add, ALU.mult,
                            t_mod[2 + half]))
            mods = [t_s1[half], t_mod[half]]
            for k in range(o, o + 4):
                col = dict(scale=fv(scale1 + k, 1), bias=fv(mod + k, 1))
                th = acti(rv(HTH + k * 256, 256), fv(XNT + k * 256, 256), ACT.Identity, t_xnt[k], mods, **col)
                e = ts(fv(HF + k * 256, 256), fv(XNT + k * 256, 256), col["scale"], ALU.mult, t_xnt[k], mods,
                       s2=col["bias"], op1=ALU.add, q=pool if k % 2 else dve)
                t_hf.append(e)
                tl = tt(rv(HTL + k * 256, 256), fv(HF + k * 256, 256), rf(HTH + k * 256, 256), ALU.subtract, th, e)
                t_h.append([th, tl])

        next(ada[1])
        x_half(0)
        next(ada[1], None)
        h_half(0)
        give(0, [x_half(1)])
        next(bias)
        next(bias)
        next(ada[2])
        W.hl.append((20, 21, []))
        pump()
        next(bias)
        next(ada[2], None)
        u0, b0 = take(), [Bank.O.next(), Bank.O.next()]
        next(ada[3])
        for i, b in enumerate(b0):
            fm(u0, 256, 8, HTH, HTL, b.at, 1, b.free, xtok=t_h, t0=i, k1=4)
            next(ada[3], None)
        h_half(1)
        W.hl.append((22, 23, []))
        pump()
        t0 = [fm(u0, 256, 8, HTH, HTL, b.at, 1, xtok=[None] * 4 + t_h[4:], t0=i, k0=4) for i, b in enumerate(b0)]
        for s in IND[1].slots:
            s.free = [t_h, t_hf]
        bg.append(bias)

        UO = Ring(Bank.U.slots + Bank.O.slots)

        def next_unit_fm(ncol, nk, xh, xl, tiles, t0=0, u=None, after=None):
            u = u or take()
            b = UO.next()
            t = fm(u, ncol, nk, xh, xl, b.at, tiles, b.free, after, t0=t0)
            return u, b, t

        t_c = []
        startup = [t_rel, t_thr]
        SQ = page(19)
        t_sq = []

        def squares(n, w, e):
            t_sq.append(acti(fv(SQ + n * 512, w), fv(CF + n * 512, w), ACT.Square, e, t_hf, t_h))

        for i, b in enumerate(b0):
            e = acti(fv(CF + i * 256, 256), PB[b.at][:, 0:256], ACT.Copy, t0[i], startup)
            b.free = [e]
            t_c.append(e)
        done(u0, t0[1])
        squares(0, 512, t_c)
        rope_table(COS, 0.25)
        tick()
        for n in range(1, 3):
            u, b, t = next_unit_fm(256, 8, HTH, HTL, 2)
            w = 512 if n < 2 else 256
            e = acti(fv(CF + n * 512, w), PB[b.at][:, 0:w], ACT.Copy, t, startup)
            b.free = [e]
            if n == 2:
                e2 = tt(fv(KPA, 256), PB[b.at][:, 256:512], fv(COS, 256), ALU.mult, e, t_rope[0])
                b.free = [e2]
            t_c.append(e)
            done(u, t)
            squares(n, w, e)
            if n == 1:
                rope_table(SIN, 0.0)
            tick()
        def latent_norm():
            sq = lambda k: fv(SQ + k * 256, 256)
            e = tt(sq(0), sq(0), sq(1), ALU.add, t_sq)
            e = tt(sq(0), sq(0), sq(2), ALU.add, e)
            e2 = tt(sq(3), sq(3), sq(4), ALU.add, t_sq)
            yield
            b = Bank.T.next()
            for i, k in ((0, 0), (1, 3)):
                for ch in range(2):
                    t = mm(PB[b.at][:, 2 * i + ch:2 * i + ch + 1], fv(SQ + k * 256 + ch * 128, 128),
                           fv(inv_n + i, 1), True, True, e, e2, t_inv, b.free)
            r4 = fv(rcol, 4)
            e = ts(r4, PB[b.at][:, 0:4], EPS, ALU.add, t)
            b.free = [e]
            t = tt(r4, r4, F[0:128, eps_half:eps_half + 1].to_broadcast([128, 4]), ALU.pow, e, t_eps, q=pool)
            yield
            b = Bank.T.next()
            for i in range(4):
                t2 = mm(PB[b.at][:, i * 128:i * 128 + 128], F[:, rcol + i:rcol + i + 1].to_broadcast([128, 128]), ident,
                        True, True, t, b.free)
            es = []
            for k in range(5):
                c = fv(CF + k * 256, 256)
                w = ccol("g_q", k) if k < 3 else ccol("g_kv", k - 3)
                r = PB[b.at][:, 0:256] if k < 3 else PB[b.at][:, 256:512]
                es.append(stt(c, c, w, r, ALU.mult, ALU.mult, t2, t_sq))
            for k, e in enumerate(es):
                c = fv(CF + k * 256, 256)
                th = acti(rv(CH + k * 256, 256), c, ACT.Copy, e, t_rope)
                tl = tt(rv(CL + k * 256, 256), c, rf(CH + k * 256, 256), ALU.subtract, th, e)
                t_cn.append([th, tl])
            b.free = [e]

        t_cn = []
        bg.append(latent_norm())
        retire(12)
        u, b, t = next_unit_fm(128, 8, HTH, HTL, 1)
        tmp = page(14) + 1792
        e = tt(fv(tmp, 256), PB[b.at][:, 0:256], fv(SIN, 256), ALU.mult, t, t_rope[1], startup)
        b.free = [e]
        done(u, t)
        e = tt(fv(KPA, 256), fv(KPA, 256), fv(tmp, 256), ALU.add, e, e2)
        t_kp = [zero(fv(KPB, 256, 0, 64), 0.0, q=dve)]
        t_kp.append(ts(fv(KPB, 256, 64, 128), fv(KPA, 256, 64, 128), -(192.0 ** -0.5), ALU.mult, e))
        t_kp.append(ts(fv(KPA, 256, 0, 64), fv(KPA, 256, 0, 64), -(192.0 ** -0.5), ALU.mult, e))
        t_kp.append(zero(fv(KPA, 256, 64, 128), 0.0, t_kp[1], q=dve))
        tick()

        DIL = [span(15, 17), span(9, 11)]
        dil_free = [[], []]
        t_dil_pages = retired(15, 16)
        dil_n = [0]

        def dil_unit(hp, free, t_qk, t_vv):
            n = dil_n[0]
            t_, g = DIL_UNITS[n % 9]
            dil_n[0] += 1
            u = take()
            b = Bank.U.next()
            dst = fv(DIL[hp % 2] + t_ * 1536 + g * 512, 512)
            if t_ < 2:
                t = fm(u, 256, 8, HTH, HTL, b.at, 2, b.free)
            else:
                for ch in range(2):
                    t = tm(u, 256, 0, 256, 8, HTH, HTL, PB[b.at][:, ch * 256:(ch + 1) * 256], ch, True, True, b.free)
            if t_ == 0:
                e = acti(dst, PB[b.at][:, :], ACT.Copy, t, free, scale=-(128.0 ** -0.5))
            elif t_ == 1 or g == 0:
                e = cp(dst, PB[b.at][:, :], t, free)
            else:
                e = acti(dst, PB[b.at][:, :], ACT.Copy, t, free)
            (t_vv if t_ == 2 else t_qk).append(e)
            b.free = [e]
            done(u, t)
            if ada_after(n) is not None:
                bg.append(ada_rest(ada_after(n)))
            tick()

        dil_toks = ([], [])
        for _ in range(DIL_AHEAD):
            dil_unit(0, t_dil_pages, *dil_toks)
        t_cst2 = load("cst2", fv(NCST1, NCST - NCST1), a["cst"][:, NCST1:NCST])
        retire(11)
        t_ind = [s.free for s in IND[0].slots]

        t_qn, t_qp = [], []
        for n in range(2):
            u = take()
            for half in range(2):
                _, b, t = next_unit_fm(512, 3, CH, CL, 2, t0=2 * half, u=u, after=t_cn)
                h = 4 * n + 2 * half
                e = cp(fv(QN + h * 256, 512), PB[b.at][:, :], t, t_ind) if half else \
                    acti(fv(QN + h * 256, 512), PB[b.at][:, :], ACT.Copy, t, t_ind)
                b.free = [e]
                t_qn += [e, e]
            done(u, t)
            tick()
        for n in range(2):
            u = take()
            for half in range(2):
                _, b, t = next_unit_fm(512, 3, CH, CL, 2, t0=2 * half, u=u)
                d = three(fv(QPE + half * 512, 512), 256)
                table = fv((COS, SIN)[n], 256).unsqueeze(1).to_broadcast([128, 2, 256])
                src = three(PB[b.at][:, :], 256)
                if n == 0:
                    e = tt(d, src, table, ALU.mult, t, t_rope)
                    b.free = [e]
                    t_qp.append(e)
                else:
                    e = tt(src, src, table, ALU.mult, t, t_rope)
                    e = tt(d, src, d, ALU.add, e, t_qp[half])
                    b.free = [e]
                    t_qp[half] = e
            done(u, t)
            tick()
        t_qp = [t_qp[0]] * 4 + [t_qp[1]] * 4

        P_RING = Ring([page(18) + 512 * i for i in range(4)])
        PT_RING = Ring([page(19) + 512 * i for i in range(4)])
        st_at = small(32)
        ST_RING = Ring([st_at + 8 * i for i in range(4)])
        t_oa, t_ob = [], []
        assert len(bias_toks) >= 15
        t_p0 = [t_h, t_hf, t_cn, t_sq, [s.free for s in IND[1].slots]]
        for r in (P_RING, PT_RING):
            for s in r.slots:
                s.free = t_p0
        t7 = []

        def mla_head(h):
            s, p, st = Bank.S.next(), P_RING.next(), ST_RING.next()
            for ch in range(2):
                o = PB[s.at][:, ch * 256:(ch + 1) * 256]
                mm(o, fv(QN + h * 256 + ch * 128, 128), fv(KN + h * 256, 256), True, False, s.free, t_qn[h], t_kn[h])
                t = mm(o, fv(QPE + (h // 2) * 256 + ch * 128, 128), fv(KPB if h % 2 else KPA, 256), False, True,
                       t_qp[h], t_kp)
            nmx, den, rd = (fv(st.at + 2 * i, 2) for i in range(3))
            t1 = red(nmx, three(PB[s.at][:, :], 256), ALU.min, t, st.free)
            t2 = [acti(fv(p.at + ch * 256, 256), PB[s.at][:, ch * 256:(ch + 1) * 256], ACT.Exp, t, t1, p.free, st.free,
                       bias=fv(st.at + ch, 1), scale=-1.0, accum=fv(st.at + 2 + ch, 1)) for ch in range(2)]
            s.free = t2
            t3 = recip(rd, den, t2)
            t4 = [ts(fv(p.at + ch * 256, 256), fv(p.at + ch * 256, 256), fv(st.at + 4 + ch, 1), ALU.mult, t3)
                  for ch in range(2)]
            st.free = t4
            yield
            s, pt = Bank.T.next(), PT_RING.next()
            for k in range(2):
                for ch in range(2):
                    t = tr(PB[s.at][:, k * 256 + ch * 128:k * 256 + ch * 128 + 128], fv(p.at + ch * 256 + k * 128, 128),
                           t4, s.free)
            p.free = [t]
            e = acti(fv(pt.at, 512), PB[s.at][:, :], ACT.Copy, t, pt.free)
            s.free = [e]
            yield
            s = Bank.O.next()
            if h == 0:
                t7.extend(retired(7))
            for k in range(2):
                t = mm(PB[s.at][:, 0:256], fv(VM + k * 1024 + h * 128, 128), fv(pt.at + k * 256, 256), k == 0, k == 1,
                       e, t_v, s.free)
            pt.free = [t]
            e = acti(fv(OA + h * 256, 256), PB[s.at][:, 0:256], ACT.Copy, t, t7)
            s.free = [e]
            t_oa.append(e)

        def mla_heads():
            live, h = [], 0
            for n in (2, 1, 2, 1, 1, 1, 0, 0):
                for _ in range(n):
                    live.append(mla_head(h))
                    h += 1
                for g in list(live):
                    if next(g, "end") == "end":
                        live.remove(g)
                yield

        t_kn, t_v = [], []
        retire(7)
        u = take()
        t11 = retired(11)
        for n in range(4):
            _, b, t = next_unit_fm(1024, 2, CH + 768, CL + 768, 2, t0=2 * n, u=u)
            e = acti(fv(KN + n * 512, 512), PB[b.at][:, :], ACT.Copy, t, t11, scale=-(192.0 ** -0.5))
            b.free = [e]
            t_kn += [e, e]
        tick()
        bg.append(mla_heads())
        tick()
        done(u, t)
        u = take()
        t12 = retired(12)
        for ch in range(2):
            for n in range(2):
                b = UO.next()
                t = tm(u, 1024, n * 512, 512, 2, CH + 768, CL + 768, PB[b.at][:, :], ch, True, True, b.free)
                e = cp(fv(VM + ch * 1024 + n * 512, 512), PB[b.at][:, :], t, t12)
                b.free = [e]
                t_v.append(e)
        done(u, t)
        tick()
        t_lat = t
        give(13, [t_lat, t_cn])
        pump()
        t_gt["rows"] = [load("rows", fv(GT + r * 1024, 1024), a["rows"][r, :].partition_broadcast(128), t_lat, t_cn,
                             t_kp) for r in range(2)][-1]

        assert len(bias_toks) == 16
        X1 = page(16)
        t_bias_read, t_ob_free = [], []

        def dil_item(hp, hh, ch, t_qk, t_vv, pair):
            at = DIL[hp % 2]
            h = 2 * hp + hh
            q = lambda g: fv(at + g * 512 + hh * 256 + ch * 128, 128)
            k = lambda g, c0, n: fv(at + 1536 + g * 512 + hh * 256 + c0, n)
            v = lambda g, c: fv(at + 3072 + g * 512 + c * 256 + hh * 128, 128)
            s, p, st = Bank.S.next(), P_RING.next(), ST_RING.next()
            mm(PB[s.at][:, 0:256], q(0), k(0, 0, 256), True, True, s.free, t_qk)
            mm(PB[s.at][:, 256:384], q(1), k(1, ch * 128, 128), True, True)
            t = mm(PB[s.at][:, 384:512], q(2), k(2, ch * 128, 128), True, True)
            dil_free[hp % 2].append(t)
            nmx, den, rd = (fv(st.at + i, 1) for i in range(3))
            sc, pv, bias = PB[s.at][:, :], fv(p.at, 512), fv(BIAS + ch * 4096 + h * 512, 512)
            t1 = dve.do(lambda e: e.tensor_tensor_reduce(out=pv, in0=sc, in1=bias, scale=1.0, scalar=3e38,
                                                         op0=ALU.add, op1=ALU.min, accum_out=nmx),
                        t, p.free, st.free, bias_toks)
            s.free = [t1]
            t2 = acti(pv, pv, ACT.Exp, t1, bias=nmx, scale=-1.0, accum=den)
            t3 = recip(rd, den, t2)
            t4 = ts(pv, pv, rd, ALU.mult, t3, t2)
            st.free = [t4]
            t_bias_read.append(t1)
            yield
            s, pt = Bank.T.next(), PT_RING.next()
            for i in range(4):
                t = tr(PB[s.at][:, i * 128:(i + 1) * 128], fv(p.at + i * 128, 128), t4, s.free)
            p.free = [t]
            if ch:
                e = acti(fv(pt.at, 512), PB[s.at][:, :], ACT.Copy, t, pt.free)
            else:
                e = cp(fv(pt.at, 512), PB[s.at][:, :], t, pt.free)
            s.free = [e]
            yield
            if "bank" not in pair:
                pair["bank"] = Bank.O.next()
            s = pair["bank"]
            o = PB[s.at][:, hh * 256 + ch * 128:hh * 256 + ch * 128 + 128]
            for i, (g, c) in enumerate(((0, 0), (0, 1), (1, ch), (2, ch))):
                t = mm(o, v(g, c), fv(pt.at + i * 128, 128), i == 0, i == 3, e, t_vv, s.free)
            pt.free = [t]
            dil_free[hp % 2].append(t)
            pair["n"] = pair.get("n", 0) + 1
            if pair["n"] == 4:
                if hp == 0:
                    t_ob_free.extend(retired(8))
                e = cp(fv(OB + hp * 512, 512), PB[s.at][:, :], t, t_ob_free)
                s.free = [e]
                t_ob.append(e)

        def dil_pair(hp, t_qk, t_vv):
            pair = {}
            live = []
            for hh, ch in ((0, 0), (0, 1), (1, 0), (1, 1), (None, None), (None, None)):
                if hh is not None:
                    live.append(dil_item(hp, hh, ch, t_qk, t_vv, pair))
                for g in list(live):
                    if next(g, "end") == "end":
                        live.remove(g)
                yield

        W.pool_share = 512
        for hp in range(4):
            free = [dil_free[hp % 2], t_dil_pages if hp == 0 else None, t_oa if hp == 1 else None]
            if hp:
                dil_toks = ([], [])
            dil_free[hp % 2] = []
            while dil_n[0] < 9 * hp + 9:
                dil_unit(hp, free, *dil_toks)
                if dil_n[0] == 35:
                    t_dil_a = dil_free[0]
                    assert len(t_dil_a) == 8
                    give(15, [t_dil_a])
                    t_xr = load("xr", fv(X1, 2048), a["xn"], t_dil_a)
                    pump()
            if hp == 0:
                assert len(t_oa) == 8
                give(12, [t_oa])
                retire(8)
            if hp == 2:
                assert len(t_bias_read) >= 8
                give(3, t_bias_read[:8])
                pump()
            bg.append(dil_pair(hp, *dil_toks))
        assert len(t_mod) == 12
        give(17, [s.free for s in part.slots] + [t_dil_a])
        pump()

        YH, YL = page(6), page(4)
        nat = lambda ap: ap.rearrange("p (l j c) -> p c j l", l=16, j=4)
        perm = lambda ap: ap.rearrange("p (c j l) -> p c j l", c=4, j=4)
        t_y = []

        def gate_mix(j):
            g, t_g = gates[j]
            e1 = stt(fv(g, 256), fv(g, 256), 1.0, fv(OA + j * 256, 256), ALU.add, ALU.mult, t_g, t_oa)
            e2 = stt(fv(g + 256, 256), fv(g + 256, 256), 1.0, fv(OB + j * 256, 256), ALU.add, ALU.mult, t_g, t_ob[j // 2])
            y = OA + j * 256
            e = tt(nat(fv(y, 256)), perm(fv(g, 256)), perm(fv(g + 256, 256)), ALU.add, e1, e2)
            th = ts(rv(YH + j * 256, 256), fv(y, 256), 0.5, ALU.mult, e, t_bias_read)
            tl = stt(rv(YL + j * 256, 256), fv(y, 256), 0.5, rf(YH + j * 256, 256), ALU.mult, ALU.subtract, th, e)
            gate_free[j % 4] = e
            t_y.append([th, tl])

        gates, gate_free = [], [t_bias_read[:8]] * 4
        W.pool_share = 1024
        for j in range(8):
            u = take()
            b = Bank.U.next()
            t = fm(u, 256, 8, HTH, HTL, b.at, 2, b.free)
            tick()
            g = page(5) + j % 4 * 512
            e = acti(fv(g, 512), PB[b.at][:, :], ACT.Tanh, t, gate_free[j % 4], scale=0.5)
            b.free = [e]
            gates.append((g, e))
            if j == 3:
                assert len(t_bias_read) == 16
            if j == 5:
                assert len(t_ob) == 4
                W.hl.append((18, 19, [s.free for r in (P_RING, PT_RING) for s in r.slots]))
                for p in (9, 10, 11):
                    give(p, [dil_free[1]])
            done(u, t)
            for i in {3: (0,), 4: (1, 2), 5: (3, 4), 6: (5, 6), 7: (7,)}.get(j, ()):
                gate_mix(i)
        t_h_read = t

        banks = [2, 3, 4, 5]
        bank_free = [[], [], [], []]

        def out_part(u, ch, half, xh, xl, first, last, *after):
            for k in range(2):
                w = k * 1024 + half * 512
                wh, wl = rv(u.hi + w, 512), rv(u.lo + w, 512)
                h, l = (rv(x + k * 256 + ch * 128, 128) for x in (xh, xl))
                o = PB[banks[2 * ch + half]][:, :]
                mm(o, h, wh, first and k == 0, False, u.tok, after, bank_free[2 * ch + half] if first else None)
                mm(o, h, wl, False, False)
                t = mm(o, l, wh, False, last and k == 1)
            return t

        def out_units(n, xh, xl, xtok, held=0, after_each=lambda: None, begun=False):
            for i in range(n - held):
                u = take()
                for ch in range(2):
                    for half in range(2):
                        t = out_part(u, ch, half, xh + i * 512, xl + i * 512, i == 0 and not begun, i == n - 1,
                                     xtok[2 * i:2 * i + 2])
                after_each()
                done(u, t)
            if not held:
                return t
            return [(take(), xh + i * 512, xl + i * 512, i == 0, i == n - 1, xtok[2 * i:2 * i + 2])
                    for i in range(n - held, n)]

        def held_part(held, ch, by_half=False, hooks={}):
            order = [(i, half) for i in range(len(held)) for half in range(2)]
            t_m, t_u = {}, {}
            for n, (i, half) in enumerate(sorted(order, key=lambda x: x[::-1]) if by_half else order):
                u, xh, xl, first, last, *after = held[i]
                t_m[half] = t_u[i] = out_part(u, ch, half, xh, xl, first, last, after)
                if n in hooks:
                    hooks[n](t_u[i])
            return t_m, t_u

        st_ms = [small(8) for _ in range(2)]

        def halves(at, ch):
            return [fv(at + ch * 1024 + h * 512, 512) for h in range(2)]

        def rsqrt_sum(out, s, *after):
            t = ts(fv(out, 1), fv(s, 1), fv(s + 1, 1), ALU.add, after, s2=EPS, op1=ALU.add, q=pool)
            return tt(fv(out, 1), fv(out, 1), fv(eps_half, 1), ALU.pow, t, t_eps, q=pool)

        bank_free[:] = [s.free for s in Bank.S.slots + Bank.T.slots]
        held = out_units(4, YH, YL, t_y, 3)
        SC, H2T = page(2), page(1)
        XET = [(page(7), page(5))[k // 4] + k % 4 * 512 for k in range(8)]

        def tiles4(half, left, ch, view=None):
            o = left * 256 + ch * 128
            return (view or fv)(XET[4 * half], 2048).rearrange("p (k c) -> p k c", c=512)[:, :, o:o + 128]

        t_s2 = stt(fv(scale2, 8), fv(mod + 32, 8), 1.0, fv(cc("g_ffn"), 8), ALU.add, ALU.mult, t_mod[8], t_mod[9])
        t_aff2 = [t_s2, t_mod[6], t_mod[7]]
        t_x1, t_xn, t_xh, t_xl = [], [], [], []

        def residual(ch, t_m):
            st = st_ms[ch]
            x, sc, xn = halves(X1, ch), halves(SC, ch), [tiles4(h, 1, ch) for h in range(2)]
            es = []
            for h in range(2):
                e = tt(sc[h], PB[banks[2 * ch + h]][:, :], fv(GT + h * 512, 512), ALU.mult, t_m[h], t_mod[4 + h], t_h_read)
                bank_free[2 * ch + h] = [e]
                es.append(tt(x[h], sc[h], x[h], ALU.add, e, t_xr))
            t_x1.append(es)
            t_s = [acti(xn[h], three(x[h], 128), ACT.Square, es[h], t_y, scale=1 / 32, accum=fv(st + h, 1)) for h in range(2)]
            t_rs = rsqrt_sum(st + 2, st, t_s)
            t_xn.append([ts(xn[h], three(x[h], 128), fv(st + 2, 1), ALU.mult, t_rs, es[h]) for h in range(2)])

        SLOT, AT, PH = page(8), page(8) + 256, page(8) + 512
        RT, WK, CUM, SEL = (GT + 256 * i for i in range(4))
        aff, stat, thr8, ST = RT, RT + 32, RT + 40, RT + 72
        w_neg = cc("w_router")
        t_wn = ts(fv(w_neg, 128), fv(cc("w_router"), 128), -1.0, ALU.mult, t_cst)
        w_sc, w_sh = small(128), small(16)
        by_k = lambda at: fv(at, 8).unsqueeze(2).to_broadcast([128, 8, 16])
        e = tt(three(fv(w_sc, 128), 16), three(fv(w_neg, 128), 16), by_k(mod + 24), ALU.mult, t_wn, t_aff2)
        t_wsh = red(fv(w_sh, 16), fv(w_sc, 128).rearrange("p (k e) -> p e k", e=16), ALU.add, e)
        t_ws = tt(three(fv(w_sc, 128), 16), three(fv(w_neg, 128), 16), by_k(scale2), ALU.mult, t_wsh, t_s2)
        w16 = lambda at, n=256: fv(at, n, 0, 16)
        t_at, t_wk, t_lg = [], [], []

        def route(ch):
            t_h2 = []
            for j in range(2):
                bk = PB[banks[2 * ch + j]]
                for k in range(4):
                    t = tr(bk[:, k * 128:(k + 1) * 128], fv(XET[4 * j + k] + 256 + ch * 128, 128), t_xn[ch][j],
                           bank_free[2 * ch + j])
                dst = fv(H2T + ch * 1024 + j * 512, 512)
                e = acti(dst, bk[:, :], ACT.Copy, t, t_h_read) if j else cp(dst, bk[:, :], t, t_h_read)
                es = [e] * 4
                bank_free[2 * ch + j] = es
                t_h2 += es
            t_xh.append([acti(tiles4(h, 0, ch, rv), tiles4(h, 1, ch), ACT.Copy, t_xn[ch][h], t_y) for h in range(2)])
            t_xl.append([tt(tiles4(h, 1, ch, rv), tiles4(h, 1, ch), tiles4(h, 0, ch, rf), ALU.subtract, t, t_xh[ch][h],
                            q=pool) for h in range(2)])
            yield
            b = Bank.O.slots[ch]
            lg = PB[b.at][:, 0:16]
            mm(lg, F[:, ones:ones + 1].to_broadcast([128, 128]), fv(w_sh, 16), True, False, t_ones, t_wsh, b.free)
            for k in range(8):
                t = mm(lg, fv(H2T + ch * 1024 + k * 128, 128), fv(w_sc + k * 16, 16), False, k == 7, t_h2[k], t_ws)
            t_lg.append(t)
            mx, sm, a_ = fv(stat + 2 * ch, 1), fv(stat + 2 * ch + 1, 1), fv(aff + ch * 16, 16)
            e = red(mx, lg, ALU.min, t, t_x1)
            e = acti(a_, lg, ACT.Exp, e, bias=mx, scale=-1.0, accum=sm)
            e1 = recip(sm, sm, e)
            e = ts(a_, a_, sm, ALU.mult, e1)
            yield
            t = tr(PB[b.at][0:16, 128:256], a_, e)
            e = cp(w16(WK + ch * 128, 128), PB[b.at][0:16, 128:256], t, t_x1)
            b.free = [e]
            t_wk.append(e)
            t_at.append(acti(w16(AT + ch * 128, 128), w16(WK + ch * 128, 128), ACT.Copy, e, t_y))
            yield

        def release(u, tok):
            for p in u.hl:
                give(p, [tok])
            pump()

        t_m, _ = held_part(held, 0)
        residual(0, t_m)
        steps = [route(ch) for ch in range(2)]

        def after_second(tok):
            release(held[1][0], tok)
            next(steps[0])

        t_m, t_o = held_part(held, 1, hooks={1: lambda tok: release(held[0][0], tok), 3: after_second})
        release(held[2][0], t_o[2])
        assert not W.hl
        give(6, [t_o[2]])
        give(4, [t_o[2]])
        pump()
        residual(1, t_m)
        give(2, [t_x1, t_h_read])
        pump()
        for ch in (0, 1, 0, 1, 1):
            next(steps[ch])
        give(1, t_lg)
        pump()

        e = t_wk
        for i in range(4):
            m8 = w16(thr8 + 8 * i, 8)
            e = dve.do(lambda e_, o=m8: e_.max(o, w16(WK)), e)
            if i < 3:
                e = dve.do(lambda e_, o=m8: e_.match_replace(w16(WK), o, w16(WK), -1.0), e, t_at)
        thr = w16(thr8 + 31, 1)
        one16 = F[0:16, ones:ones + 1].to_broadcast([16, 256])

        def cumsum(out, in_, *after):
            return dve.do(lambda e_: e_.tensor_tensor_scan(out, one16, in_, 0.0, ALU.mult, ALU.add), after)

        e1 = ts(w16(SEL), w16(AT), thr, ALU.is_gt, e, t_at)
        e2 = ts(w16(WK), w16(AT), thr, ALU.is_equal, e, t_at, q=pool)
        e3 = cumsum(w16(CUM), w16(SEL), e1, t_ones)
        e4 = cumsum(w16(SLOT), w16(WK), e2, t_ones)
        e1 = tt(w16(SEL), w16(SEL), w16(CUM), ALU.mult, e3)
        e2 = stt(w16(WK), w16(SLOT), w16(CUM + 255, 1), w16(WK), ALU.add, ALU.mult, e3, e4)
        t_slot = stt(w16(SLOT), w16(SEL), -1.0, w16(WK), ALU.add, ALU.add, e1, e2)

        b = Bank.O.slots[0]
        t_p = []
        iota = fv(cc("iota"), 32)
        for ch in range(2):
            t = tr(PB[b.at][:, ch * 16:ch * 16 + 16], w16(SLOT + ch * 128, 128), t_slot, b.free, n=16)
        e = cp(fv(ST, 32), PB[b.at][:, 0:32], t)
        b.free = [e]
        for ch in range(2):
            o = rv(PH + ch * 512, 512).rearrange("p (e s) -> p e s", s=32)
            t_p.append(tt(o, fv(ST + ch * 16, 16).unsqueeze(2).to_broadcast([128, 16, 32]),
                          iota.unsqueeze(1).to_broadcast([128, 16, 32]), ALU.is_equal, e, t_y))
        for s, f in zip(Bank.S.slots + Bank.T.slots, bank_free):
            s.free = f
        t_xe = []

        def gather(k):
            s = (Bank.S, Bank.T)[k % 2].next()
            for ch in range(2):
                c = XET[k] + ch * 128
                mm(PB[s.at][:, :], rv(c, 128), rv(PH + ch * 512, 512), ch == 0, False, t_p[ch], t_xh[ch], t_xl[ch],
                   s.free)
                t = mm(PB[s.at][:, :], rv(c + 256, 128), rv(PH + ch * 512, 512), False, ch == 1)
            t_gather.append(t)
            if k % 2:
                e = acti(fv(XET[k], 512), PB[s.at][:, :], ACT.Identity, t, t_aff2, t_h_read, t_x1,
                         bias=fv(mod + 24 + k, 1), scale=fv(scale2 + k, 1))
            else:
                e = ts(fv(XET[k], 512), PB[s.at][:, :], fv(scale2 + k, 1), ALU.mult, t, t_aff2, t_h_read, t_x1,
                       s2=fv(mod + 24 + k, 1), op1=ALU.add)
            s.free = [e]
            t_xe.append(e)

        t_gather = []
        gather(0)

        W.pool_share = 0
        XY = Ring(Bank.S.slots)
        acc = Bank.T.slots + Bank.O.slots
        PG, YR = Ring([page(8) + 512, page(8) + 768]), Ring([page(8) + 1024])
        for r in (PG, YR):
            for s in r.slots:
                s.free = [t_at, t_gather]
        work = {}
        gfin = GT
        idr, idb, tri_at = small(32), small(64), w_sc
        t_gf = [load("gfin", fv(gfin, 1024, 0, 1), a["rows"][2:3, :], t_p)]
        t_tri = load("tri", fv(tri_at, 128), a["tri"], t_p)
        W.after_moe = lambda: retire(18, 19, 20, 21, 22, 23, 1, 2, 3, 4, 6, 9, 10, 11, 12, 13, 17)
        t_idr = [acti(rv(idr, 32, p, p + 32), fv(cc("ident", p), 32, p, p + 32), ACT.Copy, t_cst) for p in (0, 32)]
        t_idb = cp(B16(idb, 128), ident, t_cst)
        C_Q = [0.0] + [1.0 / (2 * k + 1) for k in range(1, 8)]

        def softplus(out, v, ab, n, tmp, t_v, t_ab):
            e_, s_, q_ = (fv(tmp + i * n, n) for i in range(3))
            t = acti(e_, ab, ACT.Exp, t_ab, scale=-1.0)
            t1 = ts(s_, e_, 2.0, ALU.add, t)
            t1 = recip(s_, s_, t1)
            t1 = tt(s_, s_, e_, ALU.mult, t1)
            yield
            t2 = tt(e_, s_, s_, ALU.mult, t1)
            t3 = ts(q_, e_, C_Q[7], ALU.mult, t2)
            for k in range(6, 0, -1):
                if k % 2 == 0:
                    yield
                t3 = stt(q_, q_, C_Q[k], e_, ALU.add, ALU.mult, t3)
            yield
            t3 = stt(q_, q_, 1.0, s_, ALU.add, ALU.mult, t3)
            t4 = ts(v, v, 0.0, ALU.max, t_v)
            yield stt(out, q_, 2.0, v, ALU.mult, ALU.add, t3, t4)

        t_half = [ts(fv(cc(k), n), fv(cc(k), n), 0.5, ALU.mult, t_cst2) for k, n in (("conv_w", 96), ("conv_b", 24))]

        lam, lab, ltm, bgh = small(10), small(10), small(30), small(20)
        t_v = ts(fv(lam, 10), fv(cc("lam"), 10), -1.0, ALU.mult, t_cst2)
        t_ab = acti(fv(lab, 10), fv(lam, 10), ACT.Abs, t_v)
        *_, t = softplus(fv(lab, 10), fv(lam, 10), fv(lab, 10), 10, ltm, [t_v, t_ab], t_ab)
        t_lam = [ts(fv(lab, 10), fv(lab, 10), -4.0, ALU.mult, t)]
        t_lam.append(ts(fv(lam, 10), fv(lab, 10), -1.0, ALU.mult, t_lam[0]))
        t_bgh = ts(fv(bgh, 20), fv(cc("l_bgx"), 20), 0.5, ALU.mult, t_cst2)

        a_exp = small(1)
        t_a = acti(fv(a_exp, 1), ccol("a_log"), ACT.Exp, t_cst2)
        moe_pg, moe_ht, moe_y = {}, {}, {}

        def expert_up(e):
            gb, ub = Bank.U.next(), Bank.U.next()
            for b in (gb, ub):
                for k in range(8):
                    if len(t_xe) < 8:
                        gather(len(t_xe))
                    u = take()
                    for j in range(4):
                        t = mm(PB[b.at][32 * j:32 * j + 32, :], fv(XET[k] + e * 32, 32),
                               fv(page(u.page) + j * 512, 512), k == 0, k == 7, u.loaded, t_xe[k], b.free)
                    if b is ub and k == 7 and e == 0:
                        retire(u.page)
                    done(u, t)
                if b is gb:
                    t_g = t
                    if e > 1:
                        scatter(e - 2)
            if e == 0:
                p = u.page
                for name, ats in (("hid", [0]), ("ht", [512, 1024]), ("af", [1536])):
                    work[name] = Ring([page(p) + at for at in ats])
                    for s in work[name].slots:
                        s.free = [W.given[p]]
                work["page"] = p
                retired(p)
            s, af, pg = XY.next(), work["af"].next(), PG.next()
            t2 = mm(PB[s.at][:, :], F[0:16, cc("ident", e):cc("ident", e) + 1].to_broadcast([16, 128]),
                    fv(SLOT, 512, 0, 16), True, True, t_slot, s.free)
            ta = acti(fv(af.at, 256), PB[s.at][:, 256:512], ACT.Copy, t2, af.free)
            t_pg = stt(fv(pg.at, 256), PB[s.at][:, 0:256], ccol("pmod"), fv(af.at, 256), ALU.is_equal, ALU.mult,
                       t2, ta, pg.free)
            s.free, af.free = [t_pg], [t_pg]
            moe_pg[e] = pg, t_pg

            hid = work["hid"].next()
            t_sg = acti(fv(hid.at, 512), PB[gb.at][:, :], ACT.Silu, t_g, hid.free)
            t_hid = tt(fv(hid.at, 512), fv(hid.at, 512), PB[ub.at][:, :], ALU.mult, t_sg, t)
            ub.free = [t_hid]

            def turned():
                ht = work["ht"].next()
                for c in range(4):
                    t = tr(PB[gb.at][:, c * 128:(c + 1) * 128], fv(hid.at + c * 128, 128), t_hid)
                hid.free = [t]
                t_ht = cp(fv(ht.at, 512), PB[gb.at][:, :], t, ht.free)
                gb.free = [t_ht]
                moe_ht[e] = ht, t_ht

            return gb, ub, turned

        def expert_down(e, between):
            ht, t_ht = moe_ht.pop(e)
            yb, y = [XY.next(), XY.next()], YR.next()
            for n in range(8):
                u = take()
                c = n // 2
                for half in range(2):
                    for jj in range(2):
                        j = 2 * (n % 2) + jj
                        t = mm(PB[yb[half].at][32 * j:32 * j + 32, :], fv(ht.at + c * 128 + 32 * j, 32),
                               fv(page(u.page) + jj * 1024 + half * 512, 512), c == 0, c == 3, u.loaded, t_ht,
                               yb[half].free)
                done(u, t)
                if n == 3:
                    between()
            ht.free = [t]
            t_ye = [tt(fv(y.at + n * 512, 512), PB[yb[n].at][:, :], fv(GT + 1024 + n * 512, 512), ALU.mult, t, t_mod[10],
                       t_mod[11], y.free) for n in range(2)]
            yb[0].free, yb[1].free = [t_ye[0]], [t_ye[1]]
            moe_y[e] = y, t_ye

        def scatter(e):
            (pg, t_pg), (y, t_ye) = moe_pg.pop(e), moe_y.pop(e)
            t = []
            for ch in range(2):
                for n in range(2):
                    o = PB[acc[2 * ch + n].at][:, :]
                    if e == 0:
                        mm(o, ident, fv(X1 + ch * 1024 + n * 512, 512), True, False, t_x1, acc[2 * ch + n].free)
                    t.append(mm(o, fv(pg.at + ch * 128, 128), fv(y.at + n * 512, 512), False, e == NEXP - 1, t_ye[n], t_pg))
            y.free, pg.free = t, t
            return t

        def final_weights():
            for h in range(2):
                s, g = XY.next(), gfin + h * 512
                t = mm(PB[s.at][:, :], F[0:1, ones:ones + 1].to_broadcast([1, 128]), fv(g, 512, 0, 1), True, True, t_gf[0],
                       t_ones, s.free)
                s.free = [acti(fv(g, 512), PB[s.at][:, :], ACT.Copy, t)]
                t_gf.append(s.free)

        for e in range(NEXP):
            gb, ub, turned = expert_up(e)
            if e:
                expert_down(e - 1, turned)
            else:
                turned()
                final_weights()
        expert_down(NEXP - 1, lambda: scatter(NEXP - 2))
        t_moe = scatter(NEXP - 1)
        give(work["page"], [t_moe])

        HT_H, HT_L, SCA = page(1), page(2), page(11)

        def post_sums(ch, row, t_m, t_row, sca, scb, free):
            st = st_ms[ch]
            mw, junk = halves(sca, ch), halves(scb, ch)
            t_s, t_w = [], []
            for h in range(2):
                src = PB[banks[2 * ch + h]][:, :]
                t_s.append(acti(junk[h], src, ACT.Square, t_m[h], free, scale=1 / 32, accum=fv(st + h, 1)))
                t_w.append(tt(mw[h], src, fv(row + h * 512, 512), ALU.mult, t_m[h], t_row, free, t_s[h]))
                bank_free[2 * ch + h] = [t_w[h]]
            return t_s, t_w

        def post_norm(ch, sca, t_s, t_w):
            st = st_ms[ch]
            x, mw = halves(X1, ch), halves(sca, ch)
            t_rs = rsqrt_sum(st + 2, st, t_s)
            return [stt(x[h], mw[h], fv(st + 2, 1), x[h], ALU.mult, ALU.add, t_rs, t_w) for h in range(2)]

        def pre_norm(ch, t_x, sca, scb):
            st = st_ms[ch] + 4
            x, out, junk = halves(X1, ch), halves(sca, ch), halves(scb, ch)
            t_s = [acti(junk[h], x[h], ACT.Square, t_x[h], scale=1 / 32, accum=fv(st + h, 1)) for h in range(2)]
            t_rs = rsqrt_sum(st + 2, st, t_s)
            return [ts(out[h], x[h], fv(st + 2, 1), ALU.mult, t_rs, t_x) for h in range(2)]

        def turn_fm(g, ch, t_n, sca, free):
            toks = []
            for j in range(2):
                bk = PB[banks[2 * ch + j]]
                for k in range(4):
                    t = tr(bk[:, k * 128:(k + 1) * 128], fv(sca + ch * 1024 + j * 512 + k * 128, 128), t_n[j],
                           bank_free[2 * ch + j])
                out = [(4 * j + k) * 256 + ch * 128 for k in range(4)]
                src = [bk[:, k * 128:(k + 1) * 128] for k in range(4)]
                col = [ccol("pre", g * 8 + 4 * j + k) for k in range(4)]
                th = [acti(rv(HT_H + out[k], 128), src[k], ACT.Copy, t, free, scale=col[k]) for k in range(4)]
                tl = [stt(rv(HT_L + out[k], 128), src[k], col[k], rf(HT_H + out[k], 128), ALU.mult, ALU.subtract, th, free)
                      for k in range(4)]
                bank_free[2 * ch + j] = tl
                toks += zip(th, tl)
            return toks

        def lead_tm(us, ch, xtok):
            for u in us:
                o = PB[u.bank.at][:, ch * 256:(ch + 1) * 256]
                w = lambda at, k: rv(at + k * 256, 256)
                x = lambda at, k: rv(at + k * 256 + ch * 128, 128)
                for j in range(0, 8, 4):
                    for k in range(j, j + 4):
                        mm(o, x(HT_H, k), w(u.hi, k), k == 0, False, u.tok, xtok[k][0], u.bank.free)
                        mm(o, x(HT_H, k), w(u.lo, k), False, False)
                    for k in range(j, j + 4):
                        u.t = mm(o, x(HT_L, k), w(u.hi, k), False, k == 7, xtok[k][1])

        def lead_fm(us, sca):
            es = [acti(fv(sca + i * 512, 512), PB[u.bank.at][:, :], ACT.Copy, u.t) for i, u in enumerate(us[:2])]
            us[2].t = fm(us[2], 256, 8, HT_H, HT_L, us[2].bank.at, 2, us[2].bank.free)
            for i, u in enumerate(us[:2]):
                u.read = u.t
                for k in range(2):
                    for ch in range(2):
                        u.t = tr(PB[u.bank.at][:, k * 256 + ch * 128:k * 256 + ch * 128 + 128],
                                 fv(sca + i * 512 + ch * 256 + k * 128, 128), es[i])

        def take_lead(slots):
            us = []
            for s in slots:
                us.append(take())
                us[-1].bank = s
            return us

        def turn(g, held, slots, row, t_row, sca, scb, free, t_h_read):
            t_m, t_x, t_n = {}, {}, {}

            def sums(ch):
                return post_sums(ch, row, t_m[ch], t_row, sca, scb, free)

            def norms(ch, toks):
                t_x[ch] = post_norm(ch, sca, *toks)
                t_n[ch] = pre_norm(ch, t_x[ch], sca, scb)

            t_m[0], _ = held_part(held, 0)
            norms(0, sums(0))
            t_m[1], t_last = held_part(held, 1, True)
            done(held[0][0], t_last[0])
            us = take_lead(slots)
            toks = sums(1)
            xtok = turn_fm(g, 0, t_n[0], sca, t_h_read)
            norms(1, toks)
            lead_tm(us[:2], 0, xtok)
            xtok = turn_fm(g, 1, t_n[1], sca, t_h_read)
            lead_tm(us[:2], 1, xtok)
            lead_fm(us, sca)
            done(held[1][0], t_last[1])
            us[0].owed = held[2][0], t_last[2]
            return [t_x[0], t_x[1]], us, t_last[2]

        def row_load(name, at, r, *after):
            return load(name, fv(at, 1024), a["rows"][r, :].partition_broadcast(128), after)

        BC, XS, XDT, ST = page(3), span(7, 8), span(9, 10), page(11)
        DT, CS, CSR, TM, DEC, NEG = (page(4) + i for i in (0, 256, 512, 768, 928, 1056))
        E2_ = page(6) + 1536
        CBT, BTM, XDD = page(6), page(6) + 1024, page(12)
        YGH, YGL = span(9, 10), span(13, 14)

        given = retired(1, 2, 3, 4, 6, 9, 10, 11, 12, 13)
        t_old = [t_moe, given]
        t_hl = retired(18, 19, 20, 21, 22, 23)

        Y = page(9)

        def last_norm(ch):
            st = st_ms[ch]
            v = [PB[acc[2 * ch + h].at][:, :] for h in range(2)]
            x, junk, out = halves(X1, ch), halves(Y, ch), halves(SCA, ch)
            g = [fv(gfin + h * 512, 512) for h in range(2)]
            t_m = t_moe[2 * ch:2 * ch + 2]
            s0 = acti(junk[0], v[0], ACT.Square, t_m[0], given, scale=1 / 32, accum=fv(st, 1))
            w0 = tt(x[0], v[0], g[0], ALU.mult, t_m[0], t_gf, s0)
            s1 = acti(junk[1], v[1], ACT.Square, t_m[1], given, scale=1 / 32, accum=fv(st + 1, 1))
            w1 = tt(x[1], v[1], g[1], ALU.mult, t_m[1], t_gf, s1)
            q0 = acti(junk[0], x[0], ACT.Square, w0, s0, scale=1 / 32, accum=fv(st + 4, 1))
            q1 = acti(junk[1], x[1], ACT.Square, w1, s1, scale=1 / 32, accum=fv(st + 5, 1))
            r1, r2 = fv(st + 2, 1), fv(st + 6, 1)
            t = rsqrt_sum(st + 2, st, s0, s1)
            e = ts(r2, fv(st + 4, 1), fv(st + 5, 1), ALU.add, q0, q1, t, s2=r1, op1=ALU.mult, q=pool)
            e = ts(r2, r2, r1, ALU.mult, e, s2=EPS, op1=ALU.add, q=pool)
            e = tt(r2, r2, fv(eps_half, 1), ALU.pow, e, t_eps, q=pool)
            e = tt(r2, r2, r1, ALU.mult, e, q=pool)
            xn = lambda: [ts(out[h], x[h], r2, ALU.mult, e, [w0, w1][h], given) for h in range(2)]
            return [t, q0, q1], xn, [w0, w1]

        bank_free[0:2] = [s.free for s in XY.slots]
        t_r1, t_acc, t_n, t_h = [None] * 2, [None] * 2, [None] * 2, [None] * 2
        Bank.U.slots[0].free, Bank.U.slots[1].free = gb.free, ub.free
        if Bank.U.i % 2:
            Bank.U.slots.reverse()
            Bank.U.i = 0
        lead_banks = Bank.U.slots + Bank.O.slots + Bank.S.slots

        W.pool_share = 0
        t_r1[0], xn, t_acc[0] = last_norm(0)
        low = split_late(18, 19, t_hl[0:2])
        t_n[0] = xn()
        low()
        t_h[0] = turn_fm(0, 0, t_n[0], SCA, t_moe)
        low1 = split_late(20, 21, t_hl[2:4])
        t_r1[1], xn1, t_acc[1] = last_norm(1)
        low1()
        bank_free[2:4] = t_acc[0]
        for s, t in zip(Bank.O.slots, t_acc[1]):
            s.free = [t]
        W.hl.append((22, 23, t_hl[4:]))
        pump()
        lead = take_lead(lead_banks[:3])
        lead_tm(lead[:2], 0, t_h[0])
        t_n[1] = xn1()
        t_h[1] = turn_fm(0, 1, t_n[1], SCA, t_old)
        lead_tm(lead[:2], 1, t_h[1])
        give(5, [t_moe])
        lead_fm(lead, SCA)
        W.pool_share = 1024
        for u in lead:
            done(u, u.read or u.t)
            u.over = True
        for s, f in zip(Bank.S.slots + Bank.T.slots, bank_free):
            s.free = f
        t_h.append(lead[1].t)

        t_neg = cp(three(B16(NEG, 512), 128), fv(tri_at, 128).unsqueeze(1).to_broadcast([128, 4, 128]), t_tri, given)
        CV = Ring([page(12) + 1024, page(12) + 1536, page(4) + 1312])
        for s in CV.slots:
            s.free = [t_old]
        ZS = Ring([page(17) + 512 * i for i in range(3)])
        t17 = retired(17)
        t_bc, t_xs, t_ys, t_cbt_read = {}, {}, {}, []
        D_RING = Ring([page(13) + 512 * i for i in range(2)])
        SC_RING = Ring([page(13) + 1024, page(13) + 1536] + [page(14) + 512 * i for i in range(4)])
        for r in (D_RING, SC_RING):
            for s in r.slots:
                s.free = [t_h, t_neg]
        XDD_RING = Ring([XDD + 128 * i for i in range(6)])
        E2_RING = Ring([E2_ + 128 * i for i in range(4)])
        ss = {}

        def ssd_dt(b, t):
            v, ab, tmp = ST, ST + 256, ST + 512
            t_v = acti(fv(v, 256), PB[b.at][:, 0:256], ACT.Identity, t, t_h, bias=ccol("dt_b"))
            t_ab = acti(fv(ab, 256), PB[b.at][:, 0:256], ACT.Abs, t, t_h, bias=ccol("dt_b"))
            b.free = [t_ab]
            yield
            for t in softplus(fv(DT, 256), fv(v, 256), fv(ab, 256), 256, tmp, t_v, t_ab):
                if t is None:
                    yield
            t = ts(fv(tmp, 256), fv(DT, 256), fv(a_exp, 1), ALU.mult, t, t_a, s2=-1.0, op1=ALU.mult)
            one = F[:, ones:ones + 1].to_broadcast([128, 128])
            t_cs = []
            for ch in range(2):
                o, i = fv(CS + ch * 128, 128), fv(tmp + ch * 128, 128)
                t_cs.append(dve.do(lambda e, o=o, i=i: e.tensor_tensor_scan(o, one, i, 0.0, ALU.mult, ALU.add), t))
            yield
            t_dec = acti(fv(DEC, 128, 0, 32), fv(CS, 128, 0, 32), ACT.Exp, t_cs, scale=-1.0,
                         bias=F[0:32, CS + 127:CS + 128])
            t1 = acti(rv(CSR, 256, 0, 64), fv(CS, 256, 0, 64), ACT.Copy, t_cs)
            ss["csr"] = tt(rv(CSR, 256, 32, 64), fv(CS, 256, 32, 64), rf(CSR, 256, 32, 64), ALU.subtract, t1)
            ss["dt"] = t_cs
            for _ in range(1):
                yield
            s = Bank.T.next()
            for i, (src, o) in enumerate(((DT, 0), (DT, 128), (CS, 0), (CS, 128), (DEC, 0))):
                t = tr(PB[s.at][:, i * 32:i * 32 + 32], fv(src + o, 128, 0, 32), t_cs, t_dec, s.free, n=32)
            e1 = cp(fv(TM, 64), PB[s.at][:, 0:64], t)
            e2 = ts(fv(TM + 64, 64), PB[s.at][:, 64:128], -1.0, ALU.mult, t)
            e3 = cp(fv(TM + 128, 32), PB[s.at][:, 128:160], t)
            s.free = [e3]
            ss["tm"] = [e1, e2, e3]

        def ssd_bc():
            yield
            s = Bank.O.next()
            for g in range(4):
                t = tr(PB[s.at][:, g * 128:(g + 1) * 128], fv(BC + g * 256, 128), t_bc[g], s.free)
            s.free = [cp(fv(BTM, 512), PB[s.at][:, :], t)]
            ss["btm"] = s.free
            ss["cbt"] = []
            for half in range(2):
                if half:
                    yield
                s = (Bank.T, Bank.O)[half].next()
                for g in (2 * half, 2 * half + 1):
                    for ch in range(2):
                        o = (g % 2) * 256 + ch * 128
                        t = mm(PB[s.at][:, o:o + 128], fv(BC + g * 256 + ch * 128, 128),
                               fv(BC + (4 + g) * 256 + ch * 128, 128), True, True, t_bc[g], t_bc[4 + g], s.free)
                s.free = [acti(fv(CBT + half * 512, 512), PB[s.at][:, :], ACT.Copy, t)]
                ss["cbt"] += [s.free, s.free]

        def ssd_tiles(tiles):
            yield
            while "tm" not in ss:
                yield
            n = len(tiles)
            i0 = tiles[0]
            s = Bank.T.next()
            for k, i in enumerate(tiles):
                for ch in range(2):
                    t = tr(PB[s.at][:, ch * n * 128 + k * 128:ch * n * 128 + k * 128 + 128],
                           fv(XS + i * 256 + ch * 128, 128), t_xs[i], s.free)
            src = PB[s.at][:, 0:n * 256].rearrange("p (c h q) -> p c h q", c=2, q=64)
            dst = fv(XDT, 4096).rearrange("p (c f) -> p c f", c=2)[:, :, i0 * 128:(i0 + n) * 128]
            dst = dst.rearrange("p c (h q) -> p c h q", q=64)
            dtm = fv(TM, 64).rearrange("p (c h) -> p c h", c=2)[:, :, 2 * i0:2 * (i0 + n)]
            t_xdt = tt(dst, src, dtm.unsqueeze(3).to_broadcast([128, 2, 2 * n, 64]), ALU.mult, t, ss["tm"])
            s.free = [t_xdt]
            sc, t_sc = {}, {}
            for i in tiles:
                s, d, c = Bank.S.next(), D_RING.next(), SC_RING.next()
                mm(PB[s.at][:, :], B16(idb, 128), B16(NEG, 512), True, False, t_idb, t_neg, s.free)
                for hh in range(2):
                    h = 2 * i + hh
                    t = mm(PB[s.at][:, hh * 256:(hh + 1) * 256], R[0:64, idr + h:idr + h + 1].to_broadcast([64, 128]),
                           rv(CSR, 256, 0, 64), False, hh == 1, ss["csr"], t_idr)
                es = []
                for hh in range(2):
                    for ch in range(2):
                        o = hh * 256 + ch * 128
                        es.append(acti(fv(d.at + o, 128), PB[s.at][:, o:o + 128], ACT.Exp, t, d.free, ss["tm"],
                                       bias=fv(TM + 64 + ch * 32 + 2 * i + hh, 1)))
                s.free = [es]
                cb = fv(CBT + (i // 4) * 256, 256).unsqueeze(1).to_broadcast([128, 2, 256])
                t_sc[i] = tt(three(fv(c.at, 512), 256), three(fv(d.at, 512), 256), cb, ALU.mult, es, ss["cbt"][i // 4],
                             c.free, q=pool)
                d.free = [t_sc[i]]
                sc[i] = c
            xd, t_xd = {}, {}
            for i in tiles:
                xd[i] = XDD_RING.next()
                dec = fv(TM + 128 + 2 * i, 2).unsqueeze(2).to_broadcast([128, 2, 64])
                t_xd[i] = tt(three(fv(xd[i].at, 128), 64), three(fv(XDT + i * 128, 128), 64), dec, ALU.mult, t_xdt,
                             xd[i].free, ss["tm"], q=pool)
            yield
            yield
            s = Bank.T.next()
            for k, i in enumerate(tiles):
                t = mm(PB[s.at][:, k * 128:(k + 1) * 128], fv(BTM + (i // 4) * 128, 128), fv(xd[i].at, 128), True, True,
                       t_xd[i], ss["btm"], s.free)
                xd[i].free = [t]
            e2 = {}
            for k, i in enumerate(tiles):
                for hh in range(2):
                    h = cc("ident", 2 * i + hh)
                    t = mm(PB[s.at][hh * 64:hh * 64 + 64, 256 + k * 128:256 + (k + 1) * 128],
                           F[0:32, h:h + 1].to_broadcast([32, 64]), fv(CS + 128, 128, 0, 32), True, True)
            t_st = acti(fv(ST + i0 * 128, n * 128), PB[s.at][:, 0:n * 128], ACT.Copy, t, ss["dt"])
            s.free = [t_st]
            for k, i in enumerate(tiles):
                e2[i] = E2_RING.next()
                e2[i].tok = acti(fv(e2[i].at, 128), PB[s.at][:, 256 + k * 128:256 + (k + 1) * 128], ACT.Exp, t,
                                 e2[i].free)
                s.free.append(e2[i].tok)
            s = Bank.O.next()
            for k, i in enumerate(tiles):
                for ch in range(2):
                    for hh in range(2):
                        o = k * 256 + ch * 128
                        t = mm(PB[s.at][hh * 64:hh * 64 + 64, o:o + 128],
                               fv(XDT + ch * 2048 + i * 128 + hh * 64, 64), fv(sc[i].at + hh * 256 + ch * 128, 128),
                               True, True, t_sc[i], t_xdt, s.free)
                sc[i].free = [t]
            ss["xdt_read"] = t
            t_cbt_read.append(list(t_sc.values()))
            t_y1 = {}
            for k, i in enumerate(tiles):
                x = fv(XS + i * 256, 256)
                t_y1[i] = stt(x, x, ccol("d", i), PB[s.at][:, k * 256:(k + 1) * 256], ALU.mult, ALU.add, t)
            s.free = [t_y1[i] for i in tiles]
            yield
            s = Bank.O.next()
            for k, i in enumerate(tiles):
                t = mm(PB[s.at][:, k * 128:(k + 1) * 128], fv(ST + i * 128, 128), fv(BC + (4 + i // 4) * 256 + 128, 128),
                       True, True, t_st, s.free)
            es = []
            for k, i in enumerate(tiles):
                e = tt(fv(e2[i].at, 128), PB[s.at][:, k * 128:(k + 1) * 128], fv(e2[i].at, 128), ALU.mult, t, e2[i].tok)
                es.append(e)
                x = fv(XS + i * 256 + 128, 128)
                t_ys[i] = tt(x, x, fv(e2[i].at, 128), ALU.add, e, t_y1[i])
                e2[i].free = [t_ys[i]]
            s.free = es

        def conv(src, w, bias, taps, out, t, *after):
            ta = [acti(o, s, ACT.Identity, t, after, scale=F[:, wc + taps - 1:wc + taps], bias=F[:, bc:bc + 1])
                  for o, s, wc, bc in zip(out, src, w, bias)]
            last = list(ta)
            for k in range(1, taps):
                for i, (o, s, wc) in enumerate(zip(out, src, w)):
                    last[i] = stt(o[:, k:], s[:, :256 - k], F[:, wc + taps - 1 - k:wc + taps - k], o[:, k:], ALU.mult,
                                  ALU.add, ta, last[i])
            return last

        def ssd_z(i, z, t_z):
            x = fv(XS + i * 256, 256)
            t_ys[i] = stt(x, x, 0.5, z, ALU.mult, ALU.mult, t_z, t_ys[i])
            return t_ys[i]

        t_yg = []

        def ssd_group(g):
            yield
            x4 = fv(XS + g * 1024, 1024)
            sq = BC
            t = acti(fv(sq, 1024), x4, ACT.Square, [t_ys[i] for i in range(4 * g, 4 * g + 4)], t_sqfree, ss["btm"], ss["cbt"])
            if g < 3:
                yield
            t = tt(fv(sq, 512), fv(sq, 512), fv(sq + 512, 512), ALU.add, t)
            t = tt(fv(sq, 256), fv(sq, 256), fv(sq + 256, 256), ALU.add, t)
            yield
            b = Bank.O.next()
            for ch in range(2):
                t2 = mm(PB[b.at][:, ch:ch + 1], fv(sq + ch * 128, 128), fv(inv_n + 2, 1), True, True, t, t_inv, b.free)
            t_sqfree[:] = [t2]
            r2 = fv(rcol + 2 * (g % 2), 2)
            e = ts(r2, PB[b.at][:, 0:2], EPS, ALU.add, t2)
            b.free = [e]
            e = tt(r2, r2, F[0:128, eps_half:eps_half + 1].to_broadcast([128, 2]), ALU.pow, e, t_eps, q=pool)
            yield
            b = Bank.O.next()
            for ch in range(2):
                r = rcol + 2 * (g % 2) + ch
                t = mm(PB[b.at][:, ch * 128:ch * 128 + 128], F[:, r:r + 1].to_broadcast([128, 128]), ident, True, True, e,
                       b.free)
            es = []
            for i in range(4 * g, 4 * g + 4):
                x = fv(XS + i * 256, 256)
                es.append(stt(x, x, ccol("ssd_n", i), PB[b.at][:, 0:256], ALU.mult, ALU.mult, t, t_ys[i]))
            b.free = es
            th = acti(rv(YGH + g * 1024, 1024), x4, ACT.Copy, es, ss["xdt_read"])
            tl = tt(rv(YGL + g * 1024, 1024), x4, rf(YGH + g * 1024, 1024), ALU.subtract, th, es,
                    [s.free for s in D_RING.slots + SC_RING.slots])
            t_yg.extend([[th, tl]] * 4)

        t_sqfree = []
        pend = []
        for n in range(21):
            if n == 17:
                retire(24)
            W.pool_share = 1024 if n < 5 else 512 if n < 14 else 0
            tiles = SSD_TILES[2 * n:2 * n + 2]
            if n < 3:
                u = lead[n]
                b, t = u.bank, u.t
            else:
                u = take()
                b = lead_banks[n] if n < 6 else Bank.U.next()
                t = fm(u, 128 * len(tiles), 8, HT_H, HT_L, b.at, len(tiles), b.free)
            cv = CV.next()
            assert all(p[3] is not cv for p in pend)
            src = {k: PB[b.at][:, k * 256:(k + 1) * 256] for k in range(2)}
            b.free = []
            if n < 4:
                through(u, t)
            xt, cvf = [], []
            cvk = [k for k, tl in enumerate(tiles) if tl[0] in "bcx"]
            t_bank = t
            if tiles[0] == "dt":
                bg.append(ssd_dt(b, t))
                next(bg[-1])
                t_bank = b.free
            if cvk:
                chan = [{"x": 0, "b": 16, "c": 20}[tiles[k][0]] + tiles[k][1] for k in cvk]
                dst = [fv(XS + tiles[k][1] * 256, 256) if tiles[k][0] == "x" else
                       fv(BC + (tiles[k][1] + (4 if tiles[k][0] == "c" else 0)) * 256, 256) for k in cvk]
                last = conv([src[k] for k in cvk], [cc("conv_w", c * 4) for c in chan], [cc("conv_b", c) for c in chan],
                            4, dst, t_bank, t, t_half, t_old)
                b.free = last
                for k, o, tk in zip(cvk, dst, last):
                    kind, i = tiles[k]
                    th = fv(cv.at + k * 256, 256)
                    e = acti(th, o, ACT.Tanh, tk, cv.free)
                    e = stt(o, th, 1.0, o, ALU.add, ALU.mult, e)
                    cvf.append(e)
                    if kind == "x":
                        t_xs[i] = e
                        xt.append(i)
                    else:
                        t_bc[i + (4 if kind == "c" else 0)] = e
            zk = [k for k, tl in enumerate(tiles) if tl[0] == "z"]
            zs = []
            if zk:
                o, n_ = zk[0] * 256, len(zk) * 256
                zv = ZS.next() if zk[-1] and tiles[1][1] < 6 else cv
                g, ps = fv(zv.at + o, n_), PB[b.at][:, o:o + n_]
                e = acti(g, ps, ACT.Tanh, t, b.free, zv.free, t17, scale=0.5)
                e = stt(g, g, 1.0, ps, ALU.add, ALU.mult, e)
                b.free = [b.free, e]
                zs = [(tiles[k][1], fv(zv.at + k * 256, 256), e, zv) for k in zk]
            cv.free = cvf
            tick()
            if n >= 4:
                through(u, t)
            if ("c", 3) in tiles:
                bg.append(ssd_bc())
            if xt:
                bg.append(ssd_tiles(xt))
            pend += zs
            while pend and pend[0][0] in t_ys:
                i, z, e, c = pend.pop(0)
                assert i in t_ys
                c.free = [c.free, ssd_z(i, z, e)]
                if i % 4 == 3:
                    bg.append(ssd_group(i // 4))
        t_x = [[ts(x, x, fv(st_ms[ch] + 2, 1), ALU.mult, t_r1[ch], t_n[ch], q=pool) for x in halves(X1, ch)]
               for ch in range(2)]
        t_hr = t
        assert not pend
        bank_free[:] = [s.free for s in Bank.S.slots + Bank.T.slots]
        held = out_units(8, YGH, YGL, t_yg, 3, tick)

        UB = Ring(Bank.U.slots + Bank.O.slots)

        def take_pairs(*pairs):
            for p in pairs:
                for item in list(W.hl):
                    if item[:2] == p:
                        W.hl.remove(item)
                        W.dropped[p] = item[2]
                        break
                else:
                    W.dropping.add(p)

        def ffn(l, us, free):
            CG = Ring([page(3) + 512 * i for i in range(2)])
            CVV = Ring([page(3) + 1024 + 512 * i for i in range(2)])
            GVH = Ring([page(4) + 512 * i for i in range(4)])
            GVL = Ring([page(14) + 512 * i for i in range(4)])
            for r in (CG, CVV, GVH, GVL):
                for s in r.slots:
                    s.free = [free]
            ready = deque()

            def down():
                j, gh, gl, tok = ready.popleft()
                u = take()
                for ch in range(2):
                    for half in range(2):
                        t = out_part(u, ch, half, gh.at, gl.at, j == 0, j == 15, tok)
                gh.free, gl.free = [t], [t]
                done(u, t)

            us = deque(us)
            late = []
            for j in range(16):
                cvs = []
                for part_, ring in ((0, CG), (1, CVV)):
                    c = ring.next()
                    if us:
                        u = us.popleft()
                        b, t = u.bank, u.t
                    else:
                        u, b = take(), UB.next()
                        t = fm(u, 256, 8, HT_H, HT_L, b.at, 2, b.free)
                    tiles = [32 * part_ + 2 * j + k for k in range(2)]
                    out = [fv(c.at + k * 256, 256) for k in range(2)]
                    last = conv([PB[b.at][:, k * 256:(k + 1) * 256] for k in range(2)],
                                [cc("f_cw", l * 192 + x * 3) for x in tiles], [cc("f_cb", l * 64 + x) for x in tiles],
                                3, out, t, c.free)
                    b.free = last
                    cvs.append((c, last))
                    if j < 15 or part_ == 0:
                        through(u, t)
                    else:
                        late.append((u, t))
                (cg, tg), (cv, tv) = cvs
                gh, gl = GVH.next(), GVL.next()
                e = acti(fv(cg.at, 512), fv(cg.at, 512), ACT.Gelu_apprx_tanh, tg)
                e = tt(fv(cg.at, 512), fv(cg.at, 512), fv(cv.at, 512), ALU.mult, e, tv)
                th = acti(rv(gh.at, 512), fv(cg.at, 512), ACT.Copy, e, gh.free)
                tl = tt(rv(gl.at, 512), fv(cg.at, 512), rf(gh.at, 512), ALU.subtract, th, e, gl.free)
                cg.free, cv.free = [th, tl], [e]
                for x in late:
                    through(*x)
                ready.append((j, gh, gl, [th, tl]))
                if 1 < j < 15:
                    down()
            return [(take(), gh.at, gl.at, False, j == 15, tok) for j, gh, gl, tok in ready], t

        lead_slots = lambda: [UB.next() for _ in range(3)]

        assert not bg
        W.pool_share = 512
        W.hl.append((17, 24, [t_yg, retired(24)]))
        W.hl.append((6, 7, [t_cbt_read, t_yg, [s.free for s in E2_RING.slots]]))
        pump()
        t_row = [row_load("row0", page(8), 3, t_yg), row_load("row1", page(12) + 1024, 4, t_yg)]
        t_x, us, t_m = turn(1, held, lead_slots(), page(8), t_row[0], page(11), page(3), [t_yg, ss["dt"]], t_hr)
        held, t_hr = ffn(0, us, [t_yg, t_m])
        t_row.append(row_load("row2", page(12), 5, t_x))

        W.pool_share = 1024
        W.dve_hi = 0.25
        XBP = 259
        XB, YB, GA, XC, GX, AT_ = span(3, 4), *(span(6, 11) + 2560 * i for i in range(4)), span(13, 14)
        t_x, us, t_m = turn(2, held, lead_slots(), page(12) + 1024, t_row[1], page(11), page(8), [], t_hr)
        take_pairs((6, 7))
        t_bo = load("b_out", fv(page(12) + 1024, 1024, 0, 1), a["rows"][7:8, :], t_x)
        t_pad = zero(F[:, XB:XB + 10 * XBP].rearrange("p (t c) -> p t c", c=XBP)[:, :, 0:3], 0.0, t_m)
        xb = lambda i: XB + i * XBP
        pair = lambda at, n: fv(at + n * 512, 512)

        WX, WA = page(11), page(14) + 512
        t_wx = load("lru_gx", fv(WX, 1280), a["gates"][0], us[1].t)
        t_wa = load("lru_ga", fv(WA, 1280), a["gates"][1], t_m)

        for s_, f in zip(Bank.S.slots + Bank.T.slots, bank_free):
            s_.free = f
        LB = Ring([UB.slots[3]] + Bank.S.slots + Bank.T.slots + UB.slots[:3])
        t_xc = []
        for n in range(5):
            if n < 3:
                u = us[n]
                b, t = u.bank, u.t
            else:
                u, b = take(), LB.next()
                t = fm(u, 256, 8, HT_H, HT_L, b.at, 2, b.free)
            ts_ = [acti(fv(xb(2 * n + k) + 3, 256), PB[b.at][:, k * 256:(k + 1) * 256], ACT.Identity, t, t_m,
                        bias=ccol("l_bin", 10 + 2 * n + k)) for k in range(2)]
            b.free = ts_
            last = [ts(fv(XC + i * 256, 256), fv(xb(i) + 3, 256), ccol("l_cw", i * 4 + 3), ALU.mult, e, t_m,
                       s2=ccol("l_cb", i), op1=ALU.add, q=pool) for i, e in zip((2 * n, 2 * n + 1), ts_)]
            for j in range(1, 4):
                for k in range(2):
                    i = 2 * n + k
                    o = fv(XC + i * 256, 256)
                    last[k] = stt(o, fv(xb(i) + 3 - j, 256), ccol("l_cw", i * 4 + 3 - j), o, ALU.mult, ALU.add, last[k],
                                  t_pad)
            t_xc.append(last)
            through(u, t)

        t_drop = [W.dropped.pop((6, 7))]
        t_mu, t_gx, t_at, t_hl, t_yb, t_yl = [], [], [], [], [], []
        YLH, YLL = GX, AT_

        def gates(n):
            ts_ = []
            for wt, t_w, dst, bn in ((WX, t_wx, GX, 0), (WA, t_wa, GA, 10)):
                b = LB.next()
                for k in range(2):
                    i = 2 * n + k
                    t = mm(PB[b.at][:, k * 256:(k + 1) * 256], fv(wt + i * 128, 128), fv(XC + i * 256, 256), True, True,
                           t_w, t_xc[n], b.free)
                b.free = [acti(fv(dst + i * 256, 256), PB[b.at][:, k * 256:(k + 1) * 256], ACT.Tanh, t, t_bgh, t_m,
                               t_drop, bias=fv(bgh + bn + i, 1), scale=0.5) for k, i in enumerate((2 * n, 2 * n + 1))]
                ts_.append(b.free)
            t1, t2 = [], []
            for i in (2 * n, 2 * n + 1):
                g = fv(GA + i * 256, 256)
                t1.append(acti(fv(AT_ + i * 256, 256), g, ACT.Exp, ts_[1], t_lam, t_m, scale=fv(lab + i, 1),
                               bias=fv(lab + i, 1)))
                t2.append(acti(g, g, ACT.Tanh, t1, t_lam, scale=fv(lam + i, 1), bias=fv(lam + i, 1)))
            a2 = pair(XB, n)
            e = tt(a2, pair(AT_, n), pair(AT_, n), ALU.mult, t1, t_xc)
            t_mu.append(stt(pair(GA, n), a2, 1.0, pair(GA, n), ALU.add, ALU.mult, e, t2))
            t_gx.append(stt(pair(GX, n), pair(GX, n), 1.0, pair(XC, n), ALU.add, ALU.mult, ts_[0], t_xc[n]))
            t_at.append(t1)

        def scan(n):
            e = acti(pair(GA, n), pair(GA, n), ACT.Sqrt, t_mu[n])
            e = stt(pair(GA, n), pair(GA, n), 0.5, pair(GX, n), ALU.mult, ALU.mult, e, t_gx[n])
            t_hl.append([])
            for i in (2 * n, 2 * n + 1):
                o, at_, bt = (fv(r + i * 256, 256) for r in (XC, AT_, GA))
                t_hl[n].append(dve.do(lambda q, o=o, at_=at_, bt=bt: q.tensor_tensor_scan(o, at_, bt, 0.0, ALU.mult,
                                                                                          ALU.add), e, t_at[n]))

        def branch(n):
            u, b = take(), LB.next()
            t = fm(u, 256, 8, HT_H, HT_L, b.at, 2, b.free)
            done(u, t)
            b.free = [acti(fv(YB + i * 256, 256), PB[b.at][:, k * 256:(k + 1) * 256], ACT.Identity, t, t_m, t_drop,
                           bias=ccol("l_bin", i)) for k, i in enumerate((2 * n, 2 * n + 1))]
            t_yb.append(b.free)
            return t

        def product(n):
            f = pair(YB, n)
            e = acti(f, f, ACT.Gelu_apprx_tanh, t_yb[n])
            e = tt(f, f, pair(XC, n), ALU.mult, e, t_hl[n])
            th = cp(rv(YLH + n * 512, 512), f, e)
            tl = tt(rv(YLL + n * 512, 512), f, rf(YLH + n * 512, 512), ALU.subtract, th, e)
            t_yl.extend([[th, tl]] * 2)

        gates(0)
        gates(1)
        t_hr = branch(0)
        gates(2)
        gates(3)
        gates(4)
        t_hr = branch(1)
        scan(0)
        scan(1)
        scan(2)
        scan(3)
        scan(4)
        t_hr = branch(2)
        product(0)
        product(1)
        t_hr = branch(3)
        product(2)
        t_hr = branch(4)
        product(3)
        product(4)
        W.dve_hi = 0
        bank_free[:] = [s_.free for s_ in Bank.S.slots + Bank.T.slots]
        for b, f in enumerate(bank_free):
            mm(PB[banks[b]][:, :], F[0:1, ones:ones + 1].to_broadcast([1, 128]),
               fv(page(12) + 1024 + b % 2 * 512, 512, 0, 1), True, False, t_bo, t_ones, f)
        held = out_units(5, YLH, YLL, t_yl, 3, begun=True)
        W.hl.append((6, 7, [t_yl]))
        pump()
        t_x, us, t_m = turn(3, held, lead_slots(), page(12), t_row[2], page(11), page(8), [t_yl, t_hr], t_hr)
        t_row.append(row_load("row4", page(12), 6, t_x))
        held, t_hr = ffn(1, us, [t_m])
        ov = a["out"].rearrange("(c p) d -> p c d", p=128)
        for ch in range(2):
            t_x = post_norm(ch, page(11), *post_sums(ch, page(12), held_part(held, ch, ch == 1)[0], t_row[-1], page(11),
                                                     page(8), []))
            for h in range(2):
                o = h * 512
                load(f"out{ch}{h}", ov[:, ch, o:o + 512], fv(X1 + ch * 1024 + o, 512), t_x[h])
        assert W.taken == len(units)

        queues = (pe, act, dve, pool, sp)
        all_sems = page_sem + list(misc.values())
        ends = [(s.handle, s.count) for s in all_sems if s.count]
        for q in queues:
            q.number()
        with nc.Block() as block:
            @block.tensor
            def _(e):
                pe.emit(e)

            @block.scalar
            def _(e):
                act.emit(e)

            @block.vector
            def _(e):
                dve.emit(e)

            @block.gpsimd
            def _(e):
                pool.emit(e)

            @block.sync
            def _(e):
                sp.emit(e)
                for handle, count in ends:
                    e.wait_ge(handle, count)



def kernel(**inputs):
    import numpy as _np
    import concourse.bacc as _bacc
    from concourse import mybir as _mybir
    from concourse.bass_utils import run_bass_kernel_spmd as _run

    arrays = lay_out({k: _np.asarray(v) for k, v in inputs.items()})
    nc = _bacc.Bacc("TRN2", target_bir_lowering=False, num_devices=1)
    a = {k: nc.dram_tensor(k, v.shape, _mybir.dt.from_np(v.dtype), kind="ExternalInput").ap()
         for k, v in arrays.items()}
    a["out"] = nc.dram_tensor("out", (SEQ, DM), F32, kind="ExternalOutput").ap()
    program(nc, a)
    r = _run(nc, [arrays], core_ids=[0])
    return r.results[0]["out"].reshape(1, SEQ, DM)
```
